# Optimizing a Trainium2 kernel written in Bass

```python
import math
import jax, jax.numpy as jnp
from jax import lax
import numpy as np

D_MODEL = 1024
BATCH = 1
SEQ = 256
DEPTH = 2

HEAD_DIM = 64
NORM_EPS = 1e-6
NEG = -1e30
N_EVEN = (DEPTH + 1) // 2
N_ODD = DEPTH // 2

A_HEADS = 8
A_PATTERNS = ((128, 1), (512, 4), (2048, 16))
A_WIDTH = A_HEADS * HEAD_DIM

B_HEADS = 8
B_Q_LORA = D_MODEL // 4
B_KV_LORA = D_MODEL // 8
B_NOPE = HEAD_DIM
B_ROPE = HEAD_DIM // 2
B_V = HEAD_DIM
B_QBLOCK = 128
ROPE_THETA = 10000.0
B_WIDTH = B_HEADS * B_V

IN_E_WIDTH = 3 * A_WIDTH + B_Q_LORA + B_KV_LORA + B_ROPE
MIX_E_WIDTH = A_WIDTH + B_WIDTH

C_HEADS = D_MODEL // HEAD_DIM
C_WIDTH = C_HEADS * HEAD_DIM
GRID_W = 64
NA_ROWS = 8
NA_COLS = 16
NA_KEY_COLS = 2 * NA_COLS

D_FF = ((8 * D_MODEL // 3 + 255) // 256) * 256
N_EXPERTS = 8
TOP_K = 2
D_FF_EXPERT = 7 * D_MODEL // 2

kernel_name = "hybrid_dilated_mla_natten_moe_encoder"

def rms_norm(x, g):
    xf = x.astype(jnp.float32)
    y = xf * lax.rsqrt(jnp.mean(xf * xf, axis=-1, keepdims=True) + NORM_EPS)
    return (y * g.astype(jnp.float32)).astype(x.dtype)

def swiglu(x, w_gate, w_up, w_down):
    return (jax.nn.silu(x @ w_gate) * (x @ w_up)) @ w_down

def alibi_slopes(n):
    return jnp.asarray(np.array([2.0 ** (-8.0 * (h + 1) / n) for h in range(n)], np.float32))

def dilated_window_branch(q, k, v, window, dilation, slopes):
    b, s, h, dh = q.shape
    r = window // (2 * dilation)
    L = s // dilation
    n = b * dilation

    def by_residue(t):
        return t.reshape(b, L, dilation, h, dh).transpose(0, 2, 1, 3, 4).reshape(n, L, h, dh)

    qs, ks, vs = by_residue(q), by_residue(k), by_residue(v)
    blk = r
    nb = -(-L // blk)
    lp = nb * blk
    qp = jnp.pad(qs, ((0, 0), (0, lp - L), (0, 0), (0, 0))).reshape(n, nb, blk, h, dh)
    pad_kv = ((0, 0), (blk, lp - L + blk), (0, 0), (0, 0))
    kp = jnp.pad(ks, pad_kv).reshape(n, nb + 2, blk, h, dh)
    vp = jnp.pad(vs, pad_kv).reshape(n, nb + 2, blk, h, dh)

    def band(t):
        return jnp.concatenate([t[:, :-2], t[:, 1:-1], t[:, 2:]], axis=2)

    kb, vb = band(kp), band(vp)
    qi = np.arange(lp).reshape(nb, blk)
    kj = (np.arange(nb)[:, None] * blk - blk) + np.arange(3 * blk)[None]
    rel = kj[:, None, :] - qi[:, :, None]
    valid = (np.abs(rel) <= r) & (kj[:, None, :] >= 0) & (kj[:, None, :] < L)
    dist = jnp.asarray((np.abs(rel) * dilation).astype(np.float32))

    scores = jnp.einsum('nbqhd,nbkhd->nhbqk', qp, kb).astype(jnp.float32) * (dh ** -0.5)
    scores = scores - slopes[None, :, None, None, None] * dist[None, None]
    scores = jnp.where(jnp.asarray(valid)[None, None], scores, NEG)
    lse = jax.nn.logsumexp(scores, axis=-1)
    p = jnp.exp(scores - lse[..., None])
    out = jnp.einsum('nhbqk,nbkhd->nbqhd', p.astype(v.dtype), vb).reshape(n, lp, h, dh)[:, :L]
    lse = lse.transpose(0, 2, 3, 1).reshape(n, lp, h)[:, :L]
    out = out.reshape(b, dilation, L, h, dh).transpose(0, 2, 1, 3, 4).reshape(b, s, h, dh)
    lse = lse.reshape(b, dilation, L, h).transpose(0, 2, 1, 3).reshape(b, s, h)
    return out, lse

def dilated_mixture_attention(q, k, v):
    slopes = alibi_slopes(q.shape[2])
    outs, lses = [], []
    for window, dilation in A_PATTERNS:
        o, l = dilated_window_branch(q, k, v, window, dilation, slopes)
        outs.append(o)
        lses.append(l)
    w = jax.nn.softmax(jnp.stack(lses, axis=0), axis=0)
    out = w[0][..., None].astype(q.dtype) * outs[0]
    for g in range(1, len(outs)):
        out = out + w[g][..., None].astype(q.dtype) * outs[g]
    return out

def rope(x, pos):
    half = x.shape[-1] // 2
    freqs = ROPE_THETA ** (-jnp.arange(half, dtype=jnp.float32) / half)
    ang = pos[:, None].astype(jnp.float32) * freqs[None]
    cos, sin = jnp.cos(ang)[:, None, :], jnp.sin(ang)[:, None, :]
    xf = x.astype(jnp.float32)
    x1, x2 = xf[..., :half], xf[..., half:]
    return jnp.concatenate([x1 * cos - x2 * sin, x1 * sin + x2 * cos], axis=-1).astype(x.dtype)

def latent_attention(q_lat, kv_lat, k_rope, q_norm, w_uq, kv_norm, w_ukv):
    b, s, _ = q_lat.shape
    pos = jnp.arange(s)
    q = (rms_norm(q_lat, q_norm) @ w_uq).reshape(b, s, B_HEADS, B_NOPE + B_ROPE)
    q_nope, q_pe = q[..., :B_NOPE], rope(q[..., B_NOPE:], pos)
    kv = (rms_norm(kv_lat, kv_norm) @ w_ukv).reshape(b, s, B_HEADS, B_NOPE + B_V)
    k_nope, v = kv[..., :B_NOPE], kv[..., B_NOPE:]
    k_pe = rope(k_rope[:, :, None, :], pos)[:, :, 0]
    scale = (B_NOPE + B_ROPE) ** -0.5
    nblk = s // B_QBLOCK
    qn = q_nope.reshape(b, nblk, B_QBLOCK, B_HEADS, B_NOPE).transpose(1, 0, 2, 3, 4)
    qr = q_pe.reshape(b, nblk, B_QBLOCK, B_HEADS, B_ROPE).transpose(1, 0, 2, 3, 4)

    def block(args):
        qn_b, qr_b = args
        sc = (jnp.einsum('bqhd,bkhd->bhqk', qn_b, k_nope)
              + jnp.einsum('bqhr,bkr->bhqk', qr_b, k_pe)).astype(jnp.float32) * scale
        p = jax.nn.softmax(sc, axis=-1)
        return jnp.einsum('bhqk,bkhd->bqhd', p.astype(v.dtype), v)

    out = lax.map(block, (qn, qr))
    return out.transpose(1, 0, 2, 3, 4).reshape(b, s, B_HEADS * B_V)

def neighborhood_attention(q, k, v, rpb):
    b, s, h, dh = q.shape
    rows = s // GRID_W
    kr = min(NA_ROWS, rows)
    n_cb = GRID_W // NA_COLS
    qb = q.reshape(b, rows, n_cb, NA_COLS, h, dh)
    kg = k.reshape(b, rows, GRID_W, h, dh)
    vg = v.reshape(b, rows, GRID_W, h, dh)

    q_c0 = np.arange(n_cb) * NA_COLS
    k_c0 = np.clip(q_c0 - NA_COLS // 2, 0, GRID_W - NA_KEY_COLS)
    key_cols = k_c0[:, None] + np.arange(NA_KEY_COLS)[None]
    q_cols = q_c0[:, None] + np.arange(NA_COLS)[None]
    col_start = np.clip(q_cols - NA_COLS // 2, 0, GRID_W - NA_COLS)
    col_ok = (key_cols[:, None, :] >= col_start[..., None]) & (key_cols[:, None, :] < col_start[..., None] + NA_COLS)
    col_idx = np.clip(key_cols[:, None, :] - q_cols[:, :, None] + NA_COLS - 1, 0, 2 * NA_COLS - 2)
    col_ok = jnp.asarray(col_ok)[None, None, :, :, None, :]
    rpb_f = rpb.astype(jnp.float32)
    scale = dh ** -0.5

    def one_row(i):
        rs = jnp.clip(i - kr // 2, 0, rows - kr)
        k_slab = lax.dynamic_slice_in_dim(kg, rs, kr, axis=1)[:, :, key_cols]
        v_slab = lax.dynamic_slice_in_dim(vg, rs, kr, axis=1)[:, :, key_cols]
        q_row = lax.dynamic_index_in_dim(qb, i, axis=1, keepdims=False)
        sc = jnp.einsum('bcqhd,brckhd->bhcqrk', q_row, k_slab).astype(jnp.float32) * scale
        row_idx = rs + jnp.arange(kr) - i + NA_ROWS - 1
        bias = rpb_f[:, row_idx][:, :, col_idx].transpose(0, 2, 3, 1, 4)
        sc = jnp.where(col_ok, sc + bias[None], NEG)
        p = jax.nn.softmax(sc.reshape(b, h, n_cb, NA_COLS, kr * NA_KEY_COLS), axis=-1)
        p = p.reshape(b, h, n_cb, NA_COLS, kr, NA_KEY_COLS).astype(v.dtype)
        return jnp.einsum('bhcqrk,brckhd->bcqhd', p, v_slab)

    out = lax.map(one_row, jnp.arange(rows))
    return out.transpose(1, 0, 2, 3, 4, 5).reshape(b, s, h * dh)

def moe_swiglu(x, w_router, w_gate, w_up, w_down):
    b, s, d = x.shape
    xt = x.reshape(b * s, d)
    logits = (xt @ w_router).astype(jnp.float32)
    top_val, top_idx = lax.top_k(logits, TOP_K)
    top_w = jax.nn.softmax(top_val, axis=-1)
    gates = jnp.sum(jax.nn.one_hot(top_idx, N_EXPERTS, dtype=jnp.float32) * top_w[..., None], axis=1)
    gates = gates.astype(x.dtype)
    y = jnp.zeros_like(xt)
    for e in range(N_EXPERTS):
        y = y + gates[:, e:e + 1] * swiglu(xt, w_gate[e], w_up[e], w_down[e])
    return y.reshape(b, s, d)

def setup_inputs(seed: int = 0) -> dict:
    key = jax.random.key(seed)
    keys = iter(jax.random.split(key, 32))
    f32 = jnp.float32

    def normal(shape, fan_in):
        return jax.random.normal(next(keys), shape, f32) * (fan_in ** -0.5)

    def gain(shape):
        return 1.0 + 0.05 * jax.random.normal(next(keys), shape, f32)

    return {
        "x": jax.random.normal(next(keys), (BATCH, SEQ, D_MODEL), f32),
        "ln_mix_e": gain((N_EVEN, D_MODEL)),
        "w_in_e": normal((N_EVEN, D_MODEL, IN_E_WIDTH), D_MODEL),
        "mla_q_norm": gain((N_EVEN, B_Q_LORA)),
        "mla_w_uq": normal((N_EVEN, B_Q_LORA, B_HEADS * (B_NOPE + B_ROPE)), B_Q_LORA),
        "mla_kv_norm": gain((N_EVEN, B_KV_LORA)),
        "mla_w_ukv": normal((N_EVEN, B_KV_LORA, B_HEADS * (B_NOPE + B_V)), B_KV_LORA),
        "w_out_e": normal((N_EVEN, MIX_E_WIDTH, D_MODEL), MIX_E_WIDTH),
        "ln_ffn_e": gain((N_EVEN, D_MODEL)),
        "ffn_w_gate": normal((N_EVEN, D_MODEL, D_FF), D_MODEL),
        "ffn_w_up": normal((N_EVEN, D_MODEL, D_FF), D_MODEL),
        "ffn_w_down": normal((N_EVEN, D_FF, D_MODEL), D_FF),
        "ln_mix_o": gain((N_ODD, D_MODEL)),
        "na_w_qkv": normal((N_ODD, D_MODEL, 3 * C_WIDTH), D_MODEL),
        "na_rpb": 0.1 * jax.random.normal(next(keys), (N_ODD, C_HEADS, 2 * NA_ROWS - 1, 2 * NA_COLS - 1), f32),
        "na_w_out": normal((N_ODD, C_WIDTH, D_MODEL), C_WIDTH),
        "ln_ffn_o": gain((N_ODD, D_MODEL)),
        "moe_router": normal((N_ODD, D_MODEL, N_EXPERTS), D_MODEL),
        "moe_w_gate": normal((N_ODD, N_EXPERTS, D_MODEL, D_FF_EXPERT), D_MODEL),
        "moe_w_up": normal((N_ODD, N_EXPERTS, D_MODEL, D_FF_EXPERT), D_MODEL),
        "moe_w_down": normal((N_ODD, N_EXPERTS, D_FF_EXPERT, D_MODEL), D_FF_EXPERT),
        "ln_final": gain((D_MODEL,)),
    }

def reference(x, ln_mix_e, w_in_e, mla_q_norm, mla_w_uq, mla_kv_norm, mla_w_ukv, w_out_e,
              ln_ffn_e, ffn_w_gate, ffn_w_up, ffn_w_down, ln_mix_o, na_w_qkv, na_rpb, na_w_out,
              ln_ffn_o, moe_router, moe_w_gate, moe_w_up, moe_w_down, ln_final):
    b, s, _ = x.shape
    split_e = [A_WIDTH, 2 * A_WIDTH, 3 * A_WIDTH, 3 * A_WIDTH + B_Q_LORA, 3 * A_WIDTH + B_Q_LORA + B_KV_LORA]
    for layer in range(DEPTH):
        if layer % 2 == 0:
            i = layer // 2
            h = rms_norm(x, ln_mix_e[i])
            proj = h @ w_in_e[i]
            qa, ka, va, q_lat, kv_lat, k_rope = jnp.split(proj, split_e, axis=-1)
            qa = qa.reshape(b, s, A_HEADS, HEAD_DIM)
            ka = ka.reshape(b, s, A_HEADS, HEAD_DIM)
            va = va.reshape(b, s, A_HEADS, HEAD_DIM)
            oa = dilated_mixture_attention(qa, ka, va).reshape(b, s, A_WIDTH)
            ob = latent_attention(q_lat, kv_lat, k_rope, mla_q_norm[i], mla_w_uq[i],
                                  mla_kv_norm[i], mla_w_ukv[i])
            x = x + jnp.concatenate([oa, ob], axis=-1) @ w_out_e[i]
            x = x + swiglu(rms_norm(x, ln_ffn_e[i]), ffn_w_gate[i], ffn_w_up[i], ffn_w_down[i])
        else:
            j = layer // 2
            h = rms_norm(x, ln_mix_o[j])
            qc, kc, vc = jnp.split(h @ na_w_qkv[j], 3, axis=-1)
            qc = qc.reshape(b, s, C_HEADS, HEAD_DIM)
            kc = kc.reshape(b, s, C_HEADS, HEAD_DIM)
            vc = vc.reshape(b, s, C_HEADS, HEAD_DIM)
            x = x + neighborhood_attention(qc, kc, vc, na_rpb[j]) @ na_w_out[j]
            x = x + moe_swiglu(rms_norm(x, ln_ffn_o[j]), moe_router[j], moe_w_gate[j],
                               moe_w_up[j], moe_w_down[j])
    return rms_norm(x, ln_final)


_drawn_inputs = setup_inputs


def setup_inputs(seed=0):
    import zlib

    import numpy as np

    out = dict(_drawn_inputs(seed))
    spreads = {}
    factors = {'mla_q_norm': 4.611,
     'mla_kv_norm': 3.174,
     'ln_mix_o': 4.27,
     'na_rpb': 3.966,
     'ln_ffn_o': 3.456}
    for name, (base, spread) in spreads.items():
        noise = np.random.default_rng([zlib.crc32(name.encode()), seed]).standard_normal(out[name].shape)
        drawn = base * np.exp(spread * noise) if base else spread * noise
        out[name] = __import__('jax').numpy.asarray(drawn.astype(out[name].dtype))
    for name, factor in factors.items():
        out[name] = (out[name] * factor).astype(out[name].dtype)
    return out
```

```python
from contextlib import ExitStack

import numpy as np

import concourse.bass as bass
from concourse import mybir

ALU = mybir.AluOpType
ACT = mybir.ActivationFunctionType
F32 = mybir.dt.float32
F32R = mybir.dt.float32r
BF16 = mybir.dt.bfloat16
I32 = mybir.dt.int32
U32 = mybir.dt.uint32
AX_X = mybir.AxisListType.X

P = 128
D = 1024
SEQ = 256
T = SEQ // P
KD = D // P
HALF = 512
EPS = 1e-6
NEG = -1e30
HD = 64
AH, BH, CH = 8, 8, 16
A_W = AH * HD
QL, KVL, ROPE = 256, 128, 32
BK = HD + ROPE
D_FF = 2816
E, EFF = 8, 3584
GRID_W, NA_COLS = 64, 16
RPB_R, RPB_C = 15, 31
RPB_RUN = 5 * RPB_C + GRID_W

UNIT = 2048
RING = 6
PARTS = 3
FFN_STEPS = D_FF // 256
MOE_STEPS = EFF // HALF
MOE_UNITS = 6 * MOE_STEPS

U_IN = 0
U_OUT0 = U_IN + 8
U_FFN = U_OUT0 + 4
U_QKV = U_FFN + 3 * FFN_STEPS
U_OUT1 = U_QKV + 12
U_MOE = U_OUT1 + 4
IN_COLS = [(3 * A_W, QL), (3 * A_W + QL, KVL + ROPE)] + [(256 * i, 256) for i in range(6)]

C_DIST, C_LNC = 0, 512
C_COS, C_SIN = 1024, 1056
C_MASK = 1088
C_ID, C_TRI, C_IOTA, C_ONES = 1344, 1472, 1600, 1856
C_ALL = 1984


def constants():
    c = np.zeros((P, C_ALL), np.float32)
    pos = np.arange(SEQ)
    d = np.abs(pos[:, None] - pos[None])
    cover = (d <= 64).astype(np.float64) + (d % 4 == 0) + (d % 16 == 0)
    lnc = np.where(cover > 0, np.log(np.maximum(cover, 1)), NEG).astype(np.float32)
    tiles = lambda a: a.reshape(T, P, -1).transpose(1, 0, 2).reshape(P, -1)
    c[:, C_DIST:C_DIST + 512] = tiles(-d.astype(np.float32))
    c[:, C_LNC:C_LNC + 512] = tiles(lnc)
    half = ROPE // 2
    freqs = np.float32(10000.0) ** (-np.arange(half, dtype=np.float32) / np.float32(half))
    ang = pos[:, None].astype(np.float32) * freqs[None].astype(np.float32)
    c[:, C_COS:C_COS + 32] = tiles(np.cos(ang.astype(np.float64)).astype(np.float32))
    c[:, C_SIN:C_SIN + 32] = tiles(np.sin(ang.astype(np.float64)).astype(np.float32))
    col = np.arange(P) % GRID_W
    first = np.clip(col - NA_COLS // 2, 0, GRID_W - NA_COLS)
    key = np.arange(GRID_W)
    inside = (key[None] >= first[:, None]) & (key[None] < first[:, None] + NA_COLS)
    c[:, C_MASK:C_MASK + 256] = np.tile(np.where(inside, 0.0, NEG), (1, 4))
    c[:, C_ID:C_ID + P] = np.eye(P)
    c[:, C_TRI:C_TRI + P] = np.triu(np.ones((P, P)), 1)
    c[:, C_IOTA:C_IOTA + 256] = np.arange(256)[None]
    c[:, C_ONES:C_ONES + P] = 1.0
    return c


class Unit:

    def __init__(self, s, k=0):
        self.s, self.k = s, k

    def count(self, ahead=0):
        return self.k * RING + (self.s + 1 + ahead)

    def early(self, back):
        return isinstance(self.k, int) and self.s < back

    @property
    def raw(self):
        return self.s % RING

    @property
    def part(self):
        return self.s % PARTS

    def filled(self):
        return self.k * 16 + 16 * (self.s // RING + 1)


def trunk(nc, x, ln_mix_e, w_in_e, mla_q_norm, mla_w_uq, mla_kv_norm, mla_w_ukv, w_out_e,
          ln_ffn_e, ffn_w_gate, ffn_w_up, ffn_w_down, ln_mix_o, na_w_qkv, na_rpb, na_w_out,
          ln_ffn_o, moe_router, moe_w_gate, moe_w_up, moe_w_down, ln_final, tables, out):
    with ExitStack() as ctx:
        def sb(name, shape, dt=F32):
            return ctx.enter_context(nc.sbuf_tensor(name, shape, dt))

        def sem(name):
            return ctx.enter_context(nc.semaphore(name))

        raw = sb("raw", [P, RING, UNIT])
        w_hi = sb("w_hi", [P, PARTS, UNIT], F32R)
        w_lo = sb("w_lo", [P, PARTS, UNIT], F32R)
        xres = sb("xres", [P, T, D])
        xn = sb("xn", [P, T, D])
        t_hi = sb("t_hi", [P, KD, SEQ], F32R)
        t_lo = sb("t_lo", [P, KD, SEQ], F32R)
        h_hi = sb("h_hi", [P, 2, HALF], F32R)
        h_lo = sb("h_lo", [P, 2, HALF], F32R)
        gains = sb("gains", [P, 3, D])
        lat_gain = sb("lat_gain", [P, QL + KVL])
        router = sb("router", [P, KD, E])
        tab = sb("tab", [P, C_ALL])
        mask_b = sb("mask_b", [P, SEQ], BF16)
        ident_b = sb("ident_b", [P, P], BF16)
        zero_b = sb("zero_b", [P, HALF], BF16)
        small = sb("small", [P, 64])
        arena = sb("arena", [P, 16192])
        banks = ctx.enter_context(nc.psum_tensor("banks", [P, 8, HALF], F32))

        ident = tab[:, C_ID:C_ID + P]
        tri = tab[:, C_TRI:C_TRI + P]
        ones = tab[:, C_ONES:C_ONES + P]

        def part_of(offset, n):
            return arena[:, offset:offset + n]

        qa_t = part_of(0, 1024).rearrange("p (m s) -> p m s", m=4)
        ka_t = part_of(1024, 1024).rearrange("p (m s) -> p m s", m=4)
        va = part_of(2048, 1024).rearrange("p (t c) -> p t c", t=T)
        ql = part_of(3072, 512).rearrange("p (t c) -> p t c", t=T)
        qn = part_of(3584, 512).rearrange("p (t c) -> p t c", t=T)
        kl = part_of(4096, 320).rearrange("p (t c) -> p t c", t=T)
        kvn = part_of(4416, 256).rearrange("p (t c) -> p t c", t=T)
        qn_t = part_of(3072, 512).rearrange("p (k s) -> p k s", k=2)
        kvn_t = part_of(5184, 256)
        uq = part_of(5440, 1536).rearrange("p (k c) -> p k c", k=2)
        ukv = part_of(6976, 1024)
        q_tok = part_of(8000, 1536).rearrange("p (t h c) -> p t h c", t=T, h=BH)
        k_tok = part_of(9536, 1536).rearrange("p (t h c) -> p t h c", t=T, h=BH)
        vb = part_of(11072, 1024).rearrange("p (t h c) -> p t h c", t=T, h=BH)
        qk_t = part_of(12096, 4096).rearrange("p (h s) -> p h s", h=BH)
        k_tmp = part_of(4672, 128).rearrange("p (n t c) -> p n t c", n=4, t=T)
        k_pe = part_of(4800, 64).rearrange("p (t c) -> p t c", t=T)
        q_tmp = part_of(3072, 1024).rearrange("p (n t h c) -> p n t h c", n=4, t=T, h=BH)
        bias_a = part_of(5440, 1024).rearrange("p (b s) -> p b s", b=2)
        s_sb = part_of(8000, 1024).rearrange("p (b s) -> p b s", b=2)
        prob = part_of(9024, 1024).rearrange("p (b s) -> p b s", b=2)
        prob_t = part_of(10048, 1024).rearrange("p (b s) -> p b s", b=2)
        qc_t = part_of(0, 2048).rearrange("p (m s) -> p m s", m=8)
        kc_t = part_of(2048, 2048).rearrange("p (m s) -> p m s", m=8)
        vc = part_of(4096, 2048).rearrange("p (t c) -> p t c", t=T)
        rpb = part_of(11072, CH * RPB_RUN).rearrange("p (h f) -> p h f", h=CH)
        act_g = part_of(0, 512)
        hid = part_of(512, 512)
        x_t = part_of(1024, 2048).rearrange("p (k s) -> p k s", k=KD)
        y_sb = part_of(3072, 1024)
        comb = part_of(4096, 256)
        pick = part_of(4352, 256).rearrange("p (t s) -> p t s", t=T)
        pick_g = part_of(4608, 256).rearrange("p (t s) -> p t s", t=T)
        r = part_of(4864, 256)
        logits = r[:, 0:16].rearrange("p (t e) -> p t e", t=T)
        top_v = r[:, 16:32].rearrange("p (t e) -> p t e", t=T)
        top_f = r[:, 32:48].rearrange("p (t e) -> p t e", t=T)
        one_a = r[:, 48:64].rearrange("p (t e) -> p t e", t=T)
        one_b = r[:, 64:80].rearrange("p (t e) -> p t e", t=T)
        gate = r[:, 80:96].rearrange("p (t e) -> p t e", t=T)
        mask = r[:, 96:112].rearrange("p (t e) -> p t e", t=T)
        place = r[:, 112:128].rearrange("p (t e) -> p t e", t=T)
        top_w = r[:, 128:136].rearrange("p (t c) -> p t c", t=T)
        place_e = r[:, 136:138]
        gate_e = r[:, 138:140]
        most = r[:, 140:141]
        top_i = sb("top_i", [P, T, 8], U32)
        over = sb("over", [P, 1], I32)

        sums_sq = small[:, 0:2]
        mean_sq = small[:, 2:4]
        std = small[:, 4:6]
        rstd = small[:, 6:8]
        lat_ss = small[:, 8:12]
        lat_ms = small[:, 12:16]
        lat_std = small[:, 16:20]
        lat_rstd = small[:, 20:24]
        neg_max = small[:, 24:28].rearrange("p (b t) -> p b t", b=2)
        row_sum = small[:, 28:60].rearrange("p (t h) -> p t h", t=T)

        raw_full = [sem(f"raw_full{i}") for i in range(RING)]
        hi_done, lo_done, used = sem("hi_done"), sem("lo_done"), sem("used")
        tables_in, x_in, gain_in = sem("tables_in"), sem("x_in"), [sem(f"gain_in{i}") for i in range(5)]
        lat_in, router_in, rpb_in = sem("lat_in"), sem("router_in"), sem("rpb_in")
        tab_b = sem("tab_b")
        ss_done, ms_done = sem("ss_done"), sem("ms_done")
        std_done, rstd_done, xn_ready = sem("std_done"), sem("rstd_done"), sem("xn_ready")
        t_mm, t_hi_done, t_lo_done = sem("t_mm"), sem("t_hi_done"), sem("t_lo_done")
        proj_mm, proj_out = sem("proj_mm"), sem("proj_out")
        lat_a, lat_v, lat_p = sem("lat_a"), sem("lat_v"), sem("lat_p")
        bias_step, bias_ready = sem("bias_step"), sem("bias_ready")
        s_mm, s_read, s_biased = sem("s_mm"), sem("s_read"), sem("s_biased")
        max_step, max_ready = sem("max_step"), sem("max_ready")
        exp_done, pt_mm, pt_out, pv_mm = sem("exp_done"), sem("pt_mm"), sem("pt_out"), sem("pv_mm")
        inv_done = sem("inv_done")
        res_mm, x_upd = sem("res_mm"), sem("x_upd")
        gu_mm, silu_done, hid_done = sem("gu_mm"), sem("silu_done"), sem("hid_done")
        h_hi_done, h_lo_done = sem("h_hi_done"), sem("h_lo_done")
        route_v, route_mm, route_a = sem("route_v"), sem("route_mm"), sem("route_a")
        over_set = sem("over_set")
        pick_step, pick_ready, gath_mm = sem("pick_step"), sem("pick_ready"), sem("gath_mm")
        gath_hi, gath_lo = sem("gath_hi"), sem("gath_lo")
        pickg_step, pickg_ready = sem("pickg_step"), sem("pickg_ready")
        comb_mm, comb_out = sem("comb_mm"), sem("comb_out")
        ht_mm = sem("ht_mm")
        y_mm, y_out, scat_mm, y_add = sem("y_mm"), sem("y_out"), sem("scat_mm"), sem("y_add")
        out_ready, out_sent = sem("out_ready"), sem("out_sent")

        w_in = w_in_e[0].rearrange("(k p) n -> p k n", p=P)
        w_out = w_out_e[0].rearrange("(k p) n -> p k n", p=P)
        w_fg = ffn_w_gate[0].rearrange("(k p) n -> p k n", p=P)
        w_fu = ffn_w_up[0].rearrange("(k p) n -> p k n", p=P)
        w_fd = ffn_w_down[0].rearrange("(k p) n -> p k n", p=P)
        w_qkv = na_w_qkv[0].rearrange("(k p) n -> p k n", p=P)
        w_no = na_w_out[0].rearrange("(k p) n -> p k n", p=P)
        w_eg = moe_w_gate[0].rearrange("e (k p) n -> e p k n", p=P)
        w_eu = moe_w_up[0].rearrange("e (k p) n -> e p k n", p=P)
        w_ed = moe_w_down[0].rearrange("e (k p) n -> e p k n", p=P)

        def over_partitions(vector, n):
            return bass.AP(vector.tensor, 0, [[0, P], [1, n]])

        block = ctx.enter_context(nc.Block())

        def moe_sweep(eng, edge, middle, sweep):
            base = U_MOE + sweep * E * MOE_UNITS
            edge(None, 0, base, sweep)
            with eng.Fori(0, E - 1) as e:
                with eng.Fori(0, MOE_STEPS - 2) as j:
                    middle(e, j, base, sweep)
                edge(e, e + 1, base, sweep)
            with eng.Fori(0, MOE_STEPS - 2) as j:
                middle(E - 1, j, base, sweep)
            edge(E - 1, None, base, sweep)

        def unit_of(base, e, c, j=0):
            return Unit(base + c, e * MOE_STEPS + j) if not (isinstance(e, int) and isinstance(j, int)) \
                else Unit(base + c + 6 * (e * MOE_STEPS + j))

        @block.sync
        def _(sp):
            def load(u, src):
                if not u.early(RING):
                    sp.wait_ge(lo_done, u.count(-RING))
                _, k, n = src.shape
                dst = raw[:, u.raw, 0:k * n].rearrange("p (k n) -> p k n", k=k)
                sp.dma_start(dst, src).then_inc(raw_full[u.raw], 16)

            sp.dma_start(xres[:], x[0].rearrange("(t p) d -> p t d", p=P)).then_inc(x_in, 16)
            for i, (c0, n) in enumerate(IN_COLS):
                load(Unit(U_IN + i), w_in[:, :, c0:c0 + n])
            for i in range(4):
                load(Unit(U_OUT0 + i), w_out[:, 2 * i:2 * i + 2, :])

            load(Unit(U_FFN), w_fg[:, :, 0:256])
            load(Unit(U_FFN + 1), w_fu[:, :, 0:256])

            with sp.Fori(0, (FFN_STEPS - 1) // 2) as it:
                for jj in range(2):
                    cols = bass.ds(it * 512 + 256 * (jj + 1), 256)
                    load(Unit(U_FFN + 2 + 3 * jj, it), w_fg[:, :, cols])
                    load(Unit(U_FFN + 3 + 3 * jj, it), w_fu[:, :, cols])
                    load(Unit(U_FFN + 4 + 3 * jj, it), w_fd[:, bass.ds(it * 4 + 2 * jj, 2), :])
            load(Unit(U_FFN + 32), w_fd[:, 20:22, :])

            for i in range(12):
                load(Unit(U_QKV + i), w_qkv[:, :, 256 * i:256 * i + 256])
            for i in range(4):
                load(Unit(U_OUT1 + i), w_no[:, 2 * i:2 * i + 2, :])

            def gate_up(e, j, base, c):
                cols = bass.ds(j * HALF, HALF)
                for i, w in enumerate((w_eg, w_eg, w_eu, w_eu)):
                    k0 = 4 * (i % 2)
                    load(unit_of(base, *c[i]), w[e, :, k0:k0 + 4, cols])

            def down(e, j, base, c):
                for i in range(2):
                    load(unit_of(base, *c[i]), w_ed[e, :, bass.ds(j * 4 + 2 * i, 2), :])

            def middle(e, j, base, sweep):
                gate_up(e, j + 1, base, [(e, 4 + i, j) for i in range(4)])
                down(e, j, base, [(e, 8 + i, j) for i in range(2)])

            def edge(e, nxt, base, sweep):
                if e is not None:
                    gate_up(e, MOE_STEPS - 1, base, [(e, 34 + i, 0) for i in range(4)])
                    down(e, MOE_STEPS - 2, base, [(e, 38 + i, 0) for i in range(2)])
                if nxt is not None:
                    first = (nxt, 0) if e is None else (e, 40)
                    gate_up(nxt, 0, base, [(first[0], first[1] + i, 0) for i in range(4)])
                if e is not None:
                    down(e, MOE_STEPS - 1, base, [(e, (40 if nxt is None else 44) + i, 0) for i in range(2)])

            moe_sweep(sp, edge, middle, 0)
            sp.wait_ge(over_set, 1)
            n_over = sp.value_load(over[0:1, 0:1], min_val=0, max_val=SEQ)
            with sp.If(n_over > P):
                moe_sweep(sp, edge, middle, 1)
            with sp.Else():
                sp.nop()
            sp.wait_ge(out_ready, 1)
            sp.dma_start(out[0].rearrange("(t p) d -> p t d", p=P), xn[:]).then_inc(out_sent, 16)
            sp.wait_ge(out_sent, 16)

        @block.scalar
        def _(act):
            act.dma_start(tab[:], tables).then_inc(tables_in, 16)
            for n, g in enumerate((ln_mix_e, ln_ffn_e, ln_mix_o)):
                act.dma_start(gains[:, n, :], over_partitions(g, D)).then_inc(gain_in[n], 16)
                if n == 0:
                    act.dma_start(lat_gain[:, 0:QL], over_partitions(mla_q_norm, QL)).then_inc(lat_in, 16)
                    act.dma_start(lat_gain[:, QL:QL + KVL], over_partitions(mla_kv_norm, KVL)).then_inc(lat_in, 16)
                    act.dma_start(uq[:], mla_w_uq[0].rearrange("(k p) n -> p k n", p=P)).then_inc(lat_in, 16)
                    act.dma_start(ukv[:], mla_w_ukv[0]).then_inc(lat_in, 16)
            act.dma_start(router[:], moe_router[0].rearrange("(k p) n -> p k n", p=P)).then_inc(router_in, 16)

            def hi(u, n=UNIT):
                act.wait_ge(raw_full[u.raw], u.filled())
                if not u.early(PARTS):
                    act.wait_ge(used, u.count(-PARTS))
                act.copy(w_hi[:, u.part, 0:n], raw[:, u.raw, 0:n]).then_inc(hi_done, 1)

            def norm_stats(n):
                if n == 0:
                    act.wait_ge(x_in, 16)
                else:
                    act.wait_ge(x_upd, n)
                for t in range(T):
                    last = act.activation(xn[:, t, :], xres[:, t, :], ACT.Square, accum_out=sums_sq[:, t:t + 1])
                last.then_inc(ss_done, 1)
                act.wait_ge(ms_done, n + 1)
                act.activation(std, mean_sq, ACT.Sqrt).then_inc(std_done, 1)

            def split_t_hi(q):
                for i in range(4):
                    act.wait_ge(t_mm, 4 * q + i + 1)
                    act.copy(t_hi[:, 2 * i:2 * i + 2, :],
                             banks[:, i, :].rearrange("p (k s) -> p k s", k=2)).then_inc(t_hi_done, 1)

            norm_stats(0)
            hi(Unit(0))
            act.wait_ge(tables_in, 16)
            act.copy(mask_b[:], tab[:, C_MASK:C_MASK + SEQ]).then_inc(tab_b, 1)
            act.copy(ident_b[:], ident).then_inc(tab_b, 1)
            split_t_hi(0)
            act.wait_ge(xn_ready, 1)
            act.dma_start(gains[:, 0, :], over_partitions(ln_ffn_o, D)).then_inc(gain_in[3], 16)

            in_dst = [ql[:], kl[:]] + [m[:, 2 * i:2 * i + 2, :] for m in (qa_t, ka_t) for i in range(2)] \
                + [va[:, :, 0:256], va[:, :, 256:512]]

            def in_out(i):
                act.wait_ge(proj_mm, i + 1)
                src = banks[:, 4 + i % 4, :].rearrange("p (a b) -> p a b", a=2)[:, :, 0:IN_COLS[i][1]]
                act.copy(in_dst[i], src).then_inc(proj_out, 1)

            def in_hi(i):
                hi(Unit(i), 8 * IN_COLS[i][1])

            in_hi(1)
            in_hi(2)
            in_out(0)
            in_hi(3)
            in_out(1)
            act.wait_ge(proj_out, 2)
            for t in range(T):
                act.activation(qn[:, t, :], ql[:, t, :], ACT.Square, accum_out=lat_ss[:, t:t + 1])
                last = act.activation(kvn[:, t, :], kl[:, t, 0:KVL], ACT.Square, accum_out=lat_ss[:, 2 + t:3 + t])
            last.then_inc(lat_a, 1)
            act.wait_ge(lat_v, 1)
            act.activation(lat_std, lat_ms, ACT.Sqrt).then_inc(lat_a, 1)
            in_hi(4)
            in_out(2)
            in_hi(5)
            in_out(3)
            act.wait_ge(lat_p, 1)
            act.copy(qn_t[:], banks[:, 0, :].rearrange("p (k s) -> p k s", k=2))
            act.copy(kvn_t[:], banks[:, 1, 0:SEQ]).then_inc(lat_a, 1)
            in_hi(6)
            in_out(4)
            act.wait_ge(lat_p, 2)
            q_flat = q_tok.rearrange("p t h c -> p t (h c)")
            for t, b in enumerate((2, 0)):
                act.copy(q_flat[:, t, 0:512], banks[:, b, :])
                last = act.copy(q_flat[:, t, 512:768], banks[:, b + 1, 0:256])
            last.then_inc(lat_a, 1)
            in_hi(7)
            in_out(5)
            act.wait_ge(lat_p, 3)
            for b in range(2):
                src = banks[:, b, :].rearrange("p (h c) -> p h c", h=4)
                act.copy(k_tok[:, 0, 4 * b:4 * b + 4, 0:HD], src[:, :, 0:HD])
                last = act.copy(vb[:, 0, 4 * b:4 * b + 4, :], src[:, :, HD:2 * HD])
            last.then_inc(lat_a, 1)
            in_out(6)
            in_out(7)
            for i in range(3):
                hi(Unit(U_OUT0 + i))
            for h in range(0, BH, 2):
                act.wait_ge(lat_p, 4 + h)
                act.copy(qk_t[0:BK, h, :], banks[0:BK, h % 4, :]).then_inc(lat_a, 1)

            def softmax(n, kind, h):
                b = n % 2
                act.wait_ge(max_ready, n + 1)
                if n >= 2:
                    act.wait_ge(pt_mm, n - 1)
                for t in range(T):
                    src = banks[:, b, t * SEQ:(t + 1) * SEQ] if kind == "latent" else s_sb[:, b, t * SEQ:(t + 1) * SEQ]
                    last = act.activation(prob[:, b, t * SEQ:(t + 1) * SEQ], src, ACT.Exp,
                                          bias=neg_max[:, b, t:t + 1],
                                          scale=BK ** -0.5 if kind == "latent" else 1.0,
                                          accum_out=row_sum[:, t, n % 16:n % 16 + 1])
                last.then_inc(exp_done, 1)

            def prob_out(n):
                act.wait_ge(pt_mm, n + 1)
                if n >= 2:
                    act.wait_ge(pv_mm, n - 1)
                act.copy(prob_t[:, n % 2, :], banks[:, 2 + n % 2, :]).then_inc(pt_out, 1)

            for n in range(AH + BH):
                softmax(n, "dilated" if n < AH else "latent", n % 8)
                if n:
                    prob_out(n - 1)
            prob_out(AH + BH - 1)
            split_t_hi(1)
            for i in range(4):
                hi(Unit(U_OUT0 + 3 + i))

            norm_stats(1)
            split_t_hi(2)
            for half in range(2):
                src = bass.AP(na_rpb.tensor, (5 - half) * RPB_C + NA_COLS - GRID_W,
                              [[1, GRID_W], [RPB_R * RPB_C, CH], [1, RPB_RUN]])
                act.dma_start(rpb[GRID_W * half:GRID_W * (half + 1)], src).then_inc(rpb_in, 16)

            def ffn_act(j, jj):
                act.wait_ge(gu_mm, j + 1)
                act.activation(act_g[:], banks[:, 4 + 2 * jj, :], ACT.Silu).then_inc(silu_done, 1)
                act.wait_ge(hid_done, j + 1)
                act.copy(h_hi[:, jj, :], hid[:]).then_inc(h_hi_done, 1)

            ffn_act(0, 0)
            with act.Fori(0, (FFN_STEPS - 1) // 2) as it:
                for jj in range(2):
                    for i in range(3):
                        hi(Unit(U_FFN + 3 + 3 * jj + i, it))
                    ffn_act(it * 2 + (jj + 1), (jj + 1) % 2)
            for i in range(3):
                hi(Unit(U_QKV + i))
            norm_stats(2)
            split_t_hi(3)
            act.wait_ge(xn_ready, 3)
            act.dma_start(gains[:, 1, :], over_partitions(ln_final, D)).then_inc(gain_in[4], 16)

            c_dst = [m[:, 2 * i:2 * i + 2, :] for m in (qc_t, kc_t) for i in range(4)] \
                + [vc[:, :, 256 * i:256 * i + 256] for i in range(4)]

            def qkv_out(i):
                act.wait_ge(proj_mm, 8 + i + 1)
                act.copy(c_dst[i], banks[:, 4 + i % 4, :].rearrange("p (a b) -> p a b", a=2)).then_inc(proj_out, 1)

            for i in range(12):
                hi(Unit(U_QKV + 3 + i))
                qkv_out(i)

            for n in range(16, 16 + CH):
                softmax(n, "neighbourhood", n - 16)
                if n > 16:
                    prob_out(n - 1)
            prob_out(15 + CH)
            split_t_hi(4)
            for i in range(4):
                hi(Unit(U_OUT1 + 3 + i))
            norm_stats(3)
            for i in range(4):
                act.wait_ge(t_mm, 20 + i + 1)
                act.copy(x_t[:, 2 * i:2 * i + 2, :],
                         banks[:, i, :].rearrange("p (k s) -> p k s", k=2)).then_inc(t_hi_done, 1)
            act.wait_ge(route_v, 1)
            act.activation(top_w[:, :, 1], top_w[:, :, 0], ACT.Exp).then_inc(route_a, 1)

            def gather_hi(v):
                for i in range(2):
                    act.wait_ge(gath_mm, v * 2 + (i + 1))
                    act.copy(t_hi[:, 4 * i:4 * i + 4, 0:P],
                             banks[:, 2 + i, :].rearrange("p (k s) -> p k s", k=4)).then_inc(gath_hi, 1)

            def silu(s):
                act.wait_ge(gu_mm, s + (FFN_STEPS + 1))
                act.activation(act_g[:], banks[:, 4, :], ACT.Silu).then_inc(silu_done, 1)

            def hid_t_hi(s):
                act.wait_ge(ht_mm, s + 1)
                act.copy(h_hi[:, 0, :], banks[:, 6, :]).then_inc(h_hi_done, 1)

            def comb_copy(v):
                act.wait_ge(comb_mm, v + 1)
                act.copy(comb[:], banks[:, 7, 0:SEQ]).then_inc(comb_out, 1)

            def y_copy(v):
                act.wait_ge(y_mm, v + 1)
                act.copy(y_sb[:].rearrange("p (a b) -> p a b", a=2), banks[:, 0:2, :]).then_inc(y_out, 1)

            def middle(e, j, base, sweep):
                s = (e + sweep * E) * MOE_STEPS + j + 1
                for c in (6, 7, 8, 9):
                    hi(unit_of(base, e, c, j))
                silu(s)
                hi(unit_of(base, e, 10, j))
                hi(unit_of(base, e, 11, j))
                hid_t_hi(s)

            def edge(e, nxt, base, sweep):
                if e is None:
                    gather_hi(sweep * E)
                    for c in range(0 if sweep else 3, 4):
                        hi(unit_of(base, 0, c))
                    silu(sweep * E * MOE_STEPS)
                    hi(unit_of(base, 0, 4))
                    hi(unit_of(base, 0, 5))
                    hid_t_hi(sweep * E * MOE_STEPS)
                    return
                v = e + sweep * E
                s = v * MOE_STEPS + (MOE_STEPS - 1)
                for c in (36, 37, 38, 39):
                    hi(unit_of(base, e, c))
                if nxt is not None:
                    gather_hi(v + 1)
                silu(s)
                hi(unit_of(base, e, 40))
                hi(unit_of(base, e, 41))
                hid_t_hi(s)
                if nxt is not None:
                    for c in (42, 43, 44, 45):
                        hi(unit_of(base, e, c))
                    silu(s + 1)
                    hi(unit_of(base, e, 46))
                    hi(unit_of(base, e, 47))
                y_copy(v)
                if nxt is not None:
                    hid_t_hi(s + 1)
                comb_copy(v)

            moe_sweep(act, edge, middle, 0)
            act.wait_ge(over_set, 1)
            n_over = act.value_load(over[0:1, 0:1], min_val=0, max_val=SEQ)
            with act.If(n_over > P):
                moe_sweep(act, edge, middle, 1)
            with act.Else():
                act.nop()
            norm_stats(4)

        @block.vector
        def _(dve):
            dve.memset(zero_b[:], 0.0).then_inc(tab_b, 1)
            dve.engine_nop().then_inc(y_add, 1)

            def lo(u, n=UNIT):
                dve.wait_ge(hi_done, u.count())
                dve.tensor_tensor(w_lo[:, u.part, 0:n], raw[:, u.raw, 0:n],
                                  w_hi[:, u.part, 0:n].bitcast(F32), ALU.subtract).then_inc(lo_done, 1)

            def norm_apply(n, gain):
                dve.wait_ge(ss_done, n + 1)
                dve.tensor_scalar(mean_sq, sums_sq, 1.0 / D, EPS, ALU.mult, ALU.add).then_inc(ms_done, 1)
                dve.wait_ge(std_done, n + 1)
                dve.reciprocal(rstd, std).then_inc(rstd_done, 1)
                dve.wait_ge(rstd_done, n + 1)
                dve.wait_ge(gain_in[n], 16)
                for t in range(T):
                    last = dve.scalar_tensor_tensor(out=xn[:, t, :], in0=xres[:, t, :], scalar=rstd[:, t:t + 1],
                                                    in1=gains[:, gain, :], op0=ALU.mult, op1=ALU.mult)
                last.then_inc(xn_ready, 1)

            def split_t_lo(q, job):
                for i in range(4):
                    dve.wait_ge(t_hi_done, 4 * q + i + 1)
                    dve.tensor_tensor(t_lo[:, 2 * i:2 * i + 2, :],
                                      banks[:, i, :].rearrange("p (k s) -> p k s", k=2),
                                      t_hi[:, 2 * i:2 * i + 2, :].bitcast(F32), ALU.subtract).then_inc(t_lo_done, 1)

            norm_apply(0, 0)
            lo(Unit(0))
            split_t_lo(0, 0)

            def in_lo(i):
                lo(Unit(i), 8 * IN_COLS[i][1])

            for i in range(1, 4):
                in_lo(i)
            dve.wait_ge(lat_a, 1)
            dve.tensor_scalar(lat_ms[:, 0:2], lat_ss[:, 0:2], 1.0 / QL, EPS, ALU.mult, ALU.add)
            dve.tensor_scalar(lat_ms[:, 2:4], lat_ss[:, 2:4], 1.0 / KVL, EPS, ALU.mult, ALU.add).then_inc(lat_v, 1)
            dve.wait_ge(lat_a, 2)
            dve.reciprocal(lat_rstd, lat_std).then_inc(lat_v, 1)
            dve.wait_ge(lat_v, 2)
            dve.wait_ge(lat_in, 64)
            for t in range(T):
                dve.scalar_tensor_tensor(out=qn[:, t, :], in0=ql[:, t, :], scalar=lat_rstd[:, t:t + 1],
                                         in1=lat_gain[:, 0:QL], op0=ALU.mult, op1=ALU.mult)
                last = dve.scalar_tensor_tensor(out=kvn[:, t, :], in0=kl[:, t, 0:KVL],
                                                scalar=lat_rstd[:, 2 + t:3 + t],
                                                in1=lat_gain[:, QL:QL + KVL], op0=ALU.mult, op1=ALU.mult)
            last.then_inc(lat_v, 1)
            in_lo(4)

            cos = tab[:, C_COS:C_COS + 32].rearrange("p (t c) -> p t c", t=T)
            sin = tab[:, C_SIN:C_SIN + 32].rearrange("p (t c) -> p t c", t=T)
            dve.wait_ge(tables_in, 16)

            def rope(x1, x2, c, s, tmp, y1, y2, step):
                dve.tensor_tensor(tmp(0), x1, c, ALU.mult)
                dve.tensor_tensor(tmp(1), x2, s, ALU.mult)
                dve.tensor_tensor(tmp(2), x1, s, ALU.mult)
                dve.tensor_tensor(tmp(3), x2, c, ALU.mult).then_inc(lat_v, 1)
                dve.wait_ge(lat_v, step + 1)
                dve.tensor_tensor(y1, tmp(0), tmp(1), ALU.subtract)
                dve.tensor_tensor(y2, tmp(2), tmp(3), ALU.add).then_inc(lat_v, 1)

            rope(kl[:, :, KVL:KVL + 16], kl[:, :, KVL + 16:KVL + 32], cos, sin,
                 lambda i: k_tmp[:, i], k_pe[:, :, 0:16], k_pe[:, :, 16:32], 3)
            in_lo(5)
            dve.wait_ge(lat_v, 5)
            for t in range(T):
                dve.tensor_copy(k_tok[:, t, :, HD:BK], k_pe[:, t, :].unsqueeze(1).broadcast_to([P, BH, ROPE]))
            in_lo(6)
            dve.wait_ge(lat_a, 4)
            cos_h = cos.unsqueeze(2).broadcast_to([P, T, BH, 16])
            sin_h = sin.unsqueeze(2).broadcast_to([P, T, BH, 16])
            rope(q_tok[:, :, :, HD:HD + 16], q_tok[:, :, :, HD + 16:BK], cos_h, sin_h,
                 lambda i: q_tmp[:, i], q_tok[:, :, :, HD:HD + 16], q_tok[:, :, :, HD + 16:BK], 5)
            in_lo(7)
            dve.wait_ge(lat_p, 3)
            for b in range(2):
                src = banks[:, 2 + b, :].rearrange("p (h c) -> p h c", h=4)
                dve.tensor_copy(k_tok[:, 1, 4 * b:4 * b + 4, 0:HD], src[:, :, 0:HD])
                last = dve.tensor_copy(vb[:, 1, 4 * b:4 * b + 4, :], src[:, :, HD:2 * HD])
            last.then_inc(lat_v, 1)
            for i in range(3):
                lo(Unit(U_OUT0 + i))
            for h in range(1, BH, 2):
                dve.wait_ge(lat_p, 4 + h)
                dve.tensor_copy(qk_t[0:BK, h, :], banks[0:BK, h % 4, :]).then_inc(lat_v, 1)

            def row_max(n, kind, h):
                b = n % 2
                dve.wait_ge(s_mm, n + 1)
                if n >= 2:
                    dve.wait_ge(exp_done, n - 1)
                scores = banks[:, b, :]
                if kind == "latent":
                    dve.tensor_reduce(neg_max[:, b, :], scores.rearrange("p (t s) -> p t s", t=T), AX_X, ALU.max,
                                      negate=True).then_inc(max_step, 1)
                    dve.wait_ge(max_step, h + 1)
                    dve.tensor_scalar(neg_max[:, b, :], neg_max[:, b, :], BK ** -0.5, None,
                                      ALU.mult).then_inc(max_ready, 1)
                    return
                if kind == "dilated":
                    dve.wait_ge(bias_ready, h + 1)
                    dve.scalar_tensor_tensor(out=s_sb[:, b, :], in0=scores, scalar=HD ** -0.5,
                                             in1=bias_a[:, h % 2, :], op0=ALU.mult, op1=ALU.add).then_inc(s_read, 1)
                else:
                    for t in range(T):
                        cut = slice(t * SEQ, (t + 1) * SEQ)
                        first = (2 - 2 * t) * RPB_C + GRID_W - 1
                        table = bass.AP(rpb.tensor, rpb[:, h, first:first + 1].offset,
                                        [[rpb.ap[0][0], P], [RPB_C, 4], [-1, GRID_W]])
                        last = dve.scalar_tensor_tensor(
                            out=s_sb[:, b, cut].rearrange("p (r c) -> p r c", r=4),
                            in0=scores[:, cut].rearrange("p (r c) -> p r c", r=4), scalar=HD ** -0.5,
                            in1=table, op0=ALU.mult, op1=ALU.add)
                    last.then_inc(s_read, 1)
                dve.wait_ge(s_read, n + 1 if n < 16 else n + 1 - BH)
                dve.tensor_reduce(neg_max[:, b, :], s_sb[:, b, :].rearrange("p (t s) -> p t s", t=T), AX_X, ALU.max,
                                  negate=True).then_inc(max_ready, 1)

            def head_group(g, bank, col):
                dve.wait_ge(pv_mm, 8 * g + 8)
                c0 = 8 * (g % 2)
                dve.reciprocal(row_sum[:, :, c0:c0 + 8], row_sum[:, :, c0:c0 + 8]).then_inc(inv_done, 1)
                dve.wait_ge(inv_done, g + 1)
                for t in range(T):
                    last = dve.tensor_tensor(
                        xn[:, t, col:col + 512].rearrange("p (h c) -> p h c", h=8),
                        banks[:, bank + t, :].rearrange("p (h c) -> p h c", h=8),
                        row_sum[:, t, c0:c0 + 8].unsqueeze(2).broadcast_to([P, 8, HD]), ALU.mult)
                return last

            for n in range(AH + BH):
                row_max(n, "dilated" if n < AH else "latent", n % 8)
                if n == 10:
                    head_group(0, 4, 0)
            head_group(1, 6, 512).then_inc(xn_ready, 1)
            split_t_lo(1, 1)

            def residual(bank, upd):
                dve.wait_ge(res_mm, upd)
                for t in range(T):
                    last = dve.tensor_tensor(xres[:, t, :].rearrange("p (a b) -> p a b", a=2),
                                             xres[:, t, :].rearrange("p (a b) -> p a b", a=2),
                                             banks[:, bank + 2 * t:bank + 2 * t + 2, :], ALU.add)
                last.then_inc(x_upd, 1)

            for i in range(3):
                lo(Unit(U_OUT0 + 3 + i))
            residual(4, 1)
            lo(Unit(U_FFN + 2))
            dve.wait_ge(x_upd, 1)
            norm_apply(1, 1)
            split_t_lo(2, 2)

            def ffn_dve(j, jj):
                dve.wait_ge(silu_done, j + 1)
                dve.tensor_tensor(hid[:], act_g[:], banks[:, 5 + 2 * jj, :], ALU.mult).then_inc(hid_done, 1)
                dve.wait_ge(h_hi_done, j + 1)
                dve.tensor_tensor(h_lo[:, jj, :], hid[:], h_hi[:, jj, :].bitcast(F32),
                                  ALU.subtract).then_inc(h_lo_done, 1)

            ffn_dve(0, 0)
            with dve.Fori(0, (FFN_STEPS - 1) // 2) as it:
                for jj in range(2):
                    for i in range(3):
                        lo(Unit(U_FFN + 3 + 3 * jj + i, it))
                    ffn_dve(it * 2 + (jj + 1), (jj + 1) % 2)
            lo(Unit(U_QKV))
            lo(Unit(U_QKV + 1))
            residual(0, 2)
            lo(Unit(U_QKV + 2))
            dve.wait_ge(x_upd, 2)
            norm_apply(2, 2)
            split_t_lo(3, 3)
            for i in range(12):
                lo(Unit(U_QKV + 3 + i))
            dve.wait_ge(rpb_in, 32)
            for n in range(16, 16 + CH):
                row_max(n, "neighbourhood", n - 16)
                if n == 26:
                    head_group(2, 4, 0)
            head_group(3, 6, 512).then_inc(xn_ready, 1)
            split_t_lo(4, 4)
            for i in range(3):
                lo(Unit(U_OUT1 + 3 + i))
            residual(4, 3)
            lo(Unit(U_OUT1 + 6))
            dve.wait_ge(x_upd, 3)
            norm_apply(3, 0)

            dve.wait_ge(route_mm, 1)
            dve.tensor_copy(logits[:], banks[:, 4, 0:16].rearrange("p (t e) -> p t e", t=T)).then_inc(route_v, 0) \
                if False else dve.tensor_copy(logits[:], banks[:, 4, 0:16].rearrange("p (t e) -> p t e", t=T)).then_inc(pickg_step, 1)
            dve.wait_ge(pickg_step, 1)
            for t in range(T):
                last = dve.max(out=top_v[:, t, :], in_=logits[:, t, :])
            last.then_inc(pickg_step, 1)
            dve.wait_ge(pickg_step, 2)
            dve.tensor_tensor(top_w[:, :, 0], top_v[:, :, 1], top_v[:, :, 0], ALU.subtract).then_inc(route_v, 1)
            for t in range(T):
                last = dve.max_index(out=top_i[:, t, :], in_max=top_v[:, t, :], in_values=logits[:, t, :])
            last.then_inc(pickg_step, 1)
            dve.wait_ge(pickg_step, 3)
            dve.tensor_copy(top_f[:], top_i[:]).then_inc(pickg_step, 1)
            dve.wait_ge(pickg_step, 4)
            experts = tab[:, C_IOTA:C_IOTA + E]
            for t in range(T):
                dve.tensor_scalar(one_a[:, t, :], experts, top_f[:, t, 0:1], None, ALU.is_equal)
                last = dve.tensor_scalar(one_b[:, t, :], experts, top_f[:, t, 1:2], None, ALU.is_equal)
            last.then_inc(pickg_step, 1)
            dve.wait_ge(pickg_step, 5)
            dve.tensor_tensor(mask[:], one_a[:], one_b[:], ALU.add).then_inc(route_v, 1)
            dve.wait_ge(route_a, 1)
            dve.tensor_scalar(top_w[:, :, 2], top_w[:, :, 1], 1.0, None, ALU.add).then_inc(pickg_step, 1)
            dve.wait_ge(pickg_step, 6)
            dve.reciprocal(top_w[:, :, 2], top_w[:, :, 2]).then_inc(pickg_step, 1)
            dve.wait_ge(pickg_step, 7)
            dve.tensor_tensor(top_w[:, :, 3], top_w[:, :, 1], top_w[:, :, 2], ALU.mult).then_inc(pickg_step, 1)
            dve.wait_ge(pickg_step, 8)
            for t in range(T):
                last = dve.tensor_scalar(gate[:, t, :], one_a[:, t, :], top_w[:, t, 2:3], None, ALU.mult)
            last.then_inc(pickg_step, 1)
            dve.wait_ge(pickg_step, 9)
            for t in range(T):
                last = dve.scalar_tensor_tensor(out=gate[:, t, :], in0=one_b[:, t, :], scalar=top_w[:, t, 3:4],
                                                in1=gate[:, t, :], op0=ALU.mult, op1=ALU.add)
            last.then_inc(pickg_step, 1)
            dve.wait_ge(route_mm, 2)
            dve.scalar_tensor_tensor(out=place[:], in0=banks[:, 5, 0:16].rearrange("p (t e) -> p t e", t=T),
                                     scalar=1.0, in1=mask[:], op0=ALU.add, op1=ALU.mult).then_inc(pickg_step, 1)
            dve.tensor_reduce(most, banks[:, 5, 16:24], AX_X, ALU.max).then_inc(pickg_step, 1)
            dve.wait_ge(pickg_step, 12)
            dve.tensor_scalar(place[:], place[:], -1.0, None, ALU.add).then_inc(route_v, 1)
            dve.tensor_copy(over[:], most).then_inc(over_set, 1)

            def gather_lo(v):
                for i in range(2):
                    dve.wait_ge(gath_hi, v * 2 + (i + 1))
                    dve.tensor_tensor(t_lo[:, 4 * i:4 * i + 4, 0:P],
                                      banks[:, 2 + i, :].rearrange("p (k s) -> p k s", k=4),
                                      t_hi[:, 4 * i:4 * i + 4, 0:P].bitcast(F32), ALU.subtract).then_inc(gath_lo, 1)

            def gated(s):
                dve.wait_ge(silu_done, s + (FFN_STEPS + 1))
                dve.tensor_tensor(hid[:], act_g[:], banks[:, 5, :], ALU.mult).then_inc(hid_done, 1)

            def hid_t_lo(s):
                dve.wait_ge(h_hi_done, s + (FFN_STEPS + 1))
                dve.tensor_tensor(h_lo[:, 0, :], banks[:, 6, :], h_hi[:, 0, :].bitcast(F32),
                                  ALU.subtract).then_inc(h_lo_done, 1)

            def add_y(v):
                for i, (t, c) in enumerate(((0, 0), (0, 1), (1, 0), (1, 1))):
                    dve.wait_ge(scat_mm, v * 4 + (i + 1))
                    cols = xres[:, t, c * HALF:(c + 1) * HALF]
                    if i == 0:
                        dve.wait_ge(y_add, v * 4 + 1)
                    dve.tensor_tensor(cols, cols, banks[:, (7, 2, 3, 7)[i], :], ALU.add).then_inc(y_add, 1)

            def middle(e, j, base, sweep):
                s = (e + sweep * E) * MOE_STEPS + j + 1
                for c in (6, 7, 8, 9):
                    lo(unit_of(base, e, c, j))
                gated(s)
                lo(unit_of(base, e, 10, j))
                lo(unit_of(base, e, 11, j))
                hid_t_lo(s)

            def edge(e, nxt, base, sweep):
                if e is None:
                    gather_lo(sweep * E)
                    for c in range(0 if sweep else 3, 4):
                        lo(unit_of(base, 0, c))
                    gated(sweep * E * MOE_STEPS)
                    lo(unit_of(base, 0, 4))
                    lo(unit_of(base, 0, 5))
                    hid_t_lo(sweep * E * MOE_STEPS)
                    return
                v = e + sweep * E
                s = v * MOE_STEPS + (MOE_STEPS - 1)
                for c in (36, 37, 38, 39):
                    lo(unit_of(base, e, c))
                if nxt is not None:
                    gather_lo(v + 1)
                gated(s)
                lo(unit_of(base, e, 40))
                lo(unit_of(base, e, 41))
                hid_t_lo(s)
                if nxt is not None:
                    for c in (42, 43, 44, 45):
                        lo(unit_of(base, e, c))
                    gated(s + 1)
                    lo(unit_of(base, e, 46))
                    lo(unit_of(base, e, 47))
                    hid_t_lo(s + 1)
                add_y(v)

            moe_sweep(dve, edge, middle, 0)
            dve.wait_ge(over_set, 1)
            n_over = dve.value_load(over[0:1, 0:1], min_val=0, max_val=SEQ)
            with dve.If(n_over > P):
                moe_sweep(dve, edge, middle, 1)
                dve.wait_ge(y_add, 2 * 4 * E + 1)
            with dve.Else():
                dve.wait_ge(y_add, 4 * E + 1)
            dve.engine_nop().then_inc(x_upd, 1)
            norm_apply(4, 1)
            dve.wait_ge(xn_ready, 7)
            dve.engine_nop().then_inc(out_ready, 1)

        @block.tensor
        def _(pe):
            def three(out, a_hi, a_lo, b_hi, b_lo, start, stop):
                pe.matmul(out, a_hi, b_hi, start=start, stop=False)
                pe.matmul(out, a_lo, b_hi, start=False, stop=False)
                return pe.matmul(out, a_hi, b_lo, start=False, stop=stop)

            def unit_parts(u, k, n):
                cut = lambda w: w[:, u.part, 0:k * n].rearrange("p (k n) -> p k n", k=k)
                return cut(w_hi), cut(w_lo)

            def transpose_xn(q, last_read):
                pe.wait_ge(xn_ready, q + 1)
                for s, v in last_read:
                    pe.wait_ge(s, v)
                for i in range(4):
                    for k in range(2):
                        for t in range(T):
                            c = (2 * i + k) * P
                            last = pe.transpose(banks[:, i, (2 * k + t) * P:(2 * k + t + 1) * P],
                                                xn[:, t, c:c + P], ident)
                    last.then_inc(t_mm, 1)

            def columns(u, bank, n, transposed):
                pe.wait_ge(lo_done, u.count())
                hi_w, lo_w = unit_parts(u, KD, n)
                for m in range(2):
                    cut = slice(m * P, (m + 1) * P)
                    dst = banks[:, bank, m * 256:m * 256 + (256 if transposed else n)]
                    for k in range(KD):
                        if transposed:
                            last = three(dst, hi_w[:, k, cut], lo_w[:, k, cut], t_hi[:, k, :], t_lo[:, k, :],
                                         k == 0, k == KD - 1)
                        else:
                            last = three(dst, t_hi[:, k, cut], t_lo[:, k, cut], hi_w[:, k, :], lo_w[:, k, :],
                                         k == 0, k == KD - 1)
                return last

            def rows(u, bank, lhs_hi, lhs_lo, n_t, start, stop):
                pe.wait_ge(lo_done, u.count())
                hi_w, lo_w = unit_parts(u, 2, D)
                for i in range(2):
                    for t in range(n_t):
                        for c in range(2):
                            cols = slice(c * HALF, (c + 1) * HALF)
                            last = three(banks[:, bank + 2 * t + c, :], lhs_hi(i, t), lhs_lo(i, t),
                                         hi_w[:, i, cols], lo_w[:, i, cols], start and i == 0, stop and i == 1)
                return last

            pe.wait_ge(tables_in, 16)
            transpose_xn(0, [])

            pe.wait_ge(t_hi_done, 4)
            pe.wait_ge(t_lo_done, 4)

            def in_proj(i):
                if i >= 4:
                    pe.wait_ge(proj_out, i - 3)
                columns(Unit(i), 4 + i % 4, IN_COLS[i][1], 2 <= i < 6).then_inc(used, 1)
                pe.wait_ge(used, i + 1)
                pe.nop().then_inc(proj_mm, 1)

            for i in range(4):
                in_proj(i)
            pe.wait_ge(lat_v, 3)
            for k in range(2):
                for t in range(T):
                    pe.transpose(banks[:, 0, (2 * k + t) * P:(2 * k + t + 1) * P], qn[:, t, k * P:(k + 1) * P], ident)
            for t in range(T):
                last = pe.transpose(banks[:, 1, t * P:(t + 1) * P], kvn[:, t, :], ident)
            last.then_inc(lat_p, 1)
            in_proj(4)
            pe.wait_ge(lat_a, 3)
            pe.wait_ge(lat_in, 64)
            for t, b in enumerate((2, 0)):
                for c0, n, bank in ((0, 512, b), (512, 256, b + 1)):
                    for k in range(2):
                        last = pe.matmul(banks[:, bank, 0:n], qn_t[:, k, t * P:(t + 1) * P], uq[:, k, c0:c0 + n],
                                         start=(k == 0), stop=(k == 1))
            last.then_inc(lat_p, 1)
            in_proj(5)
            in_proj(6)
            pe.wait_ge(lat_a, 4)
            for t in range(T):
                for c in range(2):
                    last = pe.matmul(banks[:, 2 * t + c, :], kvn_t[:, t * P:(t + 1) * P],
                                     ukv[:, c * HALF:(c + 1) * HALF], start=True, stop=True)
            last.then_inc(lat_p, 1)
            in_proj(7)
            pe.wait_ge(lat_a, 5)
            pe.wait_ge(lat_v, 8)
            for h in range(BH):
                if h >= 4:
                    pe.wait_ge(lat_a if h % 2 == 0 else lat_v, (6 if h % 2 == 0 else 9) + (h - 4) // 2)
                for i, src in enumerate((q_tok, q_tok, k_tok, k_tok)):
                    last = pe.transpose(banks[0:BK, h % 4, i * P:(i + 1) * P], src[:, i % 2, h, :], ident)
                last.then_inc(lat_p, 1)

            def scores(n, kind, h):
                b = n % 2
                if n >= 2:
                    if n - 2 < AH:
                        pe.wait_ge(s_read, n - 1)
                    elif n - 2 < AH + BH:
                        pe.wait_ge(exp_done, n - 1)
                    else:
                        pe.wait_ge(s_read, n - 1 - BH)
                if kind == "latent":
                    for t in range(T):
                        last = pe.matmul(banks[:, b, t * SEQ:(t + 1) * SEQ], qk_t[0:BK, h, t * P:(t + 1) * P],
                                         qk_t[0:BK, h, 2 * P:4 * P], start=True, stop=True)
                    last.then_inc(s_mm, 1)
                    return
                q, k = (qa_t, ka_t) if kind == "dilated" else (qc_t, kc_t)
                rows_h = slice(HD * (h % 2), HD * (h % 2) + HD)
                for t in range(T):
                    dst = banks[:, b, t * SEQ:(t + 1) * SEQ]
                    if kind == "neighbourhood":
                        pe.matmul(dst, ident_b[:], mask_b[:], start=True, stop=False)
                    last = pe.matmul(dst, q[rows_h, h // 2, t * P:(t + 1) * P], k[rows_h, h // 2, :],
                                     start=kind == "dilated", stop=True)
                last.then_inc(s_mm, 1)

            def turn_probs(n):
                pe.wait_ge(exp_done, n + 1)
                if n >= 2:
                    pe.wait_ge(pt_out, n - 1)
                b = n % 2
                for k in range(2):
                    for t in range(T):
                        last = pe.transpose(banks[:, 2 + b, (2 * k + t) * P:(2 * k + t + 1) * P],
                                            prob[:, b, t * SEQ + k * P:t * SEQ + (k + 1) * P], ident)
                last.then_inc(pt_mm, 1)

            def values(n, v, bank):
                pe.wait_ge(pt_out, n + 1)
                c = HD * (n % 8)
                for t in range(T):
                    for k in range(2):
                        last = pe.matmul(banks[:, bank + t, c:c + HD],
                                         prob_t[:, n % 2, (2 * k + t) * P:(2 * k + t + 1) * P], v(k),
                                         start=(k == 0), stop=(k == 1))
                last.then_inc(pv_mm, 1)

            pe.wait_ge(proj_out, 8)
            pe.wait_ge(lat_a, 9)
            pe.wait_ge(lat_v, 12)
            for n in range(AH + BH + 2):
                if n < AH + BH:
                    scores(n, "dilated" if n < AH else "latent", n % 8)
                if 1 <= n <= AH + BH:
                    turn_probs(n - 1)
                if n >= 2:
                    m = n - 2
                    if m < AH:
                        values(m, lambda k: va[:, k, m * HD:(m + 1) * HD], 4)
                    else:
                        values(m, lambda k: vb[:, k, m - AH, :], 6)
            transpose_xn(1, [])

            def out_proj(first, q):
                pe.wait_ge(t_hi_done, 4 * q + 4)
                pe.wait_ge(t_lo_done, 4 * q + 4)
                for i in range(4):
                    last = rows(Unit(first + i), 4, lambda k, t: t_hi[:, 2 * i + k, t * P:(t + 1) * P],
                                lambda k, t: t_lo[:, 2 * i + k, t * P:(t + 1) * P], T, i == 0, i == 3)
                    last.then_inc(used, 1)
                pe.wait_ge(used, first + 4)
                pe.nop().then_inc(res_mm, 1)

            out_proj(U_OUT0, 1)
            transpose_xn(2, [])
            pe.wait_ge(t_hi_done, 12)
            pe.wait_ge(t_lo_done, 12)

            def ffn_gate_up(u_g, u_u, j, jj):
                columns(u_g, 4 + 2 * jj, 256, True).then_inc(used, 1)
                columns(u_u, 5 + 2 * jj, 256, True).then_inc(used, 1)
                pe.wait_ge(used, u_u.count())
                pe.nop().then_inc(gu_mm, 1)

            def ffn_down(u, j, jj, stop=False):
                pe.wait_ge(h_hi_done, j + 1)
                pe.wait_ge(h_lo_done, j + 1)
                rows(u, 0, lambda k, t: h_hi[:, jj, k * SEQ + t * P:k * SEQ + (t + 1) * P],
                     lambda k, t: h_lo[:, jj, k * SEQ + t * P:k * SEQ + (t + 1) * P], T, False, stop).then_inc(used, 1)

            def clear(bank):
                return pe.matmul(banks[:, bank, :], zero_b[:, 0:P], zero_b[:], start=True, stop=False)

            pe.wait_ge(tab_b, 3)
            for b in range(4):
                clear(b)
            ffn_gate_up(Unit(U_FFN), Unit(U_FFN + 1), 0, 0)
            with pe.Fori(0, (FFN_STEPS - 1) // 2) as it:
                for jj in range(2):
                    ffn_gate_up(Unit(U_FFN + 2 + 3 * jj, it), Unit(U_FFN + 3 + 3 * jj, it), it * 2 + (jj + 1),
                                (jj + 1) % 2)
                    ffn_down(Unit(U_FFN + 4 + 3 * jj, it), it * 2 + jj, jj)
            ffn_down(Unit(U_FFN + 32), FFN_STEPS - 1, 0, True)
            pe.wait_ge(used, U_FFN + 33)
            pe.nop().then_inc(res_mm, 1)

            transpose_xn(3, [])
            pe.wait_ge(t_hi_done, 16)
            pe.wait_ge(t_lo_done, 16)
            for i in range(12):
                if i >= 4:
                    pe.wait_ge(proj_out, 8 + i - 3)
                columns(Unit(U_QKV + i), 4 + i % 4, 256, i < 8).then_inc(used, 1)
                pe.wait_ge(used, U_QKV + i + 1)
                pe.nop().then_inc(proj_mm, 1)
            pe.wait_ge(proj_out, 20)
            for n in range(16, 16 + CH + 2):
                if n < 16 + CH:
                    scores(n, "neighbourhood", n - 16)
                if 17 <= n <= 16 + CH:
                    turn_probs(n - 1)
                if n >= 18:
                    m = n - 18
                    values(n - 2, lambda k: vc[:, k, m * HD:(m + 1) * HD], 4 if m < 8 else 6)
            transpose_xn(4, [])
            out_proj(U_OUT1, 4)

            transpose_xn(5, [])
            pe.wait_ge(t_hi_done, 24)
            pe.wait_ge(router_in, 16)
            for t in range(T):
                for k in range(KD):
                    last = pe.matmul(banks[:, 4, E * t:E * t + E], x_t[:, k, t * P:(t + 1) * P], router[:, k, :],
                                     start=(k == 0), stop=(k == KD - 1))
            last.then_inc(route_mm, 1)
            pe.wait_ge(route_v, 2)
            pe.matmul(banks[:, 5, 0:E], tri, mask[:, 0, :], start=True, stop=True)
            pe.matmul(banks[:, 5, E:2 * E], tri, mask[:, 1, :], start=True, stop=False)
            pe.matmul(banks[:, 5, E:2 * E], ones, mask[:, 0, :], start=False, stop=True)
            pe.matmul(banks[:, 5, 2 * E:3 * E], ones, mask[:, 0, :], start=True, stop=False)
            pe.matmul(banks[:, 5, 2 * E:3 * E], ones, mask[:, 1, :], start=False, stop=True).then_inc(route_mm, 1)

            def gather(v):
                pe.wait_ge(pick_ready, v + 1)
                for k in range(KD):
                    dst = banks[:, 2 + k // 4, (k % 4) * P:(k % 4 + 1) * P]
                    for t in range(T):
                        last = pe.matmul(dst, xn[:, t, k * P:(k + 1) * P], pick[:, t, :], start=(t == 0), stop=(t == 1))
                    if k % 4 == 3:
                        last.then_inc(gath_mm, 1)

            def gate_up(base, units):
                for i in range(4):
                    u = unit_of(base, *units[i])
                    pe.wait_ge(lo_done, u.count())
                    hi_w, lo_w = unit_parts(u, 4, HALF)
                    for k in range(4):
                        kk = 4 * (i % 2) + k
                        last = three(banks[:, 4 + i // 2, :], t_hi[:, kk, 0:P], t_lo[:, kk, 0:P],
                                     hi_w[:, k, :], lo_w[:, k, :], kk == 0, kk == KD - 1)
                    last.then_inc(used, 1)
                pe.wait_ge(used, u.count())
                pe.nop().then_inc(gu_mm, 1)

            def moe_down(base, units, s, stop=False):
                pe.wait_ge(h_hi_done, s + (FFN_STEPS + 1))
                pe.wait_ge(h_lo_done, s + (FFN_STEPS + 1))
                for i in range(2):
                    u = unit_of(base, *units[i])
                    rows(u, 0, lambda k, t: h_hi[:, 0, (2 * i + k) * P:(2 * i + k + 1) * P],
                         lambda k, t: h_lo[:, 0, (2 * i + k) * P:(2 * i + k + 1) * P], 1, False, stop and i == 1).then_inc(used, 1)

            def turn_hid(s):
                pe.wait_ge(hid_done, s + (FFN_STEPS + 1))
                for k in range(4):
                    last = pe.transpose(banks[:, 6, k * P:(k + 1) * P], hid[:, k * P:(k + 1) * P], ident)
                last.then_inc(ht_mm, 1)

            def scatter(v):
                pe.wait_ge(pickg_ready, v + 1)
                for t in range(T):
                    last = pe.transpose(banks[:, 7, t * P:(t + 1) * P], pick_g[:, t, :], ident)
                last.then_inc(comb_mm, 1)
                pe.wait_ge(y_out, v + 1)
                pe.wait_ge(comb_out, v + 1)
                for i, (t, c) in enumerate(((0, 0), (0, 1), (1, 0), (1, 1))):
                    if i == 3:
                        pe.wait_ge(y_add, v * 4 + 2)
                    pe.matmul(banks[:, (7, 2, 3, 7)[i], :], comb[:, t * P:(t + 1) * P],
                              y_sb[:, c * HALF:(c + 1) * HALF], start=True, stop=True).then_inc(scat_mm, 1)

            def middle(e, j, base, sweep):
                s = (e + sweep * E) * MOE_STEPS + j + 1
                gate_up(base, [(e, 4 + i, j) for i in range(4)])
                moe_down(base, [(e, 8 + i, j) for i in range(2)], s - 1)
                turn_hid(s)

            def edge(e, nxt, base, sweep):
                if e is None:
                    gather(sweep * E)
                    pe.wait_ge(gath_lo, sweep * E * 2 + 2)
                    clear(0)
                    clear(1)
                    gate_up(base, [(0, i, 0) for i in range(4)])
                    turn_hid(sweep * E * MOE_STEPS)
                    return
                v = e + sweep * E
                s = v * MOE_STEPS + (MOE_STEPS - 1)
                gate_up(base, [(e, 34 + i, 0) for i in range(4)])
                if nxt is not None:
                    if not isinstance(v, int) or v > 0:
                        pe.wait_ge(y_add, v * 4 + 1)
                    gather(v + 1)
                moe_down(base, [(e, 38 + i, 0) for i in range(2)], s - 1)
                turn_hid(s)
                if nxt is not None:
                    pe.wait_ge(gath_lo, v * 2 + 4)
                    gate_up(base, [(e, 40 + i, 0) for i in range(4)])
                c = 40 if nxt is None else 44
                moe_down(base, [(e, c + i, 0) for i in range(2)], s, True)
                pe.wait_ge(used, unit_of(base, e, c + 1).count())
                pe.nop().then_inc(y_mm, 1)
                if nxt is not None:
                    turn_hid(s + 1)
                scatter(v)
                if nxt is not None:
                    clear(0)
                    clear(1)

            moe_sweep(pe, edge, middle, 0)
            pe.wait_ge(over_set, 1)
            n_over = pe.value_load(over[0:1, 0:1], min_val=0, max_val=SEQ)
            with pe.If(n_over > P):
                moe_sweep(pe, edge, middle, 1)
            with pe.Else():
                pe.nop()

        @block.gpsimd
        def _(pool):
            pool.wait_ge(tables_in, 16)
            pool.wait_ge(lat_p, 3)
            for h in range(AH):
                if h >= 2:
                    pool.wait_ge(s_read, h - 1)
                b = bias_a[:, h % 2, :]
                pool.tensor_scalar(b, tab[:, C_DIST:C_DIST + 512], 2.0 ** -(h + 1), None, ALU.mult).then_inc(bias_step, 1)
                pool.wait_ge(bias_step, h + 1)
                pool.tensor_tensor(b, b, tab[:, C_LNC:C_LNC + 512], ALU.add).then_inc(bias_ready, 1)

            def picks(e, sweep):
                v = e + sweep * E
                first = v == 0
                places = tab[:, C_IOTA + P * sweep:C_IOTA + P * (sweep + 1)]
                if first:
                    pool.wait_ge(route_v, 3)
                else:
                    pool.wait_ge(gath_mm, v * 2)
                    pool.wait_ge(pickg_ready, v)
                pool.tensor_copy(place_e.unsqueeze(2), place[:, :, e:e + 1])
                pool.tensor_copy(gate_e.unsqueeze(2), gate[:, :, e:e + 1]).then_inc(pick_step, 1)
                pool.wait_ge(pick_step, v + 1)
                for t in range(T):
                    last = pool.tensor_scalar(pick[:, t, :], places, place_e[:, t:t + 1], None, ALU.is_equal)
                last.then_inc(pick_ready, 1)
                if not first:
                    pool.wait_ge(comb_mm, v)
                for t in range(T):
                    last = pool.tensor_scalar(pick_g[:, t, :], places, place_e[:, t:t + 1], gate_e[:, t:t + 1],
                                              ALU.is_equal, ALU.mult)
                last.then_inc(pickg_ready, 1)

            for e in range(E):
                picks(e, 0)
            pool.wait_ge(over_set, 1)
            n_over = pool.value_load(over[0:1, 0:1], min_val=0, max_val=SEQ)
            with pool.If(n_over > P):
                for e in range(E):
                    picks(e, 1)
            with pool.Else():
                pool.nop()


_INS = ["x", "ln_mix_e", "w_in_e", "mla_q_norm", "mla_w_uq", "mla_kv_norm", "mla_w_ukv", "w_out_e",
        "ln_ffn_e", "ffn_w_gate", "ffn_w_up", "ffn_w_down", "ln_mix_o", "na_w_qkv", "na_rpb", "na_w_out",
        "ln_ffn_o", "moe_router", "moe_w_gate", "moe_w_up", "moe_w_down", "ln_final"]


def kernel(**inputs):
    import concourse.bacc as bacc
    from concourse.bass_utils import run_bass_kernel_spmd

    nc = bacc.Bacc("TRN2", target_bir_lowering=False, num_devices=1, dynamic_dma_scratch_size=1024)
    arrays = {f"in_{n}": np.ascontiguousarray(inputs[n]) for n in _INS}
    arrays["in_na_rpb"] = np.ascontiguousarray(inputs["na_rpb"][..., ::-1])
    arrays["in_tables"] = constants()
    args = [nc.dram_tensor(n, a.shape, mybir.dt.from_np(a.dtype), kind="ExternalInput").ap()
            for n, a in arrays.items()]
    y = nc.dram_tensor("out_y", (1, SEQ, D), F32, kind="ExternalOutput").ap()
    trunk(nc, *args, y)
    got = run_bass_kernel_spmd(nc, [arrays], core_ids=[0])
    return got.results[0]["out_y"]
```

```python
from contextlib import ExitStack

import numpy as np

import concourse.bass as bass
from concourse import mybir

ALU = mybir.AluOpType
ACT = mybir.ActivationFunctionType
F32 = mybir.dt.float32
F32R = mybir.dt.float32r
BF16 = mybir.dt.bfloat16
I32 = mybir.dt.int32
U32 = mybir.dt.uint32
AX_X = mybir.AxisListType.X

P = 128
D = 1024
SEQ = 256
T = SEQ // P
KD = D // P
HALF = 512
EPS = 1e-6
NEG = -1e30
HD = 64
AH, BH, CH = 8, 8, 16
A_W = AH * HD
QL, KVL, ROPE = 256, 128, 32
BK = HD + ROPE
D_FF = 2816
E, EFF = 8, 3584
GRID_W, NA_COLS = 64, 16
RPB_R, RPB_C = 15, 31
RPB_RUN = 5 * RPB_C + GRID_W

UNIT = 2048
RING = 6
PARTS = 3
FFN_STEPS = D_FF // 256
MOE_STEPS = EFF // HALF
MOE_UNITS = 6 * MOE_STEPS

U_IN = 0
U_OUT0 = U_IN + 8
U_FFN = U_OUT0 + 4
U_QKV = U_FFN + 3 * FFN_STEPS
U_OUT1 = U_QKV + 12
U_MOE = U_OUT1 + 4
IN_COLS = [(3 * A_W, QL), (3 * A_W + QL, KVL + ROPE)] + [(256 * i, 256) for i in range(6)]

S_BANK, T_BANK = (0, 1, 2, 7), (3, 6)

C_DIST, C_LNC = 0, 512
C_COS, C_SIN = 1024, 1056
C_MASK = 1088
C_ID, C_TRI, C_IOTA, C_ONES = 1152, 1280, 1408, 1664
C_ALL = 1792


def constants():
    c = np.zeros((P, C_ALL), np.float32)
    pos = np.arange(SEQ)
    d = np.abs(pos[:, None] - pos[None])
    cover = (d <= 64).astype(np.float64) + (d % 4 == 0) + (d % 16 == 0)
    lnc = np.where(cover > 0, np.log(np.maximum(cover, 1)), NEG).astype(np.float32)
    tiles = lambda a: a.reshape(T, P, -1).transpose(1, 0, 2).reshape(P, -1)
    c[:, C_DIST:C_DIST + 512] = tiles(-d.astype(np.float32))
    c[:, C_LNC:C_LNC + 512] = tiles(lnc)
    half = ROPE // 2
    freqs = np.float32(10000.0) ** (-np.arange(half, dtype=np.float32) / np.float32(half))
    ang = pos[:, None].astype(np.float32) * freqs[None].astype(np.float32)
    c[:, C_COS:C_COS + 32] = tiles(np.cos(ang.astype(np.float64)).astype(np.float32))
    c[:, C_SIN:C_SIN + 32] = tiles(np.sin(ang.astype(np.float64)).astype(np.float32))
    col = np.arange(P) % GRID_W
    first = np.clip(col - NA_COLS // 2, 0, GRID_W - NA_COLS)
    key = np.arange(GRID_W)
    inside = (key[None] >= first[:, None]) & (key[None] < first[:, None] + NA_COLS)
    c[:, C_MASK:C_MASK + GRID_W] = np.where(inside, 0.0, NEG)
    c[:, C_ID:C_ID + P] = np.eye(P)
    c[:, C_TRI:C_TRI + P] = np.triu(np.ones((P, P)), 1)
    c[:, C_IOTA:C_IOTA + 256] = np.arange(256)[None]
    c[:, C_ONES:C_ONES + P] = 1.0
    return c


class Unit:

    def __init__(self, s, k=0):
        self.s, self.k = s, k

    def count(self, ahead=0):
        return self.k * RING + (self.s + 1 + ahead)

    def early(self, back):
        return isinstance(self.k, int) and self.s < back

    @property
    def raw(self):
        return self.s % RING

    @property
    def part(self):
        return self.s % PARTS

    def filled(self):
        return self.k * 16 + 16 * (self.s // RING + 1)


def trunk(nc, x, ln_mix_e, w_in_e, mla_q_norm, mla_w_uq, mla_kv_norm, mla_w_ukv, w_out_e,
          ln_ffn_e, ffn_w_gate, ffn_w_up, ffn_w_down, ln_mix_o, na_w_qkv, na_rpb, na_w_out,
          ln_ffn_o, moe_router, moe_w_gate, moe_w_up, moe_w_down, ln_final, tables, out):
    with ExitStack() as ctx:
        def sb(name, shape, dt=F32):
            return ctx.enter_context(nc.sbuf_tensor(name, shape, dt))

        def sem(name):
            return ctx.enter_context(nc.semaphore(name))

        raw = sb("raw", [P, RING, UNIT])
        w_hi = sb("w_hi", [P, PARTS, UNIT], F32R)
        w_lo = sb("w_lo", [P, PARTS, UNIT], F32R)
        xres = sb("xres", [P, T, D])
        xn = sb("xn", [P, T, D])
        t_hi = sb("t_hi", [P, KD, SEQ], F32R)
        t_lo = sb("t_lo", [P, KD, SEQ], F32R)
        h_hi = sb("h_hi", [P, 2, HALF], F32R)
        h_lo = sb("h_lo", [P, 2, HALF], F32R)
        gains = sb("gains", [P, 3, D])
        lat_gain = sb("lat_gain", [P, QL + KVL])
        router = sb("router", [P, KD, E])
        tab = sb("tab", [P, C_ALL])
        mask_b = sb("mask_b", [P, SEQ], BF16)
        ident_b = sb("ident_b", [P, P], BF16)
        zero_b = sb("zero_b", [P, HALF], BF16)
        small = sb("small", [P, 76])
        arena = sb("arena", [P, 16192])
        banks = ctx.enter_context(nc.psum_tensor("banks", [P, 8, HALF], F32))

        ident = tab[:, C_ID:C_ID + P]
        tri = tab[:, C_TRI:C_TRI + P]
        ones = tab[:, C_ONES:C_ONES + P]

        def part_of(offset, n):
            return arena[:, offset:offset + n]

        qa_t = part_of(0, 1024).rearrange("p (m s) -> p m s", m=4)
        ka_t = part_of(1024, 1024).rearrange("p (m s) -> p m s", m=4)
        va = part_of(2048, 1024).rearrange("p (t c) -> p t c", t=T)
        ql = part_of(3072, 512).rearrange("p (t c) -> p t c", t=T)
        qn = part_of(3584, 512).rearrange("p (t c) -> p t c", t=T)
        kl = part_of(4096, 320).rearrange("p (t c) -> p t c", t=T)
        kvn = part_of(4416, 256).rearrange("p (t c) -> p t c", t=T)
        qn_t = part_of(3072, 512).rearrange("p (k s) -> p k s", k=2)
        kvn_t = part_of(5184, 256)
        uq = part_of(5440, 1536).rearrange("p (k c) -> p k c", k=2)
        ukv = part_of(6976, 1024)
        q_tok = part_of(8000, 1536).rearrange("p (t h c) -> p t h c", t=T, h=BH)
        k_tok = part_of(9536, 1536).rearrange("p (t h c) -> p t h c", t=T, h=BH)
        vb = part_of(11072, 1024).rearrange("p (t h c) -> p t h c", t=T, h=BH)
        qk_t = part_of(12096, 4096).rearrange("p (h s) -> p h s", h=BH)
        k_tmp = part_of(4672, 128).rearrange("p (n t c) -> p n t c", n=4, t=T)
        k_pe = part_of(4800, 64).rearrange("p (t c) -> p t c", t=T)
        q_tmp = part_of(3072, 1024).rearrange("p (n t h c) -> p n t h c", n=4, t=T, h=BH)
        bias_a = part_of(5440, 1024).rearrange("p (b s) -> p b s", b=2)
        prob = part_of(8000, 2048).rearrange("p (b s) -> p b s", b=4)
        prob_t = part_of(10048, 1024).rearrange("p (b s) -> p b s", b=2)
        qc_t = part_of(0, 2048).rearrange("p (m s) -> p m s", m=8)
        kc_t = part_of(2048, 2048).rearrange("p (m s) -> p m s", m=8)
        vc = part_of(4096, 2048).rearrange("p (t c) -> p t c", t=T)
        rpb = part_of(11072, CH * RPB_RUN).rearrange("p (h f) -> p h f", h=CH)
        act_g = part_of(0, 512)
        hid = part_of(512, 512)
        x_t = part_of(1024, 2048).rearrange("p (k s) -> p k s", k=KD)
        y_sb = part_of(3072, 1024)
        comb = part_of(4096, 256)
        pick = part_of(4352, 256).rearrange("p (t s) -> p t s", t=T)
        pick_g = part_of(4608, 256).rearrange("p (t s) -> p t s", t=T)
        r = part_of(4864, 256)
        logits = r[:, 0:16].rearrange("p (t e) -> p t e", t=T)
        top_v = r[:, 16:32].rearrange("p (t e) -> p t e", t=T)
        top_f = r[:, 32:48].rearrange("p (t e) -> p t e", t=T)
        one_a = r[:, 48:64].rearrange("p (t e) -> p t e", t=T)
        one_b = r[:, 64:80].rearrange("p (t e) -> p t e", t=T)
        gate = r[:, 80:96].rearrange("p (t e) -> p t e", t=T)
        mask = r[:, 96:112].rearrange("p (t e) -> p t e", t=T)
        place = r[:, 112:128].rearrange("p (t e) -> p t e", t=T)
        top_w = r[:, 128:136].rearrange("p (t c) -> p t c", t=T)
        place_e = r[:, 136:138]
        gate_e = r[:, 138:140]
        most = r[:, 140:141]
        top_i = sb("top_i", [P, T, 8], U32)
        over = sb("over", [P, 1], I32)

        sums_sq = small[:, 0:2]
        mean_sq = small[:, 2:4]
        std = small[:, 4:6]
        rstd = small[:, 6:8]
        warm_out = [small[:, i:i + 1] for i in range(64, 76)]
        lat_ss = small[:, 8:12]
        lat_ms = small[:, 12:16]
        lat_std = small[:, 16:20]
        lat_rstd = small[:, 20:24]
        neg_max = small[:, 24:32].rearrange("p (b t) -> p b t", b=4)
        row_sum = small[:, 32:64].rearrange("p (t h) -> p t h", t=T)

        raw_full = [sem(f"raw_full{i}") for i in range(RING)]
        hi_done, lo_done, used = sem("hi_done"), sem("lo_done"), sem("used")
        tables_in, x_in = sem("tables_in"), [sem("x_in0"), sem("x_in1")]
        gain_in = [sem(f"gain_in{i}") for i in range(5)]
        lat_in, router_in, rpb_in = sem("lat_in"), sem("router_in"), sem("rpb_in")
        tab_b = sem("tab_b")
        ss_done, ms_done = sem("ss_done"), sem("ms_done")
        std_done, rstd_done, xn_ready = sem("std_done"), sem("rstd_done"), sem("xn_ready")
        t_mm, t_hi_done, t_lo_done = sem("t_mm"), sem("t_hi_done"), sem("t_lo_done")
        proj_out = sem("proj_out")
        lat_a, lat_v, lat_p = sem("lat_a"), sem("lat_v"), sem("lat_p")
        bias_step, bias_ready = sem("bias_step"), sem("bias_ready")
        s_mm, s_read, s_biased = sem("s_mm"), sem("s_read"), sem("s_biased")
        max_step, max_ready = sem("max_step"), sem("max_ready")
        exp_done, pt_mm, pt_out, pv_mm = sem("exp_done"), sem("pt_mm"), sem("pt_out"), sem("pv_mm")
        inv_done, heads_out = sem("inv_done"), sem("heads_out")
        x_tile = sem("x_tile")
        silu_done, hid_done = sem("silu_done"), sem("hid_done")
        h_hi_done, h_lo_done = sem("h_hi_done"), sem("h_lo_done")
        route_v, route_mm, route_a = sem("route_v"), sem("route_mm"), sem("route_a")
        over_set = sem("over_set")
        pick_step, pick_ready, gath_mm = sem("pick_step"), sem("pick_ready"), sem("gath_mm")
        gath_hi, gath_lo = sem("gath_hi"), sem("gath_lo")
        pickg_step, pickg_ready = sem("pickg_step"), sem("pickg_ready")
        comb_mm, comb_out = sem("comb_mm"), sem("comb_out")
        ht_mm = sem("ht_mm")
        y_out, scat_mm, y_add = sem("y_out"), sem("scat_mm"), sem("y_add")
        out_sent = sem("out_sent")

        w_in = w_in_e[0].rearrange("(k p) n -> p k n", p=P)
        w_out = w_out_e[0].rearrange("(k p) n -> p k n", p=P)
        w_fg = ffn_w_gate[0].rearrange("(k p) n -> p k n", p=P)
        w_fu = ffn_w_up[0].rearrange("(k p) n -> p k n", p=P)
        w_fd = ffn_w_down[0].rearrange("(k p) n -> p k n", p=P)
        w_qkv = na_w_qkv[0].rearrange("(k p) n -> p k n", p=P)
        w_no = na_w_out[0].rearrange("(k p) n -> p k n", p=P)
        w_eg = moe_w_gate[0].rearrange("e (k p) n -> e p k n", p=P)
        w_eu = moe_w_up[0].rearrange("e (k p) n -> e p k n", p=P)
        w_ed = moe_w_down[0].rearrange("e (k p) n -> e p k n", p=P)

        def over_partitions(vector, n):
            return bass.AP(vector.tensor, 0, [[0, P], [1, n]])

        block = ctx.enter_context(nc.Block())

        def moe_sweep(eng, edge, middle, sweep):
            base = U_MOE + sweep * E * MOE_UNITS
            edge(None, 0, base, sweep)
            with eng.Fori(0, E - 1) as e:
                with eng.Fori(0, MOE_STEPS - 2) as j:
                    middle(e, j, base, sweep)
                edge(e, e + 1, base, sweep)
            with eng.Fori(0, MOE_STEPS - 2) as j:
                middle(E - 1, j, base, sweep)
            edge(E - 1, None, base, sweep)

        def unit_of(base, e, c, j=0):
            return Unit(base + c, e * MOE_STEPS + j) if not (isinstance(e, int) and isinstance(j, int)) \
                else Unit(base + c + 6 * (e * MOE_STEPS + j))

        @block.sync
        def _(sp):
            def load(u, src):
                if not u.early(RING):
                    sp.wait_ge(lo_done, u.count(-RING))
                _, k, n = src.shape
                dst = raw[:, u.raw, 0:k * n].rearrange("p (k n) -> p k n", k=k)
                sp.dma_start(dst, src).then_inc(raw_full[u.raw], 16)

            for t in range(T):
                sp.dma_start(xres[:, t, :], x[0, t * P:(t + 1) * P, :]).then_inc(x_in[t], 16)
            for i, (c0, n) in enumerate(IN_COLS):
                load(Unit(U_IN + i), w_in[:, :, c0:c0 + n])
            for i in range(4):
                load(Unit(U_OUT0 + i), w_out[:, 2 * i:2 * i + 2, :])

            load(Unit(U_FFN), w_fg[:, :, 0:256])
            load(Unit(U_FFN + 1), w_fu[:, :, 0:256])

            with sp.Fori(0, (FFN_STEPS - 1) // 2) as it:
                for jj in range(2):
                    cols = bass.ds(it * 512 + 256 * (jj + 1), 256)
                    load(Unit(U_FFN + 2 + 3 * jj, it), w_fg[:, :, cols])
                    load(Unit(U_FFN + 3 + 3 * jj, it), w_fu[:, :, cols])
                    load(Unit(U_FFN + 4 + 3 * jj, it), w_fd[:, bass.ds(it * 4 + 2 * jj, 2), :])
            load(Unit(U_FFN + 32), w_fd[:, 20:22, :])

            for i in range(12):
                load(Unit(U_QKV + i), w_qkv[:, :, 256 * i:256 * i + 256])
            for i in range(4):
                load(Unit(U_OUT1 + i), w_no[:, 2 * i:2 * i + 2, :])

            def gate_up(e, j, base, c):
                cols = bass.ds(j * HALF, HALF)
                for i, w in enumerate((w_eg, w_eg, w_eu, w_eu)):
                    k0 = 4 * (i % 2)
                    load(unit_of(base, *c[i]), w[e, :, k0:k0 + 4, cols])

            def down(e, j, base, c):
                for i in range(2):
                    load(unit_of(base, *c[i]), w_ed[e, :, bass.ds(j * 4 + 2 * i, 2), :])

            def middle(e, j, base, sweep):
                gate_up(e, j + 1, base, [(e, 4 + i, j) for i in range(4)])
                down(e, j, base, [(e, 8 + i, j) for i in range(2)])

            def edge(e, nxt, base, sweep):
                if e is not None:
                    gate_up(e, MOE_STEPS - 1, base, [(e, 34 + i, 0) for i in range(4)])
                    down(e, MOE_STEPS - 2, base, [(e, 38 + i, 0) for i in range(2)])
                if nxt is not None:
                    first = (nxt, 0) if e is None else (e, 40)
                    gate_up(nxt, 0, base, [(first[0], first[1] + i, 0) for i in range(4)])
                if e is not None:
                    down(e, MOE_STEPS - 1, base, [(e, (40 if nxt is None else 44) + i, 0) for i in range(2)])

            moe_sweep(sp, edge, middle, 0)
            sp.wait_ge(over_set, 1)
            n_over = sp.value_load(over[0:1, 0:1], min_val=0, max_val=SEQ)
            with sp.If(n_over > P):
                moe_sweep(sp, edge, middle, 1)
            with sp.Else():
                sp.nop()
            for t in range(T):
                sp.wait_ge(xn_ready, 12 + t + 1)
                sp.dma_start(out[0, t * P:(t + 1) * P, :], xn[:, t, :]).then_inc(out_sent, 16)
            sp.wait_ge(out_sent, 16 * T)

        @block.scalar
        def _(act):
            act.dma_start(tab[:], tables).then_inc(tables_in, 16)
            act.dma_start(gains[:, 0, :], over_partitions(ln_mix_e, D)).then_inc(gain_in[0], 16)

            def hi(u, n=UNIT):
                act.wait_ge(raw_full[u.raw], u.filled())
                if not u.early(PARTS):
                    act.wait_ge(used, u.count(-PARTS))
                act.copy(w_hi[:, u.part, 0:n], raw[:, u.raw, 0:n]).then_inc(hi_done, 1)

            def warm(func):
                act.activation(warm_out.pop(), ones[:, 0:1], func)

            def norm_stats(n, after=None):
                for t in range(T):
                    if n == 0:
                        act.wait_ge(x_in[t], 16)
                    else:
                        act.wait_ge(x_tile, 2 * n - 1 + t)
                    last = act.activation(xn[:, t, :], xres[:, t, :], ACT.Square, accum_out=sums_sq[:, t:t + 1])
                last.then_inc(ss_done, 1)
                warm(ACT.Sqrt)
                act.wait_ge(ms_done, n + 1)
                act.activation(std, mean_sq, ACT.Sqrt).then_inc(std_done, 1)
                if after is not None:
                    warm(after)

            def split_t_hi(q):
                for i in range(4):
                    act.wait_ge(t_mm, 4 * q + i + 1)
                    act.copy(t_hi[:, 2 * i:2 * i + 2, :],
                             banks[:, i, :].rearrange("p (k s) -> p k s", k=2)).then_inc(t_hi_done, 1)

            act.wait_ge(tables_in, 16)
            norm_stats(0)
            hi(Unit(0))
            act.copy(mask_b[:].rearrange("p (r c) -> p r c", r=4),
                     tab[:, C_MASK:C_MASK + GRID_W].unsqueeze(1).broadcast_to([P, 4, GRID_W])).then_inc(tab_b, 1)
            act.copy(ident_b[:], ident).then_inc(tab_b, 1)
            split_t_hi(0)
            act.dma_start(lat_gain[:, 0:QL], over_partitions(mla_q_norm, QL)).then_inc(lat_in, 16)
            act.dma_start(lat_gain[:, QL:QL + KVL], over_partitions(mla_kv_norm, KVL)).then_inc(lat_in, 16)
            act.dma_start(uq[:], mla_w_uq[0].rearrange("(k p) n -> p k n", p=P)).then_inc(lat_in, 16)
            act.dma_start(ukv[:], mla_w_ukv[0]).then_inc(lat_in, 16)
            act.dma_start(gains[:, 1, :], over_partitions(ln_ffn_e, D)).then_inc(gain_in[1], 16)
            act.dma_start(gains[:, 2, :], over_partitions(ln_mix_o, D)).then_inc(gain_in[2], 16)
            act.dma_start(router[:], moe_router[0].rearrange("(k p) n -> p k n", p=P)).then_inc(router_in, 16)
            act.wait_ge(xn_ready, 2)
            act.dma_start(gains[:, 0, :], over_partitions(ln_ffn_o, D)).then_inc(gain_in[3], 16)

            in_dst = [ql[:], kl[:]] + [m[:, 2 * i:2 * i + 2, :] for m in (qa_t, ka_t) for i in range(2)] \
                + [va[:, :, 0:256], va[:, :, 256:512]]

            def in_out(i):
                act.wait_ge(used, U_IN + i + 1)
                src = banks[:, 4 + i % 4, :].rearrange("p (a b) -> p a b", a=2)[:, :, 0:IN_COLS[i][1]]
                act.copy(in_dst[i], src).then_inc(proj_out, 1)

            def in_hi(i):
                hi(Unit(i), 8 * IN_COLS[i][1])

            in_hi(1)
            in_hi(2)
            in_out(0)
            in_hi(3)
            in_out(1)
            act.wait_ge(proj_out, 2)
            for t in range(T):
                act.activation(qn[:, t, :], ql[:, t, :], ACT.Square, accum_out=lat_ss[:, t:t + 1])
                last = act.activation(kvn[:, t, :], kl[:, t, 0:KVL], ACT.Square, accum_out=lat_ss[:, 2 + t:3 + t])
            last.then_inc(lat_a, 1)
            act.wait_ge(lat_v, 1)
            act.activation(lat_std, lat_ms, ACT.Sqrt).then_inc(lat_a, 1)
            warm(ACT.Exp)
            in_hi(4)
            in_out(2)
            in_hi(5)
            in_out(3)
            act.wait_ge(lat_p, 1)
            act.copy(qn_t[:], banks[:, 0, :].rearrange("p (k s) -> p k s", k=2))
            act.copy(kvn_t[:], banks[:, 1, 0:SEQ]).then_inc(lat_a, 1)
            in_hi(6)
            in_out(4)
            act.wait_ge(lat_p, 2)
            q_flat = q_tok.rearrange("p t h c -> p t (h c)")
            for t, b in enumerate((2, 0)):
                act.copy(q_flat[:, t, 0:512], banks[:, b, :])
                last = act.copy(q_flat[:, t, 512:768], banks[:, b + 1, 0:256])
            last.then_inc(lat_a, 1)
            in_hi(7)
            in_out(5)
            act.wait_ge(lat_p, 3)
            for b in range(2):
                src = banks[:, b, :].rearrange("p (h c) -> p h c", h=4)
                act.copy(k_tok[:, 0, 4 * b:4 * b + 4, 0:HD], src[:, :, 0:HD])
                last = act.copy(vb[:, 0, 4 * b:4 * b + 4, :], src[:, :, HD:2 * HD])
            last.then_inc(lat_a, 1)
            in_out(6)
            in_out(7)
            for i in range(3):
                hi(Unit(U_OUT0 + i))
            for h in range(0, BH, 2):
                act.wait_ge(lat_p, 4 + h)
                act.copy(qk_t[0:BK, h, :], banks[0:BK, h % 4, :]).then_inc(lat_a, 1)

            def softmax(n, kind, h):
                b = n % 4
                act.wait_ge(max_ready, n + 1)
                for t in range(T):
                    src = (banks[:, S_BANK[b]] if kind == "latent" else prob[:, b])[:, t * SEQ:(t + 1) * SEQ]
                    last = act.activation(prob[:, b, t * SEQ:(t + 1) * SEQ], src, ACT.Exp,
                                          bias=neg_max[:, b, t:t + 1],
                                          scale=BK ** -0.5 if kind == "latent" else 1.0,
                                          accum_out=row_sum[:, t, n % 16:n % 16 + 1])
                last.then_inc(exp_done, 1)

            def prob_out(n):
                act.wait_ge(pt_mm, n + 1)
                if n >= 2:
                    act.wait_ge(pv_mm, n - 1)
                act.copy(prob_t[:, n % 2, :], banks[:, T_BANK[n % 2], :]).then_inc(pt_out, 1)

            for n in range(AH + BH):
                softmax(n, "dilated" if n < AH else "latent", n % 8)
                if n >= 2:
                    prob_out(n - 2)
            prob_out(AH + BH - 2)
            prob_out(AH + BH - 1)
            split_t_hi(1)
            for i in range(4):
                hi(Unit(U_OUT0 + 3 + i))

            norm_stats(1, ACT.Silu)
            split_t_hi(2)
            for half in range(2):
                src = bass.AP(na_rpb.tensor, (5 - half) * RPB_C + NA_COLS - GRID_W,
                              [[1, GRID_W], [RPB_R * RPB_C, CH], [1, RPB_RUN]])
                act.dma_start(rpb[GRID_W * half:GRID_W * (half + 1)], src).then_inc(rpb_in, 16)

            def ffn_act(u, j, jj):
                act.wait_ge(used, u.count())
                act.activation(act_g[:], banks[:, 4 + 2 * jj, :], ACT.Silu).then_inc(silu_done, 1)
                act.wait_ge(hid_done, j + 1)
                act.copy(h_hi[:, jj, :], hid[:]).then_inc(h_hi_done, 1)

            ffn_act(Unit(U_FFN + 1), 0, 0)
            with act.Fori(0, (FFN_STEPS - 1) // 2) as it:
                for jj in range(2):
                    for i in range(3):
                        hi(Unit(U_FFN + 3 + 3 * jj + i, it))
                    ffn_act(Unit(U_FFN + 3 + 3 * jj, it), it * 2 + (jj + 1), (jj + 1) % 2)
            for i in range(3):
                hi(Unit(U_QKV + i))
            norm_stats(2, ACT.Exp)
            split_t_hi(3)
            act.wait_ge(xn_ready, 6)
            act.dma_start(gains[:, 1, :], over_partitions(ln_final, D)).then_inc(gain_in[4], 16)

            c_dst = [m[:, 2 * i:2 * i + 2, :] for m in (qc_t, kc_t) for i in range(4)] \
                + [vc[:, :, 256 * i:256 * i + 256] for i in range(4)]

            def qkv_out(i):
                act.wait_ge(used, U_QKV + i + 1)
                act.copy(c_dst[i], banks[:, 4 + i % 4, :].rearrange("p (a b) -> p a b", a=2)).then_inc(proj_out, 1)

            for i in range(12):
                hi(Unit(U_QKV + 3 + i))
                qkv_out(i)

            for n in range(16, 16 + CH):
                softmax(n, "neighbourhood", n - 16)
                if n >= 18:
                    prob_out(n - 2)
            prob_out(14 + CH)
            prob_out(15 + CH)
            split_t_hi(4)
            for i in range(4):
                hi(Unit(U_OUT1 + 3 + i))
            norm_stats(3, ACT.Exp)
            for i in range(4):
                act.wait_ge(t_mm, 20 + i + 1)
                act.copy(x_t[:, 2 * i:2 * i + 2, :],
                         banks[:, i, :].rearrange("p (k s) -> p k s", k=2)).then_inc(t_hi_done, 1)
            act.wait_ge(route_v, 1)
            act.activation(top_w[:, :, 1], top_w[:, :, 0], ACT.Exp).then_inc(route_a, 1)
            warm(ACT.Silu)

            def gather_hi(v):
                for i in range(2):
                    act.wait_ge(gath_mm, v * 2 + (i + 1))
                    act.copy(t_hi[:, 4 * i:4 * i + 4, 0:P],
                             banks[:, 2 + i, :].rearrange("p (k s) -> p k s", k=4)).then_inc(gath_hi, 1)

            def silu(u):
                act.wait_ge(used, u.count())
                act.activation(act_g[:], banks[:, 4, :], ACT.Silu).then_inc(silu_done, 1)

            def hid_t_hi(s):
                act.wait_ge(ht_mm, s + 1)
                act.copy(h_hi[:, 0, :], banks[:, 6, :]).then_inc(h_hi_done, 1)

            def comb_copy(v):
                act.wait_ge(comb_mm, v + 1)
                act.copy(comb[:], banks[:, 7, 0:SEQ]).then_inc(comb_out, 1)

            def y_copy(u):
                act.wait_ge(used, u.count())
                for c in range(2):
                    act.copy(y_sb[:, c * HALF:(c + 1) * HALF], banks[:, c, :]).then_inc(y_out, 1)

            def middle(e, j, base, sweep):
                s = (e + sweep * E) * MOE_STEPS + j + 1
                for c in (6, 7, 8, 9):
                    hi(unit_of(base, e, c, j))
                silu(unit_of(base, e, 7, j))
                hi(unit_of(base, e, 10, j))
                hi(unit_of(base, e, 11, j))
                hid_t_hi(s)

            def edge(e, nxt, base, sweep):
                if e is None:
                    gather_hi(sweep * E)
                    for c in range(0 if sweep else 3, 4):
                        hi(unit_of(base, 0, c))
                    silu(unit_of(base, 0, 3))
                    hi(unit_of(base, 0, 4))
                    hi(unit_of(base, 0, 5))
                    hid_t_hi(sweep * E * MOE_STEPS)
                    return
                v = e + sweep * E
                s = v * MOE_STEPS + (MOE_STEPS - 1)
                for c in (36, 37, 38, 39):
                    hi(unit_of(base, e, c))
                silu(unit_of(base, e, 37))
                hi(unit_of(base, e, 40))
                comb_copy(v)
                if nxt is not None:
                    gather_hi(v + 1)
                hi(unit_of(base, e, 41))
                hid_t_hi(s)
                if nxt is not None:
                    for c in (42, 43, 44, 45):
                        hi(unit_of(base, e, c))
                    silu(unit_of(base, e, 43))
                    hi(unit_of(base, e, 46))
                    hi(unit_of(base, e, 47))
                y_copy(unit_of(base, e, 41 if nxt is None else 45))
                if nxt is not None:
                    hid_t_hi(s + 1)

            moe_sweep(act, edge, middle, 0)
            act.wait_ge(over_set, 1)
            n_over = act.value_load(over[0:1, 0:1], min_val=0, max_val=SEQ)
            with act.If(n_over > P):
                moe_sweep(act, edge, middle, 1)
            with act.Else():
                act.nop()
            norm_stats(4)

        @block.vector
        def _(dve):
            dve.memset(zero_b[:], 0.0).then_inc(tab_b, 1)
            dve.engine_nop().then_inc(y_add, 1)

            def lo(u, n=UNIT):
                dve.wait_ge(hi_done, u.count())
                dve.tensor_tensor(w_lo[:, u.part, 0:n], raw[:, u.raw, 0:n],
                                  w_hi[:, u.part, 0:n].bitcast(F32), ALU.subtract).then_inc(lo_done, 1)

            def norm_apply(n, gain):
                dve.wait_ge(ss_done, n + 1)
                dve.tensor_scalar(mean_sq, sums_sq, 1.0 / D, EPS, ALU.mult, ALU.add).then_inc(ms_done, 1)
                dve.wait_ge(std_done, n + 1)
                dve.reciprocal(rstd, std).then_inc(rstd_done, 1)
                dve.wait_ge(rstd_done, n + 1)
                dve.wait_ge(gain_in[n], 16)
                for t in range(T):
                    dve.scalar_tensor_tensor(out=xn[:, t, :], in0=xres[:, t, :], scalar=rstd[:, t:t + 1],
                                             in1=gains[:, gain, :], op0=ALU.mult, op1=ALU.mult).then_inc(xn_ready, 1)

            def split_t_lo(q, job):
                for i in range(4):
                    dve.wait_ge(t_hi_done, 4 * q + i + 1)
                    dve.tensor_tensor(t_lo[:, 2 * i:2 * i + 2, :],
                                      banks[:, i, :].rearrange("p (k s) -> p k s", k=2),
                                      t_hi[:, 2 * i:2 * i + 2, :].bitcast(F32), ALU.subtract).then_inc(t_lo_done, 1)

            norm_apply(0, 0)
            lo(Unit(0))
            split_t_lo(0, 0)

            def in_lo(i):
                lo(Unit(i), 8 * IN_COLS[i][1])

            for i in range(1, 4):
                in_lo(i)
            dve.wait_ge(lat_a, 1)
            dve.tensor_scalar(lat_ms[:, 0:2], lat_ss[:, 0:2], 1.0 / QL, EPS, ALU.mult, ALU.add)
            dve.tensor_scalar(lat_ms[:, 2:4], lat_ss[:, 2:4], 1.0 / KVL, EPS, ALU.mult, ALU.add).then_inc(lat_v, 1)
            dve.wait_ge(lat_a, 2)
            dve.reciprocal(lat_rstd, lat_std).then_inc(lat_v, 1)
            dve.wait_ge(lat_v, 2)
            dve.wait_ge(lat_in, 64)
            for t in range(T):
                dve.scalar_tensor_tensor(out=qn[:, t, :], in0=ql[:, t, :], scalar=lat_rstd[:, t:t + 1],
                                         in1=lat_gain[:, 0:QL], op0=ALU.mult, op1=ALU.mult)
                last = dve.scalar_tensor_tensor(out=kvn[:, t, :], in0=kl[:, t, 0:KVL],
                                                scalar=lat_rstd[:, 2 + t:3 + t],
                                                in1=lat_gain[:, QL:QL + KVL], op0=ALU.mult, op1=ALU.mult)
            last.then_inc(lat_v, 1)
            in_lo(4)

            cos = tab[:, C_COS:C_COS + 32].rearrange("p (t c) -> p t c", t=T)
            sin = tab[:, C_SIN:C_SIN + 32].rearrange("p (t c) -> p t c", t=T)
            dve.wait_ge(tables_in, 16)

            def rope(x1, x2, c, s, tmp, y1, y2, step):
                dve.tensor_tensor(tmp(0), x1, c, ALU.mult)
                dve.tensor_tensor(tmp(1), x2, s, ALU.mult)
                dve.tensor_tensor(tmp(2), x1, s, ALU.mult)
                dve.tensor_tensor(tmp(3), x2, c, ALU.mult).then_inc(lat_v, 1)
                dve.wait_ge(lat_v, step + 1)
                dve.tensor_tensor(y1, tmp(0), tmp(1), ALU.subtract)
                dve.tensor_tensor(y2, tmp(2), tmp(3), ALU.add).then_inc(lat_v, 1)

            rope(kl[:, :, KVL:KVL + 16], kl[:, :, KVL + 16:KVL + 32], cos, sin,
                 lambda i: k_tmp[:, i], k_pe[:, :, 0:16], k_pe[:, :, 16:32], 3)
            in_lo(5)
            dve.wait_ge(lat_v, 5)
            for t in range(T):
                dve.tensor_copy(k_tok[:, t, :, HD:BK], k_pe[:, t, :].unsqueeze(1).broadcast_to([P, BH, ROPE]))
            in_lo(6)
            dve.wait_ge(lat_a, 4)
            cos_h = cos.unsqueeze(2).broadcast_to([P, T, BH, 16])
            sin_h = sin.unsqueeze(2).broadcast_to([P, T, BH, 16])
            rope(q_tok[:, :, :, HD:HD + 16], q_tok[:, :, :, HD + 16:BK], cos_h, sin_h,
                 lambda i: q_tmp[:, i], q_tok[:, :, :, HD:HD + 16], q_tok[:, :, :, HD + 16:BK], 5)
            in_lo(7)
            dve.wait_ge(lat_p, 3)
            for b in range(2):
                src = banks[:, 2 + b, :].rearrange("p (h c) -> p h c", h=4)
                dve.tensor_copy(k_tok[:, 1, 4 * b:4 * b + 4, 0:HD], src[:, :, 0:HD])
                last = dve.tensor_copy(vb[:, 1, 4 * b:4 * b + 4, :], src[:, :, HD:2 * HD])
            last.then_inc(lat_v, 1)
            for i in range(3):
                lo(Unit(U_OUT0 + i))
            for h in range(1, BH, 2):
                dve.wait_ge(lat_p, 4 + h)
                dve.tensor_copy(qk_t[0:BK, h, :], banks[0:BK, h % 4, :]).then_inc(lat_v, 1)

            def row_max(n, kind, h):
                b = n % 4
                dve.wait_ge(s_mm, n + 1)
                if n >= 4:
                    dve.wait_ge(pt_mm, n - 3)
                scores = banks[:, S_BANK[b], :]
                if kind == "latent":
                    dve.tensor_reduce(neg_max[:, b, :], scores.rearrange("p (t s) -> p t s", t=T), AX_X, ALU.max,
                                      negate=True).then_inc(max_step, 1)
                    dve.wait_ge(max_step, h + 1)
                    dve.tensor_scalar(neg_max[:, b, :], neg_max[:, b, :], BK ** -0.5, None,
                                      ALU.mult).then_inc(max_ready, 1)
                    return
                if kind == "dilated":
                    dve.wait_ge(bias_ready, h + 1)
                    dve.scalar_tensor_tensor(out=prob[:, b, :], in0=scores, scalar=HD ** -0.5,
                                             in1=bias_a[:, h % 2, :], op0=ALU.mult, op1=ALU.add).then_inc(s_read, 1)
                else:
                    for t in range(T):
                        cut = slice(t * SEQ, (t + 1) * SEQ)
                        first = (2 - 2 * t) * RPB_C + GRID_W - 1
                        table = bass.AP(rpb.tensor, rpb[:, h, first:first + 1].offset,
                                        [[rpb.ap[0][0], P], [RPB_C, 4], [-1, GRID_W]])
                        last = dve.scalar_tensor_tensor(
                            out=prob[:, b, cut].rearrange("p (r c) -> p r c", r=4),
                            in0=scores[:, cut].rearrange("p (r c) -> p r c", r=4), scalar=HD ** -0.5,
                            in1=table, op0=ALU.mult, op1=ALU.add)
                    last.then_inc(s_read, 1)
                dve.wait_ge(s_read, n + 1 if n < 16 else n + 1 - BH)
                dve.tensor_reduce(neg_max[:, b, :], prob[:, b, :].rearrange("p (t s) -> p t s", t=T), AX_X, ALU.max,
                                  negate=True).then_inc(max_ready, 1)

            def head_group(g, col):
                dve.wait_ge(pv_mm, 8 * g + 8)
                c0 = 8 * (g % 2)
                dve.reciprocal(row_sum[:, :, c0:c0 + 8], row_sum[:, :, c0:c0 + 8]).then_inc(inv_done, 1)
                dve.wait_ge(inv_done, g + 1)
                for t in range(T):
                    dve.tensor_tensor(
                        xn[:, t, col:col + 512].rearrange("p (h c) -> p h c", h=8),
                        banks[:, 4 + t, :].rearrange("p (h c) -> p h c", h=8),
                        row_sum[:, t, c0:c0 + 8].unsqueeze(2).broadcast_to([P, 8, HD]),
                        ALU.mult).then_inc(xn_ready if g % 2 else heads_out, 1)

            for n in range(AH + BH):
                row_max(n, "dilated" if n < AH else "latent", n % 8)
                if n == 10:
                    head_group(0, 0)
            head_group(1, 512)
            split_t_lo(1, 1)

            def residual(bank, u):
                dve.wait_ge(used, u + 1)
                for t in range(T):
                    both = xres[:, t, :].rearrange("p (a b) -> p a b", a=2)
                    dve.tensor_tensor(both, both, banks[:, bank + 2 * t:bank + 2 * t + 2, :],
                                      ALU.add).then_inc(x_tile, 1)

            for i in range(3):
                lo(Unit(U_OUT0 + 3 + i))
            residual(4, U_OUT0 + 3)
            lo(Unit(U_FFN + 2))
            dve.wait_ge(x_tile, 2)
            norm_apply(1, 1)
            split_t_lo(2, 2)

            def ffn_dve(j, jj):
                dve.wait_ge(silu_done, j + 1)
                dve.tensor_tensor(hid[:], act_g[:], banks[:, 5 + 2 * jj, :], ALU.mult).then_inc(hid_done, 1)
                dve.wait_ge(h_hi_done, j + 1)
                dve.tensor_tensor(h_lo[:, jj, :], hid[:], h_hi[:, jj, :].bitcast(F32),
                                  ALU.subtract).then_inc(h_lo_done, 1)

            ffn_dve(0, 0)
            with dve.Fori(0, (FFN_STEPS - 1) // 2) as it:
                for jj in range(2):
                    for i in range(3):
                        lo(Unit(U_FFN + 3 + 3 * jj + i, it))
                    ffn_dve(it * 2 + (jj + 1), (jj + 1) % 2)
            lo(Unit(U_QKV))
            lo(Unit(U_QKV + 1))
            residual(0, U_FFN + 32)
            lo(Unit(U_QKV + 2))
            dve.wait_ge(x_tile, 4)
            norm_apply(2, 2)
            split_t_lo(3, 3)
            for i in range(12):
                lo(Unit(U_QKV + 3 + i))
            dve.wait_ge(rpb_in, 32)
            for n in range(16, 16 + CH):
                row_max(n, "neighbourhood", n - 16)
                if n == 26:
                    head_group(2, 0)
            head_group(3, 512)
            split_t_lo(4, 4)
            for i in range(3):
                lo(Unit(U_OUT1 + 3 + i))
            residual(4, U_OUT1 + 3)
            lo(Unit(U_OUT1 + 6))
            dve.wait_ge(x_tile, 6)
            norm_apply(3, 0)

            dve.wait_ge(route_mm, 1)
            dve.tensor_copy(logits[:], banks[:, 4, 0:16].rearrange("p (t e) -> p t e", t=T)).then_inc(route_v, 0) \
                if False else dve.tensor_copy(logits[:], banks[:, 4, 0:16].rearrange("p (t e) -> p t e", t=T)).then_inc(pickg_step, 1)
            dve.wait_ge(pickg_step, 1)
            for t in range(T):
                last = dve.max(out=top_v[:, t, :], in_=logits[:, t, :])
            last.then_inc(pickg_step, 1)
            dve.wait_ge(pickg_step, 2)
            dve.tensor_tensor(top_w[:, :, 0], top_v[:, :, 1], top_v[:, :, 0], ALU.subtract).then_inc(route_v, 1)
            for t in range(T):
                last = dve.max_index(out=top_i[:, t, :], in_max=top_v[:, t, :], in_values=logits[:, t, :])
            last.then_inc(pickg_step, 1)
            dve.wait_ge(pickg_step, 3)
            dve.tensor_copy(top_f[:], top_i[:]).then_inc(pickg_step, 1)
            dve.wait_ge(pickg_step, 4)
            experts = tab[:, C_IOTA:C_IOTA + E]
            for t in range(T):
                dve.tensor_scalar(one_a[:, t, :], experts, top_f[:, t, 0:1], None, ALU.is_equal)
                last = dve.tensor_scalar(one_b[:, t, :], experts, top_f[:, t, 1:2], None, ALU.is_equal)
            last.then_inc(pickg_step, 1)
            dve.wait_ge(pickg_step, 5)
            dve.tensor_tensor(mask[:], one_a[:], one_b[:], ALU.add).then_inc(route_v, 1)
            dve.wait_ge(route_a, 1)
            dve.tensor_scalar(top_w[:, :, 2], top_w[:, :, 1], 1.0, None, ALU.add).then_inc(pickg_step, 1)
            dve.wait_ge(pickg_step, 6)
            dve.reciprocal(top_w[:, :, 2], top_w[:, :, 2]).then_inc(pickg_step, 1)
            dve.wait_ge(pickg_step, 7)
            dve.tensor_tensor(top_w[:, :, 3], top_w[:, :, 1], top_w[:, :, 2], ALU.mult).then_inc(pickg_step, 1)
            dve.wait_ge(pickg_step, 8)
            for t in range(T):
                last = dve.tensor_scalar(gate[:, t, :], one_a[:, t, :], top_w[:, t, 2:3], None, ALU.mult)
            last.then_inc(pickg_step, 1)
            dve.wait_ge(pickg_step, 9)
            for t in range(T):
                last = dve.scalar_tensor_tensor(out=gate[:, t, :], in0=one_b[:, t, :], scalar=top_w[:, t, 3:4],
                                                in1=gate[:, t, :], op0=ALU.mult, op1=ALU.add)
            last.then_inc(pickg_step, 1)
            dve.wait_ge(route_mm, 2)
            dve.scalar_tensor_tensor(out=place[:], in0=banks[:, 5, 0:16].rearrange("p (t e) -> p t e", t=T),
                                     scalar=1.0, in1=mask[:], op0=ALU.add, op1=ALU.mult).then_inc(pickg_step, 1)
            dve.tensor_reduce(most, banks[:, 5, 16:24], AX_X, ALU.max).then_inc(pickg_step, 1)
            dve.wait_ge(pickg_step, 12)
            dve.tensor_scalar(place[:], place[:], -1.0, None, ALU.add).then_inc(route_v, 1)
            dve.tensor_copy(over[:], most).then_inc(over_set, 1)

            def gather_lo(v):
                for i in range(2):
                    dve.wait_ge(gath_hi, v * 2 + (i + 1))
                    dve.tensor_tensor(t_lo[:, 4 * i:4 * i + 4, 0:P],
                                      banks[:, 2 + i, :].rearrange("p (k s) -> p k s", k=4),
                                      t_hi[:, 4 * i:4 * i + 4, 0:P].bitcast(F32), ALU.subtract).then_inc(gath_lo, 1)

            def gated(s):
                dve.wait_ge(silu_done, s + (FFN_STEPS + 1))
                dve.tensor_tensor(hid[:], act_g[:], banks[:, 5, :], ALU.mult).then_inc(hid_done, 1)

            def hid_t_lo(s):
                dve.wait_ge(h_hi_done, s + (FFN_STEPS + 1))
                dve.tensor_tensor(h_lo[:, 0, :], banks[:, 6, :], h_hi[:, 0, :].bitcast(F32),
                                  ALU.subtract).then_inc(h_lo_done, 1)

            def add_y(v):
                for i, (t, c) in enumerate(((0, 0), (1, 0), (0, 1), (1, 1))):
                    dve.wait_ge(scat_mm, v * 4 + (i + 1))
                    cols = xres[:, t, c * HALF:(c + 1) * HALF]
                    if i == 0:
                        dve.wait_ge(y_add, v * 4 + 1)
                    dve.tensor_tensor(cols, cols, banks[:, (7, 2, 3, 7)[i], :], ALU.add).then_inc(y_add, 1)

            def middle(e, j, base, sweep):
                s = (e + sweep * E) * MOE_STEPS + j + 1
                for c in (6, 7, 8, 9):
                    lo(unit_of(base, e, c, j))
                gated(s)
                lo(unit_of(base, e, 10, j))
                lo(unit_of(base, e, 11, j))
                hid_t_lo(s)

            def edge(e, nxt, base, sweep):
                if e is None:
                    gather_lo(sweep * E)
                    for c in range(0 if sweep else 3, 4):
                        lo(unit_of(base, 0, c))
                    gated(sweep * E * MOE_STEPS)
                    lo(unit_of(base, 0, 4))
                    lo(unit_of(base, 0, 5))
                    hid_t_lo(sweep * E * MOE_STEPS)
                    return
                v = e + sweep * E
                s = v * MOE_STEPS + (MOE_STEPS - 1)
                for c in (36, 37, 38, 39):
                    lo(unit_of(base, e, c))
                gated(s)
                lo(unit_of(base, e, 40))
                if nxt is not None:
                    gather_lo(v + 1)
                lo(unit_of(base, e, 41))
                hid_t_lo(s)
                if nxt is not None:
                    for c in (42, 43, 44, 45):
                        lo(unit_of(base, e, c))
                    gated(s + 1)
                    lo(unit_of(base, e, 46))
                    lo(unit_of(base, e, 47))
                    hid_t_lo(s + 1)
                add_y(v)

            moe_sweep(dve, edge, middle, 0)
            dve.wait_ge(over_set, 1)
            n_over = dve.value_load(over[0:1, 0:1], min_val=0, max_val=SEQ)
            with dve.If(n_over > P):
                moe_sweep(dve, edge, middle, 1)
                dve.wait_ge(y_add, 2 * 4 * E + 1)
            with dve.Else():
                dve.wait_ge(y_add, 4 * E + 1)
            dve.engine_nop().then_inc(x_tile, 2)
            norm_apply(4, 1)

        @block.tensor
        def _(pe):
            def three(out, a_hi, a_lo, b_hi, b_lo, start, stop):
                pe.matmul(out, a_hi, b_hi, start=start, stop=False)
                pe.matmul(out, a_lo, b_hi, start=False, stop=False)
                return pe.matmul(out, a_hi, b_lo, start=False, stop=stop)

            def unit_parts(u, k, n):
                cut = lambda w: w[:, u.part, 0:k * n].rearrange("p (k n) -> p k n", k=k)
                return cut(w_hi), cut(w_lo)

            def transpose_xn(q):
                for t in range(T):
                    pe.wait_ge(xn_ready, 2 * q + t + 1)
                    for i in range(4):
                        for k in range(2):
                            c = (2 * i + k) * P
                            last = pe.transpose(banks[:, i, (2 * k + t) * P:(2 * k + t + 1) * P],
                                                xn[:, t, c:c + P], ident)
                        if t == T - 1:
                            last.then_inc(t_mm, 1)

            def columns(u, bank, n, transposed, split=None):
                pe.wait_ge(lo_done, u.count())
                hi_w, lo_w = unit_parts(u, KD, n)
                for m in range(2):
                    cut = slice(m * P, (m + 1) * P)
                    dst = banks[:, bank, m * 256:m * 256 + (256 if transposed else n)]
                    for k in range(KD):
                        if split is not None and m == 0 and k % 2 == 0:
                            pe.wait_ge(t_lo_done, 4 * split + k // 2 + 1)
                        if transposed:
                            last = three(dst, hi_w[:, k, cut], lo_w[:, k, cut], t_hi[:, k, :], t_lo[:, k, :],
                                         k == 0, k == KD - 1)
                        else:
                            last = three(dst, t_hi[:, k, cut], t_lo[:, k, cut], hi_w[:, k, :], lo_w[:, k, :],
                                         k == 0, k == KD - 1)
                return last

            def rows(u, bank, lhs_hi, lhs_lo, n_t, start, stop):
                pe.wait_ge(lo_done, u.count())
                hi_w, lo_w = unit_parts(u, 2, D)
                for i in range(2):
                    for t in range(n_t):
                        for c in range(2):
                            cols = slice(c * HALF, (c + 1) * HALF)
                            last = three(banks[:, bank + 2 * t + c, :], lhs_hi(i, t), lhs_lo(i, t),
                                         hi_w[:, i, cols], lo_w[:, i, cols], start and i == 0, stop and i == 1)
                return last

            pe.wait_ge(tables_in, 16)
            transpose_xn(0)

            def in_proj(i):
                if i >= 4:
                    pe.wait_ge(proj_out, i - 3)
                columns(Unit(i), 4 + i % 4, IN_COLS[i][1], 2 <= i < 6, 0 if i == 0 else None).then_inc(used, 1)

            for i in range(4):
                in_proj(i)
            pe.wait_ge(lat_v, 3)
            for k in range(2):
                for t in range(T):
                    pe.transpose(banks[:, 0, (2 * k + t) * P:(2 * k + t + 1) * P], qn[:, t, k * P:(k + 1) * P], ident)
            for t in range(T):
                last = pe.transpose(banks[:, 1, t * P:(t + 1) * P], kvn[:, t, :], ident)
            last.then_inc(lat_p, 1)
            in_proj(4)
            pe.wait_ge(lat_a, 3)
            pe.wait_ge(lat_in, 64)
            for t, b in enumerate((2, 0)):
                for c0, n, bank in ((0, 512, b), (512, 256, b + 1)):
                    for k in range(2):
                        last = pe.matmul(banks[:, bank, 0:n], qn_t[:, k, t * P:(t + 1) * P], uq[:, k, c0:c0 + n],
                                         start=(k == 0), stop=(k == 1))
            last.then_inc(lat_p, 1)
            in_proj(5)
            in_proj(6)
            pe.wait_ge(lat_a, 4)
            for t in range(T):
                for c in range(2):
                    last = pe.matmul(banks[:, 2 * t + c, :], kvn_t[:, t * P:(t + 1) * P],
                                     ukv[:, c * HALF:(c + 1) * HALF], start=True, stop=True)
            last.then_inc(lat_p, 1)
            in_proj(7)
            pe.wait_ge(lat_a, 5)
            pe.wait_ge(lat_v, 8)
            for h in range(BH):
                if h >= 4:
                    pe.wait_ge(lat_a if h % 2 == 0 else lat_v, (6 if h % 2 == 0 else 9) + (h - 4) // 2)
                for i, src in enumerate((q_tok, q_tok, k_tok, k_tok)):
                    last = pe.transpose(banks[0:BK, h % 4, i * P:(i + 1) * P], src[:, i % 2, h, :], ident)
                last.then_inc(lat_p, 1)

            def scores(n, kind, h):
                b = S_BANK[n % 4]
                if n >= 4:
                    if n - 4 < AH:
                        pe.wait_ge(s_read, n - 3)
                    elif n - 4 < AH + BH:
                        pe.wait_ge(exp_done, n - 3)
                    else:
                        pe.wait_ge(s_read, n - 3 - BH)
                if kind == "latent":
                    for t in range(T):
                        last = pe.matmul(banks[:, b, t * SEQ:(t + 1) * SEQ], qk_t[0:BK, h, t * P:(t + 1) * P],
                                         qk_t[0:BK, h, 2 * P:4 * P], start=True, stop=True)
                    last.then_inc(s_mm, 1)
                    return
                q, k = (qa_t, ka_t) if kind == "dilated" else (qc_t, kc_t)
                rows_h = slice(HD * (h % 2), HD * (h % 2) + HD)
                for t in range(T):
                    dst = banks[:, b, t * SEQ:(t + 1) * SEQ]
                    if kind == "neighbourhood":
                        pe.matmul(dst, ident_b[:], mask_b[:], start=True, stop=False)
                    last = pe.matmul(dst, q[rows_h, h // 2, t * P:(t + 1) * P], k[rows_h, h // 2, :],
                                     start=kind == "dilated", stop=True)
                last.then_inc(s_mm, 1)

            def turn_probs(n):
                pe.wait_ge(exp_done, n + 1)
                if n >= 2:
                    pe.wait_ge(pt_out, n - 1)
                b = n % 4
                for k in range(2):
                    for t in range(T):
                        last = pe.transpose(banks[:, T_BANK[n % 2], (2 * k + t) * P:(2 * k + t + 1) * P],
                                            prob[:, b, t * SEQ + k * P:t * SEQ + (k + 1) * P], ident)
                last.then_inc(pt_mm, 1)

            def values(n, v):
                pe.wait_ge(pt_out, n + 1)
                if n % 16 == 8:
                    pe.wait_ge(heads_out, n // 8 + 1)
                c = HD * (n % 8)
                for t in range(T):
                    for k in range(2):
                        last = pe.matmul(banks[:, 4 + t, c:c + HD],
                                         prob_t[:, n % 2, (2 * k + t) * P:(2 * k + t + 1) * P], v(k),
                                         start=(k == 0), stop=(k == 1))
                last.then_inc(pv_mm, 1)

            pe.wait_ge(proj_out, 8)
            pe.wait_ge(lat_a, 9)
            pe.wait_ge(lat_v, 12)
            for n in range(AH + BH + 3):
                if n < AH + BH:
                    scores(n, "dilated" if n < AH else "latent", n % 8)
                if 2 <= n < AH + BH + 2:
                    turn_probs(n - 2)
                if n >= 3:
                    m = n - 3
                    values(m, (lambda k: va[:, k, m * HD:(m + 1) * HD]) if m < AH else (lambda k: vb[:, k, m - AH, :]))
            transpose_xn(1)

            def out_proj(first, q):
                for i in range(4):
                    pe.wait_ge(t_lo_done, 4 * q + i + 1)
                    last = rows(Unit(first + i), 4, lambda k, t: t_hi[:, 2 * i + k, t * P:(t + 1) * P],
                                lambda k, t: t_lo[:, 2 * i + k, t * P:(t + 1) * P], T, i == 0, i == 3)
                    last.then_inc(used, 1)

            out_proj(U_OUT0, 1)
            transpose_xn(2)

            def ffn_gate_up(u_g, u_u, j, jj, split=None):
                columns(u_g, 4 + 2 * jj, 256, True, split).then_inc(used, 1)
                columns(u_u, 5 + 2 * jj, 256, True).then_inc(used, 1)

            def ffn_down(u, j, jj, stop=False):
                pe.wait_ge(h_hi_done, j + 1)
                pe.wait_ge(h_lo_done, j + 1)
                rows(u, 0, lambda k, t: h_hi[:, jj, k * SEQ + t * P:k * SEQ + (t + 1) * P],
                     lambda k, t: h_lo[:, jj, k * SEQ + t * P:k * SEQ + (t + 1) * P], T, False, stop).then_inc(used, 1)

            def clear(bank):
                return pe.matmul(banks[:, bank, :], zero_b[:, 0:P], zero_b[:], start=True, stop=False)

            ffn_gate_up(Unit(U_FFN), Unit(U_FFN + 1), 0, 0, 2)
            pe.wait_ge(tab_b, 3)
            for b in range(4):
                clear(b)
            with pe.Fori(0, (FFN_STEPS - 1) // 2) as it:
                for jj in range(2):
                    ffn_gate_up(Unit(U_FFN + 2 + 3 * jj, it), Unit(U_FFN + 3 + 3 * jj, it), it * 2 + (jj + 1),
                                (jj + 1) % 2)
                    ffn_down(Unit(U_FFN + 4 + 3 * jj, it), it * 2 + jj, jj)
            ffn_down(Unit(U_FFN + 32), FFN_STEPS - 1, 0, True)

            transpose_xn(3)
            for i in range(12):
                if i >= 4:
                    pe.wait_ge(proj_out, 8 + i - 3)
                columns(Unit(U_QKV + i), 4 + i % 4, 256, i < 8, 3 if i == 0 else None).then_inc(used, 1)
            pe.wait_ge(proj_out, 20)
            for n in range(16, 16 + CH + 3):
                if n < 16 + CH:
                    scores(n, "neighbourhood", n - 16)
                if 18 <= n < 16 + CH + 2:
                    turn_probs(n - 2)
                if n >= 19:
                    m = n - 19
                    values(n - 3, lambda k: vc[:, k, m * HD:(m + 1) * HD])
            transpose_xn(4)
            out_proj(U_OUT1, 4)

            transpose_xn(5)
            pe.wait_ge(t_hi_done, 24)
            pe.wait_ge(router_in, 16)
            for t in range(T):
                for k in range(KD):
                    last = pe.matmul(banks[:, 4, E * t:E * t + E], x_t[:, k, t * P:(t + 1) * P], router[:, k, :],
                                     start=(k == 0), stop=(k == KD - 1))
            last.then_inc(route_mm, 1)
            pe.wait_ge(route_v, 2)
            pe.matmul(banks[:, 5, 0:E], tri, mask[:, 0, :], start=True, stop=True)
            pe.matmul(banks[:, 5, E:2 * E], tri, mask[:, 1, :], start=True, stop=False)
            pe.matmul(banks[:, 5, E:2 * E], ones, mask[:, 0, :], start=False, stop=True)
            pe.matmul(banks[:, 5, 2 * E:3 * E], ones, mask[:, 0, :], start=True, stop=False)
            pe.matmul(banks[:, 5, 2 * E:3 * E], ones, mask[:, 1, :], start=False, stop=True).then_inc(route_mm, 1)

            def gather(v):
                pe.wait_ge(pick_ready, v + 1)
                for k in range(KD):
                    dst = banks[:, 2 + k // 4, (k % 4) * P:(k % 4 + 1) * P]
                    for t in range(T):
                        last = pe.matmul(dst, xn[:, t, k * P:(k + 1) * P], pick[:, t, :], start=(t == 0), stop=(t == 1))
                    if k % 4 == 3:
                        last.then_inc(gath_mm, 1)

            def gate_up(base, units):
                for i in range(4):
                    u = unit_of(base, *units[i])
                    pe.wait_ge(lo_done, u.count())
                    hi_w, lo_w = unit_parts(u, 4, HALF)
                    for k in range(4):
                        kk = 4 * (i % 2) + k
                        last = three(banks[:, 4 + i // 2, :], t_hi[:, kk, 0:P], t_lo[:, kk, 0:P],
                                     hi_w[:, k, :], lo_w[:, k, :], kk == 0, kk == KD - 1)
                    last.then_inc(used, 1)

            def moe_down(base, units, s, stop=False):
                pe.wait_ge(h_hi_done, s + (FFN_STEPS + 1))
                pe.wait_ge(h_lo_done, s + (FFN_STEPS + 1))
                for i in range(2):
                    u = unit_of(base, *units[i])
                    rows(u, 0, lambda k, t: h_hi[:, 0, (2 * i + k) * P:(2 * i + k + 1) * P],
                         lambda k, t: h_lo[:, 0, (2 * i + k) * P:(2 * i + k + 1) * P], 1, False, stop and i == 1).then_inc(used, 1)

            def turn_hid(s):
                pe.wait_ge(hid_done, s + (FFN_STEPS + 1))
                for k in range(4):
                    last = pe.transpose(banks[:, 6, k * P:(k + 1) * P], hid[:, k * P:(k + 1) * P], ident)
                last.then_inc(ht_mm, 1)

            def turn_pick(v):
                pe.wait_ge(pickg_ready, v + 1)
                pe.wait_ge(y_add, v * 4 + 1)
                for t in range(T):
                    last = pe.transpose(banks[:, 7, t * P:(t + 1) * P], pick_g[:, t, :], ident)
                last.then_inc(comb_mm, 1)

            def scatter(v):
                pe.wait_ge(comb_out, v + 1)
                for i, (t, c) in enumerate(((0, 0), (1, 0), (0, 1), (1, 1))):
                    if t == 0:
                        pe.wait_ge(y_out, v * 2 + (c + 1))
                    if i == 3:
                        pe.wait_ge(y_add, v * 4 + 2)
                    pe.matmul(banks[:, (7, 2, 3, 7)[i], :], comb[:, t * P:(t + 1) * P],
                              y_sb[:, c * HALF:(c + 1) * HALF], start=True, stop=True).then_inc(scat_mm, 1)

            def middle(e, j, base, sweep):
                s = (e + sweep * E) * MOE_STEPS + j + 1
                gate_up(base, [(e, 4 + i, j) for i in range(4)])
                moe_down(base, [(e, 8 + i, j) for i in range(2)], s - 1)
                turn_hid(s)

            def edge(e, nxt, base, sweep):
                if e is None:
                    if sweep:
                        pe.wait_ge(y_add, sweep * 4 * E + 1)
                    gather(sweep * E)
                    pe.wait_ge(gath_lo, sweep * E * 2 + 2)
                    clear(0)
                    clear(1)
                    gate_up(base, [(0, i, 0) for i in range(4)])
                    turn_hid(sweep * E * MOE_STEPS)
                    return
                v = e + sweep * E
                s = v * MOE_STEPS + (MOE_STEPS - 1)
                gate_up(base, [(e, 34 + i, 0) for i in range(4)])
                turn_pick(v)
                if nxt is not None:
                    gather(v + 1)
                moe_down(base, [(e, 38 + i, 0) for i in range(2)], s - 1)
                turn_hid(s)
                if nxt is not None:
                    pe.wait_ge(gath_lo, v * 2 + 4)
                    gate_up(base, [(e, 40 + i, 0) for i in range(4)])
                c = 40 if nxt is None else 44
                moe_down(base, [(e, c + i, 0) for i in range(2)], s, True)
                if nxt is not None:
                    turn_hid(s + 1)
                scatter(v)
                if nxt is not None:
                    clear(0)
                    clear(1)

            moe_sweep(pe, edge, middle, 0)
            pe.wait_ge(over_set, 1)
            n_over = pe.value_load(over[0:1, 0:1], min_val=0, max_val=SEQ)
            with pe.If(n_over > P):
                moe_sweep(pe, edge, middle, 1)
            with pe.Else():
                pe.nop()

        @block.gpsimd
        def _(pool):
            pool.wait_ge(tables_in, 16)
            pool.wait_ge(lat_p, 3)
            for h in range(AH):
                if h >= 2:
                    pool.wait_ge(s_read, h - 1)
                b = bias_a[:, h % 2, :]
                pool.tensor_scalar(b, tab[:, C_DIST:C_DIST + 512], 2.0 ** -(h + 1), None, ALU.mult).then_inc(bias_step, 1)
                pool.wait_ge(bias_step, h + 1)
                pool.tensor_tensor(b, b, tab[:, C_LNC:C_LNC + 512], ALU.add).then_inc(bias_ready, 1)

            def picks(e, sweep):
                v = e + sweep * E
                first = v == 0
                places = tab[:, C_IOTA + P * sweep:C_IOTA + P * (sweep + 1)]
                if first:
                    pool.wait_ge(route_v, 3)
                else:
                    pool.wait_ge(gath_mm, v * 2)
                    pool.wait_ge(pickg_ready, v)
                pool.tensor_copy(place_e.unsqueeze(2), place[:, :, e:e + 1])
                pool.tensor_copy(gate_e.unsqueeze(2), gate[:, :, e:e + 1]).then_inc(pick_step, 1)
                pool.wait_ge(pick_step, v + 1)
                for t in range(T):
                    last = pool.tensor_scalar(pick[:, t, :], places, place_e[:, t:t + 1], None, ALU.is_equal)
                last.then_inc(pick_ready, 1)
                if not first:
                    pool.wait_ge(comb_mm, v)
                for t in range(T):
                    last = pool.tensor_scalar(pick_g[:, t, :], places, place_e[:, t:t + 1], gate_e[:, t:t + 1],
                                              ALU.is_equal, ALU.mult)
                last.then_inc(pickg_ready, 1)

            for e in range(E):
                picks(e, 0)
            pool.wait_ge(over_set, 1)
            n_over = pool.value_load(over[0:1, 0:1], min_val=0, max_val=SEQ)
            with pool.If(n_over > P):
                for e in range(E):
                    picks(e, 1)
            with pool.Else():
                pool.nop()


_INS = ["x", "ln_mix_e", "w_in_e", "mla_q_norm", "mla_w_uq", "mla_kv_norm", "mla_w_ukv", "w_out_e",
        "ln_ffn_e", "ffn_w_gate", "ffn_w_up", "ffn_w_down", "ln_mix_o", "na_w_qkv", "na_rpb", "na_w_out",
        "ln_ffn_o", "moe_router", "moe_w_gate", "moe_w_up", "moe_w_down", "ln_final"]


def kernel(**inputs):
    import concourse.bacc as bacc
    from concourse.bass_utils import run_bass_kernel_spmd

    nc = bacc.Bacc("TRN2", target_bir_lowering=False, num_devices=1, dynamic_dma_scratch_size=1024)
    arrays = {f"in_{n}": np.ascontiguousarray(inputs[n]) for n in _INS}
    arrays["in_na_rpb"] = np.ascontiguousarray(inputs["na_rpb"][..., ::-1])
    arrays["in_tables"] = constants()
    args = [nc.dram_tensor(n, a.shape, mybir.dt.from_np(a.dtype), kind="ExternalInput").ap()
            for n, a in arrays.items()]
    y = nc.dram_tensor("out_y", (1, SEQ, D), F32, kind="ExternalOutput").ap()
    trunk(nc, *args, y)
    got = run_bass_kernel_spmd(nc, [arrays], core_ids=[0])
    return got.results[0]["out_y"]
```

```python
from contextlib import ExitStack

import numpy as np

import concourse.bass as bass
from concourse import mybir

ALU = mybir.AluOpType
ACT = mybir.ActivationFunctionType
F32 = mybir.dt.float32
F32R = mybir.dt.float32r
BF16 = mybir.dt.bfloat16
I32 = mybir.dt.int32
U32 = mybir.dt.uint32
AX_X = mybir.AxisListType.X

P = 128
D = 1024
SEQ = 256
T = SEQ // P
KD = D // P
HALF = 512
EPS = 1e-6
NEG = -1e30
HD = 64
AH, BH, CH = 8, 8, 16
A_W = AH * HD
QL, KVL, ROPE = 256, 128, 32
BK = HD + ROPE
D_FF = 2816
E, EFF = 8, 3584
GRID_W, NA_COLS = 64, 16
RPB_R, RPB_C = 15, 31
RPB_RUN = 5 * RPB_C + GRID_W

UNIT = 2048
RING = 6
PARTS = 3
FFN_STEPS = D_FF // 256
MOE_STEPS = EFF // HALF
MOE_UNITS = 6 * MOE_STEPS
GAP = 20

U_IN = 0
U_OUT0 = U_IN + 8
U_FFN = U_OUT0 + 4
U_QKV = U_FFN + 3 * FFN_STEPS
U_OUT1 = U_QKV + 12
U_MOE = U_OUT1 + 4
QKV_ORDER = (0, 1, 2, 3, 8, 9, 10, 11, 4, 5, 6, 7)
IN_COLS = [(3 * A_W, QL), (3 * A_W + QL, KVL + ROPE)] + [(256 * i, 256) for i in range(6)]

S_BANK, T_BANK = (0, 1, 2, 7), (3, 6)

C_DIST, C_LNC = 0, 512
C_COS, C_SIN = 1024, 1056
C_MASK = 1088
C_ID, C_TRI, C_IOTA, C_ONES = 1152, 1280, 1408, 1664
C_ALL = 1792


def constants():
    c = np.zeros((P, C_ALL), np.float32)
    pos = np.arange(SEQ)
    d = np.abs(pos[:, None] - pos[None])
    cover = (d <= 64).astype(np.float64) + (d % 4 == 0) + (d % 16 == 0)
    lnc = np.where(cover > 0, np.log(np.maximum(cover, 1)), NEG).astype(np.float32)
    tiles = lambda a: a.reshape(T, P, -1).transpose(1, 0, 2).reshape(P, -1)
    c[:, C_DIST:C_DIST + 512] = tiles(-d.astype(np.float32))
    c[:, C_LNC:C_LNC + 512] = tiles(lnc)
    half = ROPE // 2
    freqs = np.float32(10000.0) ** (-np.arange(half, dtype=np.float32) / np.float32(half))
    ang = pos[:, None].astype(np.float32) * freqs[None].astype(np.float32)
    c[:, C_COS:C_COS + 32] = tiles(np.cos(ang.astype(np.float64)).astype(np.float32))
    c[:, C_SIN:C_SIN + 32] = tiles(np.sin(ang.astype(np.float64)).astype(np.float32))
    col = np.arange(P) % GRID_W
    first = np.clip(col - NA_COLS // 2, 0, GRID_W - NA_COLS)
    key = np.arange(GRID_W)
    inside = (key[None] >= first[:, None]) & (key[None] < first[:, None] + NA_COLS)
    c[:, C_MASK:C_MASK + GRID_W] = np.where(inside, 0.0, NEG)
    c[:, C_ID:C_ID + P] = np.eye(P)
    c[:, C_TRI:C_TRI + P] = np.triu(np.ones((P, P)), 1)
    c[:, C_IOTA:C_IOTA + 256] = np.arange(256)[None]
    c[:, C_ONES:C_ONES + P] = 1.0
    return c


class Unit:

    def __init__(self, s, k=0):
        self.s, self.k = s, k

    def count(self, ahead=0):
        return self.k * RING + (self.s + 1 + ahead)

    def early(self, back):
        return isinstance(self.k, int) and self.s < back

    @property
    def raw(self):
        return self.s % RING

    @property
    def part(self):
        return self.s % PARTS

    def filled(self):
        return self.k * 16 + 16 * (self.s // RING + 1)


def trunk(nc, x, ln_mix_e, w_in_e, mla_q_norm, mla_w_uq, mla_kv_norm, mla_w_ukv, w_out_e,
          ln_ffn_e, ffn_w_gate, ffn_w_up, ffn_w_down, ln_mix_o, na_w_qkv, na_rpb, na_w_out,
          ln_ffn_o, moe_router, moe_w_gate, moe_w_up, moe_w_down, ln_final, tables, out):
    with ExitStack() as ctx:
        def sb(name, shape, dt=F32):
            return ctx.enter_context(nc.sbuf_tensor(name, shape, dt))

        def sem(name):
            return ctx.enter_context(nc.semaphore(name))

        raw = sb("raw", [P, RING, UNIT])
        w_hi = sb("w_hi", [P, PARTS, UNIT], F32R)
        w_lo = sb("w_lo", [P, PARTS, UNIT], F32R)
        xres = sb("xres", [P, T, D])
        xn = sb("xn", [P, T, D])
        t_hi = sb("t_hi", [P, KD, SEQ], F32R)
        t_lo = sb("t_lo", [P, KD, SEQ], F32R)
        h_hi = sb("h_hi", [P, 2, HALF], F32R)
        h_lo = sb("h_lo", [P, 2, HALF], F32R)
        gains = sb("gains", [P, 2, D])
        lat_gain = sb("lat_gain", [P, QL + KVL])
        router = sb("router", [P, KD, E])
        tab = sb("tab", [P, C_ALL])
        mask_b = sb("mask_b", [P, GRID_W], BF16)
        ident_b = sb("ident_b", [P, P], BF16)
        zero_b = sb("zero_b", [P, P], BF16)
        small = sb("small", [P, 77])
        qk_hi = sb("qk_hi", [P, 4096], F32R)
        qk_lo = sb("qk_lo", [P, 4096], F32R)
        arena = sb("arena", [P, 8928])
        banks = ctx.enter_context(nc.psum_tensor("banks", [P, 8, HALF], F32))

        ident = tab[:, C_ID:C_ID + P]
        tri = tab[:, C_TRI:C_TRI + P]
        ones = tab[:, C_ONES:C_ONES + P]

        def part_of(offset, n):
            return arena[:, offset:offset + n]

        def heads_of(w, offset, n, k):
            return w[:, offset:offset + n].rearrange("p (m s) -> p m s", m=k)

        def padded(w, pairs):
            return w[:, 0:2 * SEQ * pairs].rearrange("p (m a s) -> p m a s", a=2, s=SEQ)

        qa_t = [padded(w, AH // 2) for w in (qk_hi, qk_lo)]
        ka_t = [heads_of(w, 2048, 1024, AH // 2) for w in (qk_hi, qk_lo)]
        qc_t = [padded(w, CH // 2) for w in (qk_hi, qk_lo)]
        kc_t = [t_hi, t_lo]
        lat_t = [[heads_of(w, 3072, 1024, 2)[:, h, :] for h in range(2)]
                 + [v.rearrange("p k s -> p (k s)")[:, 512 * h:512 * h + 512] for h in range(4)]
                 + [hid_w[:, h, :] for h in range(2)]
                 for w, v, hid_w in ((qk_hi, t_hi, h_hi), (qk_lo, t_lo, h_lo))]

        va = part_of(0, 1024).rearrange("p (t c) -> p t c", t=T)
        ql = part_of(1024, 512).rearrange("p (t c) -> p t c", t=T)
        qn = part_of(1536, 512).rearrange("p (t c) -> p t c", t=T)
        kl = part_of(2048, 320).rearrange("p (t c) -> p t c", t=T)
        kvn = part_of(2368, 256).rearrange("p (t c) -> p t c", t=T)
        k_tmp = part_of(2624, 128).rearrange("p (n t c) -> p n t c", n=4, t=T)
        k_pe = part_of(2752, 64).rearrange("p (t c) -> p t c", t=T)
        kvn_t = part_of(2816, 256)
        ukv = part_of(3072, 1024)
        uq = part_of(4096, 1536).rearrange("p (k c) -> p k c", k=2)
        k_tok = part_of(5632, 1536).rearrange("p (t h c) -> p t h c", t=T, h=BH)
        vb = part_of(7168, 1024).rearrange("p (t h c) -> p t h c", t=T, h=BH)
        qn_t = part_of(1024, 512).rearrange("p (k s) -> p k s", k=2)
        q_tmp = part_of(1024, 1024).rearrange("p (n t h c) -> p n t h c", n=4, t=T, h=BH)
        q_tok = part_of(4096, 1536).rearrange("p (t h c) -> p t h c", t=T, h=BH)
        bias_a = [part_of(o, 512) for o in (8192, 3072, 3584, 1024, 1536, 2048, 2560)]
        prob = part_of(4096, 2048).rearrange("p (b s) -> p b s", b=4)
        prob_t = part_of(6144, 1024).rearrange("p (b s) -> p b s", b=2)
        vc = part_of(0, 2048).rearrange("p (t c) -> p t c", t=T)
        rpb = [part_of(o, 8 * RPB_RUN).rearrange("p (h f) -> p h f", h=8) for o in (2048, 7168)]
        act_g = part_of(0, 512)
        hid = part_of(512, 512)
        x_t = part_of(1024, 2048).rearrange("p (k s) -> p k s", k=KD)
        xn_split = [w[:, 0:T * D].rearrange("p (t c) -> p t c", t=T) for w in (qk_hi, qk_lo)]
        y_hi, y_lo = (w[:, T * D:T * D + D] for w in (qk_hi, qk_lo))
        pick = qk_hi[:, 3072:3328].rearrange("p (t s) -> p t s", t=T)
        comb = qk_hi[:, 3328:3584]
        pick_c = part_of(4608, 256).rearrange("p (t s) -> p t s", t=T)
        r = part_of(4864, 256)
        logits = r[:, 0:16].rearrange("p (t e) -> p t e", t=T)
        top_v = r[:, 16:32].rearrange("p (t e) -> p t e", t=T)
        top_f = r[:, 32:48].rearrange("p (t e) -> p t e", t=T)
        one_a = r[:, 48:64].rearrange("p (t e) -> p t e", t=T)
        one_b = r[:, 64:80].rearrange("p (t e) -> p t e", t=T)
        gate = r[:, 80:96].rearrange("p (t e) -> p t e", t=T)
        mask = r[:, 96:112].rearrange("p (t e) -> p t e", t=T)
        place = r[:, 112:128].rearrange("p (t e) -> p t e", t=T)
        top_w = r[:, 128:136].rearrange("p (t c) -> p t c", t=T)
        place_e = r[:, 136:138]
        gate_e = r[:, 138:140]
        most = r[:, 140:141]
        top_i = sb("top_i", [P, T, 8], U32)
        over = sb("over", [P, 1], I32)

        sums_sq = small[:, 0:2]
        mean_sq = small[:, 2:4]
        std = small[:, 4:6]
        rstd = small[:, 6:8]
        one = small[:, 76:77]
        warm_out = [small[:, i:i + 1] for i in range(64, 76)]
        lat_ss = small[:, 8:12]
        lat_ms = small[:, 12:16]
        lat_std = small[:, 16:20]
        lat_rstd = small[:, 20:24]
        neg_max = small[:, 24:32].rearrange("p (b t) -> p b t", b=4)
        row_sum = small[:, 32:64].rearrange("p (t h) -> p t h", t=T)

        raw_full = [sem(f"raw_full{i}") for i in range(RING)]
        hi_done, lo_done, used = sem("hi_done"), sem("lo_done"), sem("used")
        tables_in, x_in = sem("tables_in"), [sem("x_in0"), sem("x_in1")]
        gain_in = [sem(f"gain_in{i}") for i in range(5)]
        lat_in, router_in, rpb_in = sem("lat_in"), sem("router_in"), sem("rpb_in")
        tab_b = sem("tab_b")
        ss_done, ms_done = sem("ss_done"), sem("ms_done")
        std_done, rstd_done, xn_ready = sem("std_done"), sem("rstd_done"), sem("xn_ready")
        t_mm, t_hi_done, t_lo_done = sem("t_mm"), sem("t_hi_done"), sem("t_lo_done")
        proj_out, qk_rest = sem("proj_out"), sem("qk_rest")
        lat_zero = sem("lat_zero")
        q_zero = sem("q_zero")
        lat_a, lat_v, lat_p = sem("lat_a"), sem("lat_v"), sem("lat_p")
        bias_step, bias_ready = sem("bias_step"), sem("bias_ready")
        s_mm, s_read = sem("s_mm"), sem("s_read")
        max_step, max_ready = sem("max_step"), sem("max_ready")
        exp_done, pt_mm, pt_out, pv_mm = sem("exp_done"), sem("pt_mm"), sem("pt_out"), sem("pv_mm")
        inv_done, heads_out = sem("inv_done"), sem("heads_out")
        x_tile = sem("x_tile")
        silu_done, hid_done = sem("silu_done"), sem("hid_done")
        h_hi_done, h_lo_done = sem("h_hi_done"), sem("h_lo_done")
        route_v, route_mm, route_a = sem("route_v"), sem("route_mm"), sem("route_a")
        over_set = sem("over_set")
        pick_step, pick_ready, gath_mm = sem("pick_step"), sem("pick_ready"), sem("gath_mm")
        gath_hi, gath_lo = sem("gath_hi"), sem("gath_lo")
        pickc_ready = sem("pickc_ready")
        comb_mm, comb_out = sem("comb_mm"), sem("comb_out")
        ht_mm = sem("ht_mm")
        y_out, y_rest = sem("y_out"), sem("y_rest")
        scat_mm, y_add, gate_ready = sem("scat_mm"), sem("y_add"), sem("gate_ready")
        xn_hi_done, xn_lo_done = sem("xn_hi_done"), sem("xn_lo_done")
        route_step = sem("route_step")
        out_sent = sem("out_sent")

        w_in = w_in_e[0].rearrange("(k p) n -> p k n", p=P)
        w_out = w_out_e[0].rearrange("(k p) n -> p k n", p=P)
        w_fg = ffn_w_gate[0].rearrange("(k p) n -> p k n", p=P)
        w_fu = ffn_w_up[0].rearrange("(k p) n -> p k n", p=P)
        w_fd = ffn_w_down[0].rearrange("(k p) n -> p k n", p=P)
        w_qkv = na_w_qkv[0].rearrange("(k p) n -> p k n", p=P)
        w_no = na_w_out[0].rearrange("(k p) n -> p k n", p=P)
        w_eg = moe_w_gate[0].rearrange("e (k p) n -> e p k n", p=P)
        w_eu = moe_w_up[0].rearrange("e (k p) n -> e p k n", p=P)
        w_ed = moe_w_down[0].rearrange("e (k p) n -> e p k n", p=P)

        def over_partitions(vector, n):
            return bass.AP(vector.tensor, 0, [[0, P], [1, n]])

        block = ctx.enter_context(nc.Block())

        def moe_sweep(eng, edge, middle, sweep):
            base = U_MOE + sweep * E * MOE_UNITS
            edge(None, 0, base, sweep)
            with eng.Fori(0, E - 1) as e:
                with eng.Fori(0, MOE_STEPS - 2) as j:
                    middle(e, j, base, sweep)
                edge(e, e + 1, base, sweep)
            with eng.Fori(0, MOE_STEPS - 2) as j:
                middle(E - 1, j, base, sweep)
            edge(E - 1, None, base, sweep)

        def unit_of(base, e, c, j=0):
            return Unit(base + c, e * MOE_STEPS + j) if not (isinstance(e, int) and isinstance(j, int)) \
                else Unit(base + c + 6 * (e * MOE_STEPS + j))

        @block.sync
        def _(sp):
            def load(u, src):
                if not u.early(RING):
                    sp.wait_ge(lo_done, u.count(-RING))
                _, k, n = src.shape
                dst = raw[:, u.raw, 0:k * n].rearrange("p (k n) -> p k n", k=k)
                sp.dma_start(dst, src).then_inc(raw_full[u.raw], 16)

            for t in range(T):
                sp.dma_start(xres[:, t, :], x[0, t * P:(t + 1) * P, :]).then_inc(x_in[t], 16)
            for i, (c0, n) in enumerate(IN_COLS):
                load(Unit(U_IN + i), w_in[:, :, c0:c0 + n])
            for i in range(4):
                load(Unit(U_OUT0 + i), w_out[:, 2 * i:2 * i + 2, :])

            load(Unit(U_FFN), w_fg[:, :, 0:256])
            load(Unit(U_FFN + 1), w_fu[:, :, 0:256])

            with sp.Fori(0, (FFN_STEPS - 1) // 2) as it:
                for jj in range(2):
                    cols = bass.ds(it * 512 + 256 * (jj + 1), 256)
                    load(Unit(U_FFN + 2 + 3 * jj, it), w_fg[:, :, cols])
                    load(Unit(U_FFN + 3 + 3 * jj, it), w_fu[:, :, cols])
                    load(Unit(U_FFN + 4 + 3 * jj, it), w_fd[:, bass.ds(it * 4 + 2 * jj, 2), :])
            load(Unit(U_FFN + 32), w_fd[:, 20:22, :])

            for i in range(12):
                c0 = 256 * QKV_ORDER[i]
                load(Unit(U_QKV + i), w_qkv[:, :, c0:c0 + 256])
            for i in range(4):
                load(Unit(U_OUT1 + i), w_no[:, 2 * i:2 * i + 2, :])

            def gate_up(e, j, base, c):
                cols = bass.ds(j * HALF, HALF)
                for i, w in enumerate((w_eg, w_eg, w_eu, w_eu)):
                    k0 = 4 * (i % 2)
                    load(unit_of(base, *c[i]), w[e, :, k0:k0 + 4, cols])

            def down(e, j, base, c):
                for i in range(2):
                    load(unit_of(base, *c[i]), w_ed[e, :, bass.ds(j * 4 + 2 * i, 2), :])

            def middle(e, j, base, sweep):
                gate_up(e, j + 1, base, [(e, 4 + i, j) for i in range(4)])
                down(e, j, base, [(e, 8 + i, j) for i in range(2)])

            def edge(e, nxt, base, sweep):
                if e is not None:
                    gate_up(e, MOE_STEPS - 1, base, [(e, 34 + i, 0) for i in range(4)])
                    down(e, MOE_STEPS - 2, base, [(e, 38 + i, 0) for i in range(2)])
                if nxt is not None:
                    first = (nxt, 0) if e is None else (e, 40)
                    gate_up(nxt, 0, base, [(first[0], first[1] + i, 0) for i in range(4)])
                if e is not None:
                    down(e, MOE_STEPS - 1, base, [(e, (40 if nxt is None else 44) + i, 0) for i in range(2)])

            moe_sweep(sp, edge, middle, 0)
            sp.wait_ge(over_set, 1)
            n_over = sp.value_load(over[0:1, 0:1], min_val=0, max_val=SEQ)
            with sp.If(n_over > P):
                moe_sweep(sp, edge, middle, 1)
            with sp.Else():
                sp.nop()
            for t in range(T):
                sp.wait_ge(xn_ready, 12 + t + 1)
                sp.dma_start(out[0, t * P:(t + 1) * P, :], xn[:, t, :]).then_inc(out_sent, 16)
            sp.wait_ge(out_sent, 16 * T)

        @block.scalar
        def _(act):
            act.dma_start(gains[:, 0, :], over_partitions(ln_mix_e, D)).then_inc(gain_in[0], 16)
            act.dma_start(tab[:], tables).then_inc(tables_in, 16)

            def hi(u, n=UNIT):
                act.wait_ge(raw_full[u.raw], u.filled())
                if not u.early(PARTS):
                    act.wait_ge(used, u.count(-PARTS))
                act.copy(w_hi[:, u.part, 0:n], raw[:, u.raw, 0:n]).then_inc(hi_done, 1)

            def warm(func):
                act.activation(warm_out.pop(), one, func)

            def norm_stats(n, after=None):
                warm(ACT.Sqrt)
                for t in range(T):
                    if n == 0:
                        act.wait_ge(x_in[t], 16)
                    else:
                        act.wait_ge(x_tile, 2 * n - 1 + t)
                    act.activation(xn[:, t, :], xres[:, t, :], ACT.Square,
                                   accum_out=sums_sq[:, t:t + 1]).then_inc(ss_done, 1)
                    act.wait_ge(ms_done, 2 * n + t + 1)
                    act.activation(std[:, t:t + 1], mean_sq[:, t:t + 1], ACT.Sqrt).then_inc(std_done, 1)
                if after is not None:
                    warm(after)

            def split_t_hi(q):
                for i in range(4):
                    act.wait_ge(t_mm, 4 * q + i + 1)
                    act.copy(t_hi[:, 2 * i:2 * i + 2, :],
                             banks[:, i, :].rearrange("p (k s) -> p k s", k=2)).then_inc(t_hi_done, 1)

            act.wait_ge(tab_b, 1)
            norm_stats(0)
            act.wait_ge(tables_in, 16)
            act.copy(ident_b[:], ident).then_inc(tab_b, 1)
            act.copy(mask_b[:], tab[:, C_MASK:C_MASK + GRID_W]).then_inc(tab_b, 1)
            hi(Unit(0))
            split_t_hi(0)
            act.dma_start(lat_gain[:, 0:QL], over_partitions(mla_q_norm, QL)).then_inc(lat_in, 16)
            act.dma_start(lat_gain[:, QL:QL + KVL], over_partitions(mla_kv_norm, KVL)).then_inc(lat_in, 16)
            act.dma_start(uq[:], mla_w_uq[0].rearrange("(k p) n -> p k n", p=P)).then_inc(lat_in, 16)
            act.dma_start(ukv[:], mla_w_ukv[0]).then_inc(lat_in, 16)
            act.dma_start(gains[:, 1, :], over_partitions(ln_ffn_e, D)).then_inc(gain_in[1], 16)
            act.dma_start(router[:], moe_router[0].rearrange("(k p) n -> p k n", p=P)).then_inc(router_in, 16)
            act.wait_ge(xn_ready, 2)
            act.dma_start(gains[:, 0, :], over_partitions(ln_mix_o, D)).then_inc(gain_in[2], 16)

            in_dst = [ql[:], kl[:], None, None] + [ka_t[0][:, 2 * i:2 * i + 2, :] for i in range(2)] \
                + [va[:, :, 0:256], va[:, :, 256:512]]

            def queries(dst, i, src):
                for half in range(2):
                    rows_h = slice(HD * half, HD * half + HD)
                    last = act.copy(dst[rows_h, 2 * i:2 * i + 2, half, :], src[rows_h])
                return last

            def in_out(i):
                act.wait_ge(used, U_IN + i + 1)
                src = banks[:, 4 + i % 4, :].rearrange("p (a b) -> p a b", a=2)[:, :, 0:IN_COLS[i][1]]
                last = queries(qa_t[0], i - 2, src) if i in (2, 3) else act.copy(in_dst[i], src)
                last.then_inc(proj_out, 1)

            def in_hi(i):
                hi(Unit(i), 8 * IN_COLS[i][1])

            in_hi(1)
            in_hi(2)
            in_out(0)
            in_hi(3)
            in_out(1)
            act.wait_ge(proj_out, 2)
            for t in range(T):
                act.activation(qn[:, t, :], ql[:, t, :], ACT.Square, accum_out=lat_ss[:, t:t + 1])
                last = act.activation(kvn[:, t, :], kl[:, t, 0:KVL], ACT.Square, accum_out=lat_ss[:, 2 + t:3 + t])
            last.then_inc(lat_a, 1)
            act.wait_ge(lat_v, 1)
            act.activation(lat_std, lat_ms, ACT.Sqrt).then_inc(lat_a, 1)
            warm(ACT.Exp)
            in_hi(4)
            in_out(2)
            in_hi(5)
            in_out(3)
            act.wait_ge(lat_p, 1)
            act.copy(qn_t[:], banks[:, 0, :].rearrange("p (k s) -> p k s", k=2))
            act.copy(kvn_t[:], banks[:, 1, 0:SEQ]).then_inc(lat_a, 1)
            in_hi(6)
            in_out(4)
            act.wait_ge(lat_p, 2)
            q_flat = q_tok.rearrange("p t h c -> p t (h c)")
            for t, b in enumerate((2, 0)):
                act.copy(q_flat[:, t, 0:512], banks[:, b, :])
                last = act.copy(q_flat[:, t, 512:768], banks[:, b + 1, 0:256])
            last.then_inc(lat_a, 1)
            in_hi(7)
            in_out(5)
            act.wait_ge(lat_p, 3)
            for b in range(2):
                src = banks[:, b, :].rearrange("p (h c) -> p h c", h=4)
                act.copy(k_tok[:, 0, 4 * b:4 * b + 4, 0:HD], src[:, :, 0:HD])
                last = act.copy(vb[:, 0, 4 * b:4 * b + 4, :], src[:, :, HD:2 * HD])
            last.then_inc(lat_a, 1)
            in_out(6)
            in_out(7)
            for h in range(BH):
                act.wait_ge(lat_p, 4 + h)
                act.copy(lat_t[0][h][0:BK, :], banks[0:BK, h % 4, :]).then_inc(lat_a, 1)

            def softmax(n, kind, h):
                b = n % 4
                act.wait_ge(max_ready, n + 1)
                for t in range(T):
                    src = (banks[:, S_BANK[b]] if kind == "latent" else prob[:, b])[:, t * SEQ:(t + 1) * SEQ]
                    last = act.activation(prob[:, b, t * SEQ:(t + 1) * SEQ], src, ACT.Exp,
                                          bias=neg_max[:, b, t:t + 1],
                                          scale=BK ** -0.5 if kind == "latent" else 1.0,
                                          accum_out=row_sum[:, t, n % 16:n % 16 + 1])
                last.then_inc(exp_done, 1)

            def prob_out(n):
                act.wait_ge(pt_mm, n + 1)
                if n >= 2:
                    act.wait_ge(pv_mm, n - 1)
                act.copy(prob_t[:, n % 2, :], banks[:, T_BANK[n % 2], :]).then_inc(pt_out, 1)

            for n in range(AH + BH):
                softmax(n, "dilated" if n < AH else "latent", n % 8)
                if n >= 2:
                    prob_out(n - 2)
                if n in (3, 7, 11):
                    hi(Unit(U_OUT0 + n // 4))
            prob_out(AH + BH - 2)
            prob_out(AH + BH - 1)
            split_t_hi(1)
            for i in range(3):
                hi(Unit(U_OUT0 + 3 + i))

            norm_stats(1, ACT.Silu)
            split_t_hi(2)
            hi(Unit(U_FFN + 2))
            act.wait_ge(xn_ready, 6)
            act.dma_start(gains[:, 1, :], over_partitions(ln_ffn_o, D)).then_inc(gain_in[3], 16)
            for half in range(2):
                for g in range(2):
                    src = bass.AP(na_rpb.tensor, (8 * g * RPB_R + 5 - half) * RPB_C + NA_COLS - GRID_W,
                                  [[1, GRID_W], [RPB_R * RPB_C, 8], [1, RPB_RUN]])
                    act.dma_start(rpb[g][GRID_W * half:GRID_W * (half + 1)], src).then_inc(rpb_in, 16)

            def ffn_act(u, j, jj):
                act.wait_ge(used, u.count())
                act.activation(act_g[:], banks[:, 4 + 2 * jj, :], ACT.Silu).then_inc(silu_done, 1)
                act.wait_ge(hid_done, j + 1)
                act.copy(h_hi[:, jj, :], hid[:]).then_inc(h_hi_done, 1)

            ffn_act(Unit(U_FFN + 1), 0, 0)
            with act.Fori(0, (FFN_STEPS - 1) // 2) as it:
                for jj in range(2):
                    for i in range(3):
                        hi(Unit(U_FFN + 3 + 3 * jj + i, it))
                    ffn_act(Unit(U_FFN + 3 + 3 * jj, it), it * 2 + (jj + 1), (jj + 1) % 2)
            for i in range(2):
                hi(Unit(U_QKV + i))
            norm_stats(2, ACT.Exp)
            split_t_hi(3)
            hi(Unit(U_QKV + 2))
            act.wait_ge(xn_ready, 8)
            act.dma_start(gains[:, 0, :], over_partitions(ln_final, D)).then_inc(gain_in[4], 16)

            def qkv_out(i):
                act.wait_ge(used, U_QKV + (12 if i >= 8 else i + 1))
                src = banks[:, 4 + i % 4, :].rearrange("p (a b) -> p a b", a=2)
                if i == 0:
                    act.wait_ge(q_zero, 2)
                if i < 4:
                    last = queries(qc_t[0], i, src)
                elif i < 8:
                    last = act.copy(vc[:, :, 256 * (i - 4):256 * (i - 4) + 256], src)
                else:
                    last = act.copy(kc_t[0][:, 2 * (i - 8):2 * (i - 8) + 2, :], src)
                last.then_inc(proj_out, 1)

            for i in range(12):
                if i < 9:
                    hi(Unit(U_QKV + 3 + i))
                qkv_out(i)

            for n in range(16, 16 + CH):
                softmax(n, "neighbourhood", n - 16)
                if n >= 18:
                    prob_out(n - 2)
                if n in (19, 23, 27):
                    hi(Unit(U_OUT1 + n // 4 - 4))
            prob_out(14 + CH)
            prob_out(15 + CH)
            split_t_hi(4)
            for i in range(3):
                hi(Unit(U_OUT1 + 3 + i))
            norm_stats(3, ACT.Exp)
            for i in range(4):
                act.wait_ge(t_mm, 20 + i + 1)
                act.copy(x_t[:, 2 * i:2 * i + 2, :],
                         banks[:, i, :].rearrange("p (k s) -> p k s", k=2)).then_inc(t_hi_done, 1)
            for t in range(T):
                act.copy(xn_split[0][:, t, :], xn[:, t, :]).then_inc(xn_hi_done, 1)
            act.wait_ge(route_v, 1)
            act.activation(top_w[:, :, 1], top_w[:, :, 0], ACT.Exp).then_inc(route_a, 1)
            warm(ACT.Silu)
            hi(Unit(U_MOE + 2))

            def gather_hi(v):
                for i in range(2):
                    act.wait_ge(gath_mm, v * 2 + (i + 1))
                    act.copy(t_hi[:, 4 * i:4 * i + 4, 0:P],
                             banks[:, 2 + i, :].rearrange("p (k s) -> p k s", k=4)).then_inc(gath_hi, 1)

            def silu(u):
                act.wait_ge(used, u.count())
                act.activation(act_g[:], banks[:, 4, :], ACT.Silu).then_inc(silu_done, 1)

            def hid_t_hi(s, slot=0):
                act.wait_ge(ht_mm, s + 1)
                act.copy(h_hi[:, slot, :], banks[:, 6, :]).then_inc(h_hi_done, 1)

            def comb_copy(v):
                act.wait_ge(comb_mm, v + 1)
                act.copy(comb[:], banks[:, 7, 0:SEQ]).then_inc(comb_out, 1)

            def y_copy(u):
                act.wait_ge(used, u.count())
                for c in range(2):
                    act.copy(y_hi[:, c * HALF:(c + 1) * HALF], banks[:, c, :]).then_inc(y_out, 1)

            def middle(e, j, base, sweep):
                s = (e + sweep * E) * MOE_STEPS + j + 1
                for c in (6, 7, 8, 9):
                    hi(unit_of(base, e, c, j))
                silu(unit_of(base, e, 7, j))
                hi(unit_of(base, e, 10, j))
                hi(unit_of(base, e, 11, j))
                hid_t_hi(s)

            def edge(e, nxt, base, sweep):
                if e is None:
                    gather_hi(sweep * E)
                    for c in range(0 if sweep else 3, 4):
                        hi(unit_of(base, 0, c))
                    silu(unit_of(base, 0, 3))
                    hi(unit_of(base, 0, 4))
                    hi(unit_of(base, 0, 5))
                    hid_t_hi(sweep * E * MOE_STEPS)
                    return
                v = e + sweep * E
                s = v * MOE_STEPS + (MOE_STEPS - 1)
                for c in (36, 37, 38, 39):
                    hi(unit_of(base, e, c))
                silu(unit_of(base, e, 37))
                hi(unit_of(base, e, 40))
                comb_copy(v)
                if nxt is not None:
                    gather_hi(v + 1)
                if nxt is None:
                    hid_t_hi(s, 1)
                    hi(unit_of(base, e, 41))
                else:
                    hi(unit_of(base, e, 41))
                    hid_t_hi(s)
                if nxt is not None:
                    for c in (42, 43, 44, 45):
                        hi(unit_of(base, e, c))
                    silu(unit_of(base, e, 43))
                    hi(unit_of(base, e, 46))
                    hi(unit_of(base, e, 47))
                y_copy(unit_of(base, e, 41 if nxt is None else 45))
                if nxt is not None:
                    hid_t_hi(s + 1)

            moe_sweep(act, edge, middle, 0)
            act.wait_ge(over_set, 1)
            n_over = act.value_load(over[0:1, 0:1], min_val=0, max_val=SEQ)
            with act.If(n_over > P):
                moe_sweep(act, edge, middle, 1)
            with act.Else():
                act.nop()
            norm_stats(4)

        @block.vector
        def _(dve):
            dve.memset(one, 1.0)
            dve.memset(zero_b[:], 0.0).then_inc(tab_b, 1)
            dve.engine_nop().then_inc(y_add, 1)

            def lo(u, n=UNIT):
                dve.wait_ge(hi_done, u.count())
                dve.tensor_tensor(w_lo[:, u.part, 0:n], raw[:, u.raw, 0:n],
                                  w_hi[:, u.part, 0:n].bitcast(F32), ALU.subtract).then_inc(lo_done, 1)

            def norm_apply(n, gain):
                for t in range(T):
                    col = slice(t, t + 1)
                    dve.wait_ge(ss_done, 2 * n + t + 1)
                    dve.tensor_scalar(mean_sq[:, col], sums_sq[:, col], 1.0 / D, EPS, ALU.mult,
                                      ALU.add).then_inc(ms_done, 1)
                    dve.wait_ge(std_done, 2 * n + t + 1)
                    dve.reciprocal(rstd[:, col], std[:, col]).then_inc(rstd_done, 1)
                    dve.wait_ge(rstd_done, 2 * n + t + 1)
                    dve.wait_ge(gain_in[n], 16)
                    dve.scalar_tensor_tensor(out=xn[:, t, :], in0=xres[:, t, :], scalar=rstd[:, col],
                                             in1=gains[:, gain, :], op0=ALU.mult, op1=ALU.mult).then_inc(xn_ready, 1)

            def split_t_lo(q):
                for i in range(4):
                    dve.wait_ge(t_hi_done, 4 * q + i + 1)
                    dve.tensor_tensor(t_lo[:, 2 * i:2 * i + 2, :],
                                      banks[:, i, :].rearrange("p (k s) -> p k s", k=2),
                                      t_hi[:, 2 * i:2 * i + 2, :].bitcast(F32), ALU.subtract).then_inc(t_lo_done, 1)

            norm_apply(0, 0)
            lo(Unit(0))
            split_t_lo(0)

            def in_lo(i):
                lo(Unit(i), 8 * IN_COLS[i][1])

            def rest(dst, dst_hi, bank, n_out):
                dve.wait_ge(proj_out, n_out)
                dve.tensor_tensor(dst, banks[:, bank, :].rearrange("p (a b) -> p a b", a=2), dst_hi.bitcast(F32),
                                  ALU.subtract).then_inc(qk_rest, 1)

            def rest_queries(q, i, bank, n_out):
                dve.wait_ge(proj_out, n_out)
                src = banks[:, bank, :].rearrange("p (a b) -> p a b", a=2)
                for half in range(2):
                    rows_h = slice(HD * half, HD * half + HD)
                    hi_h, lo_h = (w[rows_h, 2 * i:2 * i + 2, half, :] for w in q)
                    last = dve.tensor_tensor(lo_h, src[rows_h], hi_h.bitcast(F32), ALU.subtract)
                last.then_inc(qk_rest, 1)

            def in_rest(i):
                if i < 4:
                    rest_queries(qa_t, i - 2, 4 + i % 4, i + 1)
                else:
                    c = slice(2 * (i - 4), 2 * (i - 4) + 2)
                    rest(ka_t[1][:, c, :], ka_t[0][:, c, :], 4 + i % 4, i + 1)

            for i in range(1, 4):
                in_lo(i)
            dve.wait_ge(lat_a, 1)
            dve.tensor_scalar(lat_ms[:, 0:2], lat_ss[:, 0:2], 1.0 / QL, EPS, ALU.mult, ALU.add)
            dve.tensor_scalar(lat_ms[:, 2:4], lat_ss[:, 2:4], 1.0 / KVL, EPS, ALU.mult, ALU.add).then_inc(lat_v, 1)
            dve.wait_ge(lat_a, 2)
            dve.reciprocal(lat_rstd, lat_std).then_inc(lat_v, 1)
            dve.wait_ge(lat_v, 2)
            dve.wait_ge(lat_in, 64)
            for t in range(T):
                dve.scalar_tensor_tensor(out=qn[:, t, :], in0=ql[:, t, :], scalar=lat_rstd[:, t:t + 1],
                                         in1=lat_gain[:, 0:QL], op0=ALU.mult, op1=ALU.mult)
                last = dve.scalar_tensor_tensor(out=kvn[:, t, :], in0=kl[:, t, 0:KVL],
                                                scalar=lat_rstd[:, 2 + t:3 + t],
                                                in1=lat_gain[:, QL:QL + KVL], op0=ALU.mult, op1=ALU.mult)
            last.then_inc(lat_v, 1)
            in_lo(4)

            cos = tab[:, C_COS:C_COS + 32].rearrange("p (t c) -> p t c", t=T)
            sin = tab[:, C_SIN:C_SIN + 32].rearrange("p (t c) -> p t c", t=T)
            dve.wait_ge(tables_in, 16)

            def rope(x1, x2, c, s, tmp, y1, y2, step):
                dve.tensor_tensor(tmp(0), x1, c, ALU.mult)
                dve.tensor_tensor(tmp(1), x2, s, ALU.mult)
                dve.tensor_tensor(tmp(2), x1, s, ALU.mult)
                dve.tensor_tensor(tmp(3), x2, c, ALU.mult).then_inc(lat_v, 1)
                dve.wait_ge(lat_v, step + 1)
                dve.tensor_tensor(y1, tmp(0), tmp(1), ALU.subtract)
                dve.tensor_tensor(y2, tmp(2), tmp(3), ALU.add).then_inc(lat_v, 1)

            rope(kl[:, :, KVL:KVL + 16], kl[:, :, KVL + 16:KVL + 32], cos, sin,
                 lambda i: k_tmp[:, i], k_pe[:, :, 0:16], k_pe[:, :, 16:32], 3)
            in_lo(5)
            in_rest(2)
            dve.wait_ge(lat_v, 5)
            for t in range(T):
                dve.tensor_copy(k_tok[:, t, :, HD:BK], k_pe[:, t, :].unsqueeze(1).broadcast_to([P, BH, ROPE]))
            in_lo(6)
            in_rest(3)
            dve.wait_ge(lat_a, 4)
            cos_h = cos.unsqueeze(2).broadcast_to([P, T, BH, 16])
            sin_h = sin.unsqueeze(2).broadcast_to([P, T, BH, 16])
            rope(q_tok[:, :, :, HD:HD + 16], q_tok[:, :, :, HD + 16:BK], cos_h, sin_h,
                 lambda i: q_tmp[:, i], q_tok[:, :, :, HD:HD + 16], q_tok[:, :, :, HD + 16:BK], 5)
            in_lo(7)
            in_rest(4)
            dve.wait_ge(lat_p, 3)
            for b in range(2):
                src = banks[:, 2 + b, :].rearrange("p (h c) -> p h c", h=4)
                dve.tensor_copy(k_tok[:, 1, 4 * b:4 * b + 4, 0:HD], src[:, :, 0:HD])
                last = dve.tensor_copy(vb[:, 1, 4 * b:4 * b + 4, :], src[:, :, HD:2 * HD])
            last.then_inc(lat_v, 1)
            in_rest(5)
            for h in range(BH):
                dve.wait_ge(lat_a, 6 + h)
                dve.tensor_tensor(lat_t[1][h][0:BK, :], banks[0:BK, h % 4, :], lat_t[0][h][0:BK, :].bitcast(F32),
                                  ALU.subtract).then_inc(lat_v, 1)

            def row_max(n, kind, h):
                b = n % 4
                dve.wait_ge(s_mm, n + 1)
                if n >= 4:
                    dve.wait_ge(pt_mm, n - 3)
                scores = banks[:, S_BANK[b], :]
                if kind == "latent":
                    dve.tensor_reduce(neg_max[:, b, :], scores.rearrange("p (t s) -> p t s", t=T), AX_X, ALU.max,
                                      negate=True).then_inc(max_step, 1)
                    dve.wait_ge(max_step, h + 1)
                    dve.tensor_scalar(neg_max[:, b, :], neg_max[:, b, :], BK ** -0.5, None,
                                      ALU.mult).then_inc(max_ready, 1)
                    return
                if kind == "dilated":
                    dve.wait_ge(bias_ready, h + 1)
                    dve.scalar_tensor_tensor(out=prob[:, b, :], in0=scores, scalar=HD ** -0.5,
                                             in1=bias_a[h % len(bias_a)], op0=ALU.mult, op1=ALU.add).then_inc(s_read, 1)
                else:
                    for t in range(T):
                        cut = slice(t * SEQ, (t + 1) * SEQ)
                        first = (2 - 2 * t) * RPB_C + GRID_W - 1
                        row = rpb[h // 8]
                        table = bass.AP(row.tensor, row[:, h % 8, first:first + 1].offset,
                                        [[row.ap[0][0], P], [RPB_C, 4], [-1, GRID_W]])
                        last = dve.scalar_tensor_tensor(
                            out=prob[:, b, cut].rearrange("p (r c) -> p r c", r=4),
                            in0=scores[:, cut].rearrange("p (r c) -> p r c", r=4), scalar=HD ** -0.5,
                            in1=table, op0=ALU.mult, op1=ALU.add)
                    last.then_inc(s_read, 1)
                dve.wait_ge(s_read, n + 1 if n < 16 else n + 1 - BH)
                dve.tensor_reduce(neg_max[:, b, :], prob[:, b, :].rearrange("p (t s) -> p t s", t=T), AX_X, ALU.max,
                                  negate=True).then_inc(max_ready, 1)

            def head_group(g, col):
                dve.wait_ge(pv_mm, 8 * g + 8)
                c0 = 8 * (g % 2)
                dve.reciprocal(row_sum[:, :, c0:c0 + 8], row_sum[:, :, c0:c0 + 8]).then_inc(inv_done, 1)
                dve.wait_ge(inv_done, g + 1)
                for t in range(T):
                    dve.tensor_tensor(
                        xn[:, t, col:col + 512].rearrange("p (h c) -> p h c", h=8),
                        banks[:, 4 + t, :].rearrange("p (h c) -> p h c", h=8),
                        row_sum[:, t, c0:c0 + 8].unsqueeze(2).broadcast_to([P, 8, HD]),
                        ALU.mult).then_inc(xn_ready if g % 2 else heads_out, 1)

            for n in range(AH + BH):
                row_max(n, "dilated" if n < AH else "latent", n % 8)
                if n in (5, 9, 13):
                    lo(Unit(U_OUT0 + n // 4 - 1))
                if n == 11:
                    head_group(0, 0)
            head_group(1, 512)
            split_t_lo(1)

            def residual(bank, u):
                dve.wait_ge(used, u + 1)
                for t in range(T):
                    both = xres[:, t, :].rearrange("p (a b) -> p a b", a=2)
                    dve.tensor_tensor(both, both, banks[:, bank + 2 * t:bank + 2 * t + 2, :],
                                      ALU.add).then_inc(x_tile, 1)

            for i in range(3):
                lo(Unit(U_OUT0 + 3 + i))
            residual(4, U_OUT0 + 3)
            dve.wait_ge(x_tile, 2)
            norm_apply(1, 1)
            split_t_lo(2)
            lo(Unit(U_FFN + 2))

            def ffn_dve(j, jj):
                dve.wait_ge(silu_done, j + 1)
                dve.tensor_tensor(hid[:], act_g[:], banks[:, 5 + 2 * jj, :], ALU.mult).then_inc(hid_done, 1)
                dve.wait_ge(h_hi_done, j + 1)
                dve.tensor_tensor(h_lo[:, jj, :], hid[:], h_hi[:, jj, :].bitcast(F32),
                                  ALU.subtract).then_inc(h_lo_done, 1)

            ffn_dve(0, 0)
            with dve.Fori(0, (FFN_STEPS - 1) // 2) as it:
                for jj in range(2):
                    for i in range(3):
                        lo(Unit(U_FFN + 3 + 3 * jj + i, it))
                    ffn_dve(it * 2 + (jj + 1), (jj + 1) % 2)
            lo(Unit(U_QKV))
            lo(Unit(U_QKV + 1))
            residual(0, U_FFN + 32)
            dve.wait_ge(x_tile, 4)
            norm_apply(2, 0)
            split_t_lo(3)
            lo(Unit(U_QKV + 2))
            for i in range(12):
                if i < 9:
                    lo(Unit(U_QKV + 3 + i))
                if i < 4:
                    rest_queries(qc_t, i, 4 + i % 4, 8 + i + 1)
                elif i >= 8:
                    c = slice(2 * (i - 8), 2 * (i - 8) + 2)
                    rest(kc_t[1][:, c, :], kc_t[0][:, c, :], 4 + i % 4, 8 + i + 1)
            dve.wait_ge(rpb_in, 64)
            for n in range(16, 16 + CH):
                row_max(n, "neighbourhood", n - 16)
                if n in (21, 25, 29):
                    lo(Unit(U_OUT1 + n // 4 - 5))
                if n == 27:
                    head_group(2, 0)
            head_group(3, 512)
            split_t_lo(4)
            for i in range(3):
                lo(Unit(U_OUT1 + 3 + i))
            residual(4, U_OUT1 + 3)
            dve.wait_ge(x_tile, 6)
            norm_apply(3, 1)

            def xn_lo(t):
                dve.wait_ge(xn_hi_done, t + 1)
                dve.tensor_tensor(xn_split[1][:, t, :], xn[:, t, :], xn_split[0][:, t, :].bitcast(F32),
                                  ALU.subtract).then_inc(xn_lo_done, 1)

            xn_lo(0)
            dve.wait_ge(route_mm, 1)
            dve.tensor_copy(logits[:], banks[:, 4:6, 0:E]).then_inc(route_step, 1)
            dve.wait_ge(route_step, 1)
            for t in range(T):
                last = dve.max(out=top_v[:, t, :], in_=logits[:, t, :])
            last.then_inc(route_step, 1)
            dve.wait_ge(route_step, 2)
            dve.tensor_tensor(top_w[:, :, 0], top_v[:, :, 1], top_v[:, :, 0], ALU.subtract).then_inc(route_v, 1)
            for t in range(T):
                last = dve.max_index(out=top_i[:, t, :], in_max=top_v[:, t, :], in_values=logits[:, t, :])
            last.then_inc(route_step, 1)
            dve.wait_ge(route_step, 3)
            dve.tensor_copy(top_f[:], top_i[:]).then_inc(route_step, 1)
            dve.wait_ge(route_step, 4)
            experts = tab[:, C_IOTA:C_IOTA + E]
            for t in range(T):
                dve.tensor_scalar(one_a[:, t, :], experts, top_f[:, t, 0:1], None, ALU.is_equal)
                last = dve.tensor_scalar(one_b[:, t, :], experts, top_f[:, t, 1:2], None, ALU.is_equal)
            last.then_inc(route_step, 1)
            dve.wait_ge(route_step, 5)
            dve.tensor_tensor(mask[:], one_a[:], one_b[:], ALU.add).then_inc(route_v, 1)
            xn_lo(1)
            dve.wait_ge(route_mm, 2)
            dve.scalar_tensor_tensor(out=place[:], in0=banks[:, 6, 0:16].rearrange("p (t e) -> p t e", t=T),
                                     scalar=1.0, in1=mask[:], op0=ALU.add, op1=ALU.mult).then_inc(route_step, 1)
            dve.wait_ge(route_step, 6)
            dve.tensor_scalar(place[:], place[:], -1.0, None, ALU.add).then_inc(route_v, 1)
            dve.wait_ge(route_v, 3)
            for t in range(T):
                last = dve.tensor_scalar(pick[:, t, :], tab[:, C_IOTA:C_IOTA + P], place[:, t, 0:1], None,
                                         ALU.is_equal)
            last.then_inc(pick_ready, 1)
            dve.tensor_reduce(most, banks[:, 6, 16:24], AX_X, ALU.max).then_inc(route_step, 1)
            dve.wait_ge(route_a, 1)
            dve.tensor_scalar(top_w[:, :, 2], top_w[:, :, 1], 1.0, None, ALU.add).then_inc(route_step, 1)
            dve.wait_ge(route_step, 7)
            dve.tensor_copy(over[:], most).then_inc(over_set, 1)
            dve.wait_ge(route_step, 8)
            dve.reciprocal(top_w[:, :, 2], top_w[:, :, 2]).then_inc(route_step, 1)
            dve.wait_ge(route_step, 9)
            dve.tensor_tensor(top_w[:, :, 3], top_w[:, :, 1], top_w[:, :, 2], ALU.mult).then_inc(route_step, 1)
            dve.wait_ge(route_step, 10)
            for t in range(T):
                last = dve.tensor_scalar(gate[:, t, :], one_a[:, t, :], top_w[:, t, 2:3], None, ALU.mult)
            last.then_inc(route_step, 1)
            dve.wait_ge(route_step, 11)
            for t in range(T):
                last = dve.scalar_tensor_tensor(out=gate[:, t, :], in0=one_b[:, t, :], scalar=top_w[:, t, 3:4],
                                                in1=gate[:, t, :], op0=ALU.mult, op1=ALU.add)
            last.then_inc(route_v, 1)

            def gather_lo(v):
                for i in range(2):
                    dve.wait_ge(gath_hi, v * 2 + (i + 1))
                    dve.tensor_tensor(t_lo[:, 4 * i:4 * i + 4, 0:P],
                                      banks[:, 2 + i, :].rearrange("p (k s) -> p k s", k=4),
                                      t_hi[:, 4 * i:4 * i + 4, 0:P].bitcast(F32), ALU.subtract).then_inc(gath_lo, 1)

            def gated(s):
                dve.wait_ge(silu_done, s + (FFN_STEPS + 1))
                dve.tensor_tensor(hid[:], act_g[:], banks[:, 5, :], ALU.mult).then_inc(hid_done, 1)

            def hid_t_lo(s, slot=0):
                dve.wait_ge(h_hi_done, s + (FFN_STEPS + 1))
                dve.tensor_tensor(h_lo[:, slot, :], banks[:, 6, :], h_hi[:, slot, :].bitcast(F32),
                                  ALU.subtract).then_inc(h_lo_done, 1)

            def y_split(v):
                for c in range(2):
                    cols = slice(c * HALF, (c + 1) * HALF)
                    dve.wait_ge(y_out, v * 2 + (c + 1))
                    dve.tensor_tensor(y_lo[:, cols], banks[:, c, :], y_hi[:, cols].bitcast(F32),
                                      ALU.subtract).then_inc(y_rest, 1)

            def add_y(v):
                dve.wait_ge(gate_ready, v + 1)
                for i, (t, c) in enumerate(((0, 0), (1, 0), (0, 1), (1, 1))):
                    dve.wait_ge(scat_mm, v * 4 + (i + 1))
                    cols = xres[:, t, c * HALF:(c + 1) * HALF]
                    if i == 0:
                        dve.wait_ge(y_add, v * 4 + 1)
                    dve.scalar_tensor_tensor(out=cols, in0=banks[:, (7, 2, 3, 7)[i], :], scalar=gate_e[:, t:t + 1],
                                             in1=cols, op0=ALU.mult, op1=ALU.add).then_inc(y_add, 1)

            def middle(e, j, base, sweep):
                s = (e + sweep * E) * MOE_STEPS + j + 1
                for c in (6, 7, 8, 9):
                    lo(unit_of(base, e, c, j))
                gated(s)
                lo(unit_of(base, e, 10, j))
                lo(unit_of(base, e, 11, j))
                hid_t_lo(s)

            def edge(e, nxt, base, sweep):
                if e is None:
                    gather_lo(sweep * E)
                    if not sweep:
                        lo(Unit(U_MOE + 2))
                    for c in range(0 if sweep else 3, 4):
                        lo(unit_of(base, 0, c))
                    gated(sweep * E * MOE_STEPS)
                    lo(unit_of(base, 0, 4))
                    lo(unit_of(base, 0, 5))
                    hid_t_lo(sweep * E * MOE_STEPS)
                    return
                v = e + sweep * E
                s = v * MOE_STEPS + (MOE_STEPS - 1)
                for c in (36, 37, 38):
                    lo(unit_of(base, e, c))
                if nxt is None:
                    gated(s)
                    lo(unit_of(base, e, 39))
                    hid_t_lo(s, 1)
                    lo(unit_of(base, e, 40))
                    lo(unit_of(base, e, 41))
                else:
                    lo(unit_of(base, e, 39))
                    gated(s)
                    lo(unit_of(base, e, 40))
                    gather_lo(v + 1)
                    lo(unit_of(base, e, 41))
                    hid_t_lo(s)
                if nxt is not None:
                    for c in (42, 43, 44, 45):
                        lo(unit_of(base, e, c))
                    gated(s + 1)
                    lo(unit_of(base, e, 46))
                    lo(unit_of(base, e, 47))
                y_split(v)
                if nxt is not None:
                    hid_t_lo(s + 1)
                add_y(v)

            moe_sweep(dve, edge, middle, 0)
            dve.wait_ge(over_set, 1)
            n_over = dve.value_load(over[0:1, 0:1], min_val=0, max_val=SEQ)
            with dve.If(n_over > P):
                moe_sweep(dve, edge, middle, 1)
                dve.wait_ge(y_add, 2 * 4 * E + 1)
            with dve.Else():
                dve.wait_ge(y_add, 4 * E + 1)
            dve.engine_nop().then_inc(x_tile, 2)
            norm_apply(4, 0)

        @block.tensor
        def _(pe):
            def three(out, a_hi, a_lo, b_hi, b_lo, start, stop):
                pe.matmul(out, a_hi, b_hi, start=start, stop=False)
                pe.matmul(out, a_lo, b_hi, start=False, stop=False)
                return pe.matmul(out, a_hi, b_lo, start=False, stop=stop)

            def unit_parts(u, k, n):
                cut = lambda w: w[:, u.part, 0:k * n].rearrange("p (k n) -> p k n", k=k)
                return cut(w_hi), cut(w_lo)

            def transpose_xn(q):
                for t in range(T):
                    pe.wait_ge(xn_ready, 2 * q + t + 1)
                    for i in range(4):
                        for k in range(2):
                            c = (2 * i + k) * P
                            last = pe.transpose(banks[:, i, (2 * k + t) * P:(2 * k + t + 1) * P],
                                                xn[:, t, c:c + P], ident)
                        if t == T - 1:
                            last.then_inc(t_mm, 1)

            def columns(u, bank, n, transposed, split=None):
                pe.wait_ge(lo_done, u.count())
                hi_w, lo_w = unit_parts(u, KD, n)
                for m in range(2):
                    cut = slice(m * P, (m + 1) * P)
                    dst = banks[:, bank, m * 256:m * 256 + (256 if transposed else n)]
                    for k in range(KD):
                        if split is not None and m == 0 and k % 2 == 0:
                            pe.wait_ge(t_lo_done, 4 * split + k // 2 + 1)
                        if transposed:
                            last = three(dst, hi_w[:, k, cut], lo_w[:, k, cut], t_hi[:, k, :], t_lo[:, k, :],
                                         k == 0, k == KD - 1)
                        else:
                            last = three(dst, t_hi[:, k, cut], t_lo[:, k, cut], hi_w[:, k, :], lo_w[:, k, :],
                                         k == 0, k == KD - 1)
                return last

            def rows(u, bank, lhs_hi, lhs_lo, n_t, start, stop):
                pe.wait_ge(lo_done, u.count())
                hi_w, lo_w = unit_parts(u, 2, D)
                for i in range(2):
                    for t in range(n_t):
                        for c in range(2):
                            cols = slice(c * HALF, (c + 1) * HALF)
                            last = three(banks[:, bank + 2 * t + c, :], lhs_hi(i, t), lhs_lo(i, t),
                                         hi_w[:, i, cols], lo_w[:, i, cols], start and i == 0, stop and i == 1)
                return last

            def keep_busy(bank, n):
                for _ in range(n):
                    pe.matmul(banks[:, bank, :].rearrange("p (r c) -> p r c", r=4), ident_b[:],
                              ident_b[:].unsqueeze(1).broadcast_to([P, 4, P]), start=True, stop=True)

            pe.wait_ge(tables_in, 16)
            pe.wait_ge(tab_b, 2)
            keep_busy(7, 10)
            transpose_xn(0)

            def in_proj(i):
                if i >= 4:
                    pe.wait_ge(proj_out, i - 3)
                    if i >= 6:
                        pe.wait_ge(qk_rest, i - 5)
                columns(Unit(i), 4 + i % 4, IN_COLS[i][1], 2 <= i < 6, 0 if i == 0 else None).then_inc(used, 1)

            for i in range(4):
                in_proj(i)
            pe.wait_ge(lat_v, 3)
            for k in range(2):
                for t in range(T):
                    pe.transpose(banks[:, 0, (2 * k + t) * P:(2 * k + t + 1) * P], qn[:, t, k * P:(k + 1) * P], ident)
            for t in range(T):
                last = pe.transpose(banks[:, 1, t * P:(t + 1) * P], kvn[:, t, :], ident)
            last.then_inc(lat_p, 1)
            in_proj(4)
            pe.wait_ge(lat_a, 3)
            pe.wait_ge(lat_in, 64)
            for t, b in enumerate((2, 0)):
                for c0, n, bank in ((0, 512, b), (512, 256, b + 1)):
                    for k in range(2):
                        last = pe.matmul(banks[:, bank, 0:n], qn_t[:, k, t * P:(t + 1) * P], uq[:, k, c0:c0 + n],
                                         start=(k == 0), stop=(k == 1))
            last.then_inc(lat_p, 1)
            in_proj(5)
            in_proj(6)
            pe.wait_ge(lat_a, 4)
            for t in range(T):
                for c in range(2):
                    last = pe.matmul(banks[:, 2 * t + c, :], kvn_t[:, t * P:(t + 1) * P],
                                     ukv[:, c * HALF:(c + 1) * HALF], start=True, stop=True)
            last.then_inc(lat_p, 1)
            in_proj(7)
            pe.wait_ge(lat_a, 5)
            pe.wait_ge(lat_v, 8)
            for h in range(BH):
                if h >= 4:
                    pe.wait_ge(lat_v, 8 + h - 3)
                for i, src in enumerate((q_tok, q_tok, k_tok, k_tok)):
                    last = pe.transpose(banks[0:BK, h % 4, i * P:(i + 1) * P], src[:, i % 2, h, :], ident)
                last.then_inc(lat_p, 1)

            def scores(n, kind, h):
                b = S_BANK[n % 4]
                if n >= 4:
                    if n - 4 < AH:
                        pe.wait_ge(s_read, n - 3)
                    elif n - 4 < AH + BH:
                        pe.wait_ge(exp_done, n - 3)
                    else:
                        pe.wait_ge(s_read, n - 3 - BH)
                if kind == "latent":
                    if h == 0:
                        pe.wait_ge(lat_zero, 2)
                    for t in range(T):
                        last = three(banks[:, b, t * SEQ:(t + 1) * SEQ], *(w[h][:, t * P:(t + 1) * P] for w in lat_t),
                                     *(w[h][:, 2 * P:4 * P] for w in lat_t), True, True)
                    last.then_inc(s_mm, 1)
                    return
                q, k = (qa_t, ka_t) if kind == "dilated" else (qc_t, kc_t)
                if kind == "neighbourhood" and h % 4 == 0:
                    pe.wait_ge(qk_rest, 9 + h // 4)
                for t in range(T):
                    dst = banks[:, b, t * SEQ:(t + 1) * SEQ]
                    if kind == "neighbourhood":
                        pe.matmul(dst.rearrange("p (r c) -> p r c", r=4), ident_b[:],
                                  mask_b[:].unsqueeze(1).broadcast_to([P, 4, GRID_W]), start=True, stop=False)
                    last = three(dst, *(w[:, h // 2, h % 2, t * P:(t + 1) * P] for w in q),
                                 *(w[:, h // 2, :] for w in k), kind == "dilated", True)
                last.then_inc(s_mm, 1)

            def turn_probs(n):
                pe.wait_ge(exp_done, n + 1)
                if n >= 2:
                    pe.wait_ge(pt_out, n - 1)
                b = n % 4
                for k in range(2):
                    for t in range(T):
                        last = pe.transpose(banks[:, T_BANK[n % 2], (2 * k + t) * P:(2 * k + t + 1) * P],
                                            prob[:, b, t * SEQ + k * P:t * SEQ + (k + 1) * P], ident)
                last.then_inc(pt_mm, 1)

            def values(n, v):
                pe.wait_ge(pt_out, n + 1)
                if n % 16 == 8:
                    pe.wait_ge(heads_out, n // 8 + 1)
                c = HD * (n % 8)
                for t in range(T):
                    for k in range(2):
                        last = pe.matmul(banks[:, 4 + t, c:c + HD],
                                         prob_t[:, n % 2, (2 * k + t) * P:(2 * k + t + 1) * P], v(k),
                                         start=(k == 0), stop=(k == 1))
                last.then_inc(pv_mm, 1)

            pe.wait_ge(proj_out, 8)
            pe.wait_ge(qk_rest, 4)
            pe.wait_ge(lat_v, 16)
            pe.wait_ge(q_zero, 1)
            for n in range(AH + BH + 4):
                if n < AH + BH:
                    scores(n, "dilated" if n < AH else "latent", n % 8)
                if 2 <= n < AH + BH + 2:
                    turn_probs(n - 2)
                if n >= 4:
                    m = n - 4
                    values(m, (lambda k: va[:, k, m * HD:(m + 1) * HD]) if m < AH else (lambda k: vb[:, k, m - AH, :]))
            transpose_xn(1)

            def out_proj(first, q):
                for i in range(4):
                    pe.wait_ge(t_lo_done, 4 * q + i + 1)
                    last = rows(Unit(first + i), 4, lambda k, t: t_hi[:, 2 * i + k, t * P:(t + 1) * P],
                                lambda k, t: t_lo[:, 2 * i + k, t * P:(t + 1) * P], T, i == 0, i == 3)
                    last.then_inc(used, 1)

            out_proj(U_OUT0, 1)
            keep_busy(0, GAP)
            transpose_xn(2)

            def ffn_gate_up(u_g, u_u, j, jj, split=None):
                columns(u_g, 4 + 2 * jj, 256, True, split).then_inc(used, 1)
                columns(u_u, 5 + 2 * jj, 256, True).then_inc(used, 1)

            def ffn_down(u, j, jj, stop=False):
                pe.wait_ge(h_hi_done, j + 1)
                pe.wait_ge(h_lo_done, j + 1)
                rows(u, 0, lambda k, t: h_hi[:, jj, k * SEQ + t * P:k * SEQ + (t + 1) * P],
                     lambda k, t: h_lo[:, jj, k * SEQ + t * P:k * SEQ + (t + 1) * P], T, False, stop).then_inc(used, 1)

            def clear(bank):
                return pe.matmul(banks[:, bank, :].rearrange("p (r c) -> p r c", r=4), zero_b[:],
                                 zero_b[:].unsqueeze(1).broadcast_to([P, 4, P]), start=True, stop=False)

            ffn_gate_up(Unit(U_FFN), Unit(U_FFN + 1), 0, 0, 2)
            pe.wait_ge(tab_b, 3)
            for b in range(4):
                clear(b)
            with pe.Fori(0, (FFN_STEPS - 1) // 2) as it:
                for jj in range(2):
                    ffn_gate_up(Unit(U_FFN + 2 + 3 * jj, it), Unit(U_FFN + 3 + 3 * jj, it), it * 2 + (jj + 1),
                                (jj + 1) % 2)
                    ffn_down(Unit(U_FFN + 4 + 3 * jj, it), it * 2 + jj, jj)
            ffn_down(Unit(U_FFN + 32), FFN_STEPS - 1, 0, True)

            keep_busy(6, GAP)
            transpose_xn(3)
            for i in range(12):
                if i >= 4:
                    pe.wait_ge(proj_out, 8 + i - 3)
                    pe.wait_ge(qk_rest, 4 + min(i - 3, 4))
                columns(Unit(U_QKV + i), 4 + i % 4, 256, not 4 <= i < 8, 3 if i == 0 else None).then_inc(used, 1)
            for n in range(16, 16 + CH + 4):
                if n < 16 + CH:
                    scores(n, "neighbourhood", n - 16)
                if 18 <= n < 16 + CH + 2:
                    turn_probs(n - 2)
                if n >= 20:
                    m = n - 20
                    values(n - 4, lambda k: vc[:, k, m * HD:(m + 1) * HD])
            transpose_xn(4)
            out_proj(U_OUT1, 4)
            keep_busy(0, GAP)

            transpose_xn(5)
            pe.wait_ge(router_in, 16)
            for k in range(KD):
                if k % 2 == 0:
                    pe.wait_ge(t_hi_done, 20 + k // 2 + 1)
                for t in range(T):
                    last = pe.matmul(banks[:, 4 + t, 0:E], x_t[:, k, t * P:(t + 1) * P], router[:, k, :],
                                     start=(k == 0), stop=(k == KD - 1))
            last.then_inc(route_mm, 1)
            keep_busy(7, 8)
            pe.wait_ge(route_v, 2)
            pe.matmul(banks[:, 6, 0:E], tri, mask[:, 0, :], start=True, stop=True)
            pe.matmul(banks[:, 6, E:2 * E], tri, mask[:, 1, :], start=True, stop=False)
            pe.matmul(banks[:, 6, E:2 * E], ones, mask[:, 0, :], start=False, stop=True)
            pe.matmul(banks[:, 6, 2 * E:3 * E], ones, mask[:, 0, :], start=True, stop=False)
            pe.matmul(banks[:, 6, 2 * E:3 * E], ones, mask[:, 1, :], start=False, stop=True).then_inc(route_mm, 1)
            keep_busy(7, 8)

            def gather(v):
                pe.wait_ge(pick_ready, v + 1)
                for k in range(KD):
                    dst = banks[:, 2 + k // 4, (k % 4) * P:(k % 4 + 1) * P]
                    for t in range(T):
                        for i in range(2):
                            last = pe.matmul(dst, xn_split[i][:, t, k * P:(k + 1) * P], pick[:, t, :],
                                             start=(t == 0 and i == 0), stop=(t == 1 and i == 1))
                    if k % 4 == 3:
                        last.then_inc(gath_mm, 1)

            def gate_up(base, units, gathered=None):
                for i in range(4):
                    u = unit_of(base, *units[i])
                    if gathered is not None and i < 2:
                        pe.wait_ge(gath_lo, gathered * 2 + i + 1)
                    pe.wait_ge(lo_done, u.count())
                    hi_w, lo_w = unit_parts(u, 4, HALF)
                    for k in range(4):
                        kk = 4 * (i % 2) + k
                        last = three(banks[:, 4 + i // 2, :], t_hi[:, kk, 0:P], t_lo[:, kk, 0:P],
                                     hi_w[:, k, :], lo_w[:, k, :], kk == 0, kk == KD - 1)
                    last.then_inc(used, 1)

            def moe_down(base, units, s, stop=False, which=(0, 1), slot=0):
                pe.wait_ge(h_hi_done, s + (FFN_STEPS + 1))
                pe.wait_ge(h_lo_done, s + (FFN_STEPS + 1))
                for i in which:
                    u = unit_of(base, *units[i])
                    rows(u, 0, lambda k, t: h_hi[:, slot, (2 * i + k) * P:(2 * i + k + 1) * P],
                         lambda k, t: h_lo[:, slot, (2 * i + k) * P:(2 * i + k + 1) * P], 1, False, stop and i == 1).then_inc(used, 1)

            def turn_hid(s):
                pe.wait_ge(hid_done, s + (FFN_STEPS + 1))
                for k in range(4):
                    last = pe.transpose(banks[:, 6, k * P:(k + 1) * P], hid[:, k * P:(k + 1) * P], ident)
                last.then_inc(ht_mm, 1)

            def turn_pick(v):
                pe.wait_ge(pickc_ready, v + 1)
                pe.wait_ge(y_add, v * 4 + 1)
                for t in range(T):
                    last = pe.transpose(banks[:, 7, t * P:(t + 1) * P], pick_c[:, t, :], ident)
                last.then_inc(comb_mm, 1)

            def scatter(v):
                pe.wait_ge(comb_out, v + 1)
                for i, (t, c) in enumerate(((0, 0), (1, 0), (0, 1), (1, 1))):
                    if t == 0:
                        pe.wait_ge(y_rest, v * 2 + (c + 1))
                    if i == 3:
                        pe.wait_ge(y_add, v * 4 + 2)
                    cols = slice(c * HALF, (c + 1) * HALF)
                    dst, lhs = banks[:, (7, 2, 3, 7)[i], :], comb[:, t * P:(t + 1) * P]
                    pe.matmul(dst, lhs, y_hi[:, cols], start=True, stop=False)
                    pe.matmul(dst, lhs, y_lo[:, cols], start=False, stop=True).then_inc(scat_mm, 1)

            def middle(e, j, base, sweep):
                s = (e + sweep * E) * MOE_STEPS + j + 1
                gate_up(base, [(e, 4 + i, j) for i in range(4)])
                moe_down(base, [(e, 8 + i, j) for i in range(2)], s - 1)
                turn_hid(s)

            def edge(e, nxt, base, sweep):
                if e is None:
                    if sweep:
                        pe.wait_ge(y_add, sweep * 4 * E + 1)
                    pe.wait_ge(xn_lo_done, T)
                    gather(sweep * E)
                    clear(0)
                    clear(1)
                    gate_up(base, [(0, i, 0) for i in range(4)], sweep * E)
                    turn_hid(sweep * E * MOE_STEPS)
                    return
                v = e + sweep * E
                s = v * MOE_STEPS + (MOE_STEPS - 1)
                gate_up(base, [(e, 34 + i, 0) for i in range(4)])
                turn_pick(v)
                if nxt is not None:
                    gather(v + 1)
                units = [(e, 38 + i, 0) for i in range(2)]
                if nxt is not None:
                    moe_down(base, units, s - 1)
                    turn_hid(s)
                else:
                    moe_down(base, units, s - 1, which=(0,))
                    turn_hid(s)
                    moe_down(base, units, s - 1, which=(1,))
                if nxt is not None:
                    pe.wait_ge(gath_lo, v * 2 + 4)
                    gate_up(base, [(e, 40 + i, 0) for i in range(4)])
                c = 40 if nxt is None else 44
                moe_down(base, [(e, c + i, 0) for i in range(2)], s, True, slot=0 if nxt is not None else 1)
                if nxt is not None:
                    turn_hid(s + 1)
                scatter(v)
                if nxt is not None:
                    clear(0)
                    clear(1)

            moe_sweep(pe, edge, middle, 0)
            pe.wait_ge(over_set, 1)
            n_over = pe.value_load(over[0:1, 0:1], min_val=0, max_val=SEQ)
            with pe.If(n_over > P):
                moe_sweep(pe, edge, middle, 1)
            with pe.Else():
                pe.nop()

        @block.gpsimd
        def _(pool):
            def zeros(pairs):
                for w in qc_t:
                    pool.memset(w[HD:P, pairs, 0, :].bitcast(F32), 0.0)
                    last = pool.memset(w[0:HD, pairs, 1, :].bitcast(F32), 0.0)
                last.then_inc(q_zero, 1)

            zeros(slice(0, AH // 2))
            pool.wait_ge(q_zero, 1)
            for w in (qk_hi, qk_lo):
                pool.memset(w[BK:P, 3072:4096].bitcast(F32), 0.0)
            for w in (h_hi, h_lo):
                last = pool.memset(w[BK:P].bitcast(F32), 0.0)
            last.then_inc(lat_zero, 1)
            pool.wait_ge(lat_zero, 1)
            pool.wait_ge(tables_in, 16)
            for h in range(AH):
                if h == 1:
                    pool.wait_ge(lat_p, 3)
                if h == 3:
                    pool.wait_ge(lat_v, 8)
                if h >= len(bias_a):
                    pool.wait_ge(s_read, h - len(bias_a) + 1)
                b = bias_a[h % len(bias_a)]
                pool.tensor_scalar(b, tab[:, C_DIST:C_DIST + 512], 2.0 ** -(h + 1), None, ALU.mult).then_inc(bias_step, 1)
                pool.wait_ge(bias_step, h + 1)
                pool.tensor_tensor(b, b, tab[:, C_LNC:C_LNC + 512], ALU.add).then_inc(bias_ready, 1)
            pool.wait_ge(bias_ready, AH)
            pool.wait_ge(used, U_IN + 8)
            for w in (t_hi, t_lo):
                last = pool.memset(w[BK:P].bitcast(F32), 0.0)
            last.then_inc(lat_zero, 1)
            pool.wait_ge(lat_zero, 2)
            pool.wait_ge(s_mm, AH + BH)
            zeros(slice(AH // 2, CH // 2))
            pool.wait_ge(q_zero, 2)

            def picks(e, sweep):
                v = e + sweep * E
                first = v == 0
                places = tab[:, C_IOTA + P * sweep:C_IOTA + P * (sweep + 1)]
                if first:
                    pool.wait_ge(route_v, 4)
                else:
                    pool.wait_ge(gath_mm, v * 2)
                    pool.wait_ge(pickc_ready, v)
                pool.tensor_copy(place_e.unsqueeze(2), place[:, :, e:e + 1]).then_inc(pick_step, 1)
                pool.wait_ge(pick_step, v + 1)
                if not first:
                    for t in range(T):
                        last = pool.tensor_scalar(pick[:, t, :], places, place_e[:, t:t + 1], None, ALU.is_equal)
                    last.then_inc(pick_ready, 1)
                if not first:
                    pool.wait_ge(comb_mm, v)
                for t in range(T):
                    last = pool.tensor_scalar(pick_c[:, t, :], places, place_e[:, t:t + 1], None, ALU.is_equal)
                last.then_inc(pickc_ready, 1)
                pool.wait_ge(y_add, 4 * v + 1)
                pool.tensor_copy(gate_e.unsqueeze(2), gate[:, :, e:e + 1]).then_inc(gate_ready, 1)

            for e in range(E):
                picks(e, 0)
            pool.wait_ge(over_set, 1)
            n_over = pool.value_load(over[0:1, 0:1], min_val=0, max_val=SEQ)
            with pool.If(n_over > P):
                for e in range(E):
                    picks(e, 1)
            with pool.Else():
                pool.nop()


_INS = ["x", "ln_mix_e", "w_in_e", "mla_q_norm", "mla_w_uq", "mla_kv_norm", "mla_w_ukv", "w_out_e",
        "ln_ffn_e", "ffn_w_gate", "ffn_w_up", "ffn_w_down", "ln_mix_o", "na_w_qkv", "na_rpb", "na_w_out",
        "ln_ffn_o", "moe_router", "moe_w_gate", "moe_w_up", "moe_w_down", "ln_final"]


def kernel(**inputs):
    import concourse.bacc as bacc
    from concourse.bass_utils import run_bass_kernel_spmd

    nc = bacc.Bacc("TRN2", target_bir_lowering=False, num_devices=1, dynamic_dma_scratch_size=1024)
    arrays = {f"in_{n}": np.ascontiguousarray(inputs[n]) for n in _INS}
    arrays["in_na_rpb"] = np.ascontiguousarray(inputs["na_rpb"][..., ::-1])
    arrays["in_tables"] = constants()
    args = [nc.dram_tensor(n, a.shape, mybir.dt.from_np(a.dtype), kind="ExternalInput").ap()
            for n, a in arrays.items()]
    y = nc.dram_tensor("out_y", (1, SEQ, D), F32, kind="ExternalOutput").ap()
    trunk(nc, *args, y)
    got = run_bass_kernel_spmd(nc, [arrays], core_ids=[0])
    return got.results[0]["out_y"]
```
